# Optimizing a Trainium2 kernel written in Bass

```python
import jax, jax.numpy as jnp
from jax import lax
import numpy as np

D_MODEL = 2048
BATCH = 1
SEQ = 256
DEPTH = 1

MEM_LEN = 256
NORM_EPS = 1e-6

SWA_Q_HEADS = 16
SWA_KV_HEADS = 4
SWA_HEAD_DIM = 64
SWA_WINDOW = 128
SWA_BLOCK = 128
SWA_Q_W = SWA_Q_HEADS * SWA_HEAD_DIM
SWA_KV_W = SWA_KV_HEADS * SWA_HEAD_DIM

RET_HEADS = 8
RET_HEAD_DIM = 128
RET_CHUNK = 128
RET_W = RET_HEADS * RET_HEAD_DIM
RET_ROPE_BASE = 10000.0

LRU_WIDTH = 1024
LRU_BLOCKS = 8
LRU_BLOCK_DIM = LRU_WIDTH // LRU_BLOCKS
LRU_CONV = 4
LRU_C = 8.0

N_BRANCH = 3
BRANCH_W = 1024
IN_SPLIT_SIZES = (SWA_Q_W, SWA_KV_W, SWA_KV_W,
                  RET_W, RET_W, RET_W, RET_W,
                  LRU_WIDTH, LRU_WIDTH,
                  D_MODEL, D_MODEL, D_MODEL)
IN_W = sum(IN_SPLIT_SIZES)

XATTN_HEADS = 4
XATTN_HEAD_DIM = D_MODEL // XATTN_HEADS

FFN_DIM = 5504
FFN_CONV = 3

kernel_name = "hybrid_swa_retention_rglru_convffn_trunk"

def rms_norm(x, g):
    x32 = x.astype(jnp.float32)
    y = x32 * lax.rsqrt(jnp.mean(x32 * x32, axis=-1, keepdims=True) + NORM_EPS)
    return (y * g.astype(jnp.float32)).astype(x.dtype)

def causal_dwconv(x, w, b):
    width = w.shape[0]
    y = lax.conv_general_dilated(
        x, w[:, None, :].astype(x.dtype), window_strides=(1,), padding=[(width - 1, 0)],
        dimension_numbers=("NWC", "WIO", "NWC"), feature_group_count=x.shape[-1])
    return y + b.astype(x.dtype)

def sliding_window_attention(q, k, v, sinks):
    b, s, hq, dh = q.shape
    hkv = k.shape[2]
    g = hq // hkv
    nb = s // SWA_BLOCK
    qb = q.reshape(b, nb, SWA_BLOCK, hkv, g, dh)
    kb = k.reshape(b, nb, SWA_BLOCK, hkv, dh)
    vb = v.reshape(b, nb, SWA_BLOCK, hkv, dh)

    def with_prev(t):
        prev = jnp.pad(t, ((0, 0), (1, 0), (0, 0), (0, 0), (0, 0)))[:, :-1]
        return jnp.concatenate([prev, t], axis=2)

    kw = with_prev(kb)
    vw = with_prev(vb)
    scores = jnp.einsum("bnqhgd,bnkhd->bnhgqk", qb, kw).astype(jnp.float32) * (dh ** -0.5)
    blk = jnp.arange(nb)[:, None] * SWA_BLOCK
    q_pos = blk + jnp.arange(SWA_BLOCK)[None, :]
    k_pos = blk - SWA_BLOCK + jnp.arange(2 * SWA_BLOCK)[None, :]
    rel = q_pos[:, :, None] - k_pos[:, None, :]
    allowed = (rel >= 0) & (rel < SWA_WINDOW) & (k_pos[:, None, :] >= 0)
    scores = jnp.where(allowed[None, :, None, None], scores, -jnp.inf)
    sink = sinks.astype(jnp.float32).reshape(hkv, g)[None, None, :, :, None, None]
    m = jnp.maximum(jnp.max(scores, axis=-1, keepdims=True), sink)
    p = jnp.exp(scores - m)
    probs = p / (jnp.sum(p, axis=-1, keepdims=True) + jnp.exp(sink - m))
    out = jnp.einsum("bnhgqk,bnkhd->bnqhgd", probs.astype(v.dtype), vw)
    return out.reshape(b, s, hq * dh)

def rotate(t, cos, sin):
    t1, t2 = jnp.split(t, 2, axis=-1)
    return jnp.concatenate([t1 * cos - t2 * sin, t1 * sin + t2 * cos], axis=-1)

def retention(q, k, v):
    b, s, h, d = q.shape
    nc = s // RET_CHUNK
    log_gamma = jnp.log1p(-jnp.exp2(-5.0 - jnp.arange(h, dtype=jnp.float32)))
    qc = q.reshape(b, nc, RET_CHUNK, h, d)
    kc = k.reshape(b, nc, RET_CHUNK, h, d)
    vc = v.reshape(b, nc, RET_CHUNK, h, d)
    idx = jnp.arange(RET_CHUNK, dtype=jnp.float32)
    diff = idx[:, None] - idx[None, :]
    intra_decay = jnp.where(diff[None] >= 0,
                            jnp.exp(jnp.maximum(diff, 0.0)[None] * log_gamma[:, None, None]), 0.0)
    scores = jnp.einsum("bnqhd,bnkhd->bnhqk", qc, kc) * intra_decay[None, None]
    intra = jnp.einsum("bnhqk,bnkhd->bnqhd", scores, vc)
    k_decay = jnp.exp((RET_CHUNK - 1.0 - idx)[:, None] * log_gamma[None, :])
    q_decay = jnp.exp((idx + 1.0)[:, None] * log_gamma[None, :])
    chunk_kv = jnp.einsum("bnkhd,bnkhe->nbhde", kc * k_decay[:, :, None], vc)
    chunk_decay = jnp.exp(RET_CHUNK * log_gamma)[None, :, None, None]

    def step(state, kv):
        return state * chunk_decay + kv, state

    _, prev_states = lax.scan(step, jnp.zeros((b, h, d, d), jnp.float32), chunk_kv)
    inter = jnp.einsum("bnqhd,nbhde->bnqhe", qc * q_decay[:, :, None], prev_states)
    return (intra + inter).reshape(b, s, h, d)

def head_group_norm(y):
    mu = jnp.mean(y, axis=-1, keepdims=True)
    yc = y - mu
    return yc * lax.rsqrt(jnp.mean(yc * yc, axis=-1, keepdims=True) + NORM_EPS)

def rg_lru(x, w_a, b_a, w_x, b_x, lam):
    b, s, w = x.shape
    xb = x.reshape(b, s, LRU_BLOCKS, LRU_BLOCK_DIM)
    gate_r = jax.nn.sigmoid(jnp.einsum("bsnd,nde->bsne", xb, w_a).reshape(b, s, w) + b_a)
    gate_i = jax.nn.sigmoid(jnp.einsum("bsnd,nde->bsne", xb, w_x).reshape(b, s, w) + b_x)
    log_a = -LRU_C * gate_r.astype(jnp.float32) * jax.nn.softplus(-lam.astype(jnp.float32))
    a = jnp.exp(log_a)
    u = jnp.sqrt(-jnp.expm1(2.0 * log_a)) * (gate_i * x).astype(jnp.float32)

    def combine(left, right):
        a_l, b_l = left
        a_r, b_r = right
        return a_l * a_r, a_r * b_l + b_r

    _, hs = lax.associative_scan(combine, (a, u), axis=1)
    return hs.astype(x.dtype)

def hybrid_mixer(h, w_in, attn_sinks, lru_conv_w, lru_conv_b, lru_wa, lru_ba, lru_wx, lru_bx,
                 lru_lambda, w_branch, w_out):
    b, s, _ = h.shape
    proj = h @ w_in
    parts = []
    off = 0
    for size in IN_SPLIT_SIZES:
        parts.append(proj[..., off:off + size])
        off += size
    q_a, k_a, v_a, q_r, k_r, v_r, g_r, x_c, y_c, gate_a, gate_b, gate_c = parts

    o_a = sliding_window_attention(q_a.reshape(b, s, SWA_Q_HEADS, SWA_HEAD_DIM),
                                   k_a.reshape(b, s, SWA_KV_HEADS, SWA_HEAD_DIM),
                                   v_a.reshape(b, s, SWA_KV_HEADS, SWA_HEAD_DIM), attn_sinks)

    theta = RET_ROPE_BASE ** (-jnp.linspace(0.0, 1.0, RET_HEAD_DIM // 2, dtype=jnp.float32))
    ang = jnp.arange(s, dtype=jnp.float32)[:, None] * theta[None, :]
    cos = jnp.cos(ang)[:, None, :]
    sin = jnp.sin(ang)[:, None, :]
    qr = rotate(q_r.astype(jnp.float32).reshape(b, s, RET_HEADS, RET_HEAD_DIM), cos, sin)
    kr = rotate(k_r.astype(jnp.float32).reshape(b, s, RET_HEADS, RET_HEAD_DIM), cos, sin) * (RET_HEAD_DIM ** -0.5)
    vr = v_r.astype(jnp.float32).reshape(b, s, RET_HEADS, RET_HEAD_DIM)
    y_ret = head_group_norm(retention(qr, kr, vr)).reshape(b, s, RET_W).astype(h.dtype)
    o_b = jax.nn.silu(g_r) * y_ret

    xc = causal_dwconv(x_c, lru_conv_w, lru_conv_b)
    o_c = rg_lru(xc, lru_wa, lru_ba, lru_wx, lru_bx, lru_lambda) * jax.nn.gelu(y_c)

    merged = (jax.nn.sigmoid(gate_a) * (o_a @ w_branch[0])
              + jax.nn.sigmoid(gate_b) * (o_b @ w_branch[1])
              + jax.nn.sigmoid(gate_c) * (o_c @ w_branch[2]))
    return merged @ w_out

def memory_cross_attention(h, mem_n, wq, wkv, wo):
    b, s, _ = h.shape
    m = mem_n.shape[1]
    q = (h @ wq).reshape(b, s, XATTN_HEADS, XATTN_HEAD_DIM)
    kv = mem_n @ wkv
    k = kv[..., :D_MODEL].reshape(b, m, XATTN_HEADS, XATTN_HEAD_DIM)
    v = kv[..., D_MODEL:].reshape(b, m, XATTN_HEADS, XATTN_HEAD_DIM)
    scores = jnp.einsum("bshd,bmhd->bhsm", q, k).astype(jnp.float32) * (XATTN_HEAD_DIM ** -0.5)
    p = jax.nn.softmax(scores, axis=-1).astype(v.dtype)
    o = jnp.einsum("bhsm,bmhd->bshd", p, v).reshape(b, s, D_MODEL)
    return o @ wo

def conv_ffn(h, w_up, conv_w, conv_b, w_down):
    gate = causal_dwconv(h @ w_up[:, :FFN_DIM], conv_w, conv_b)
    val = h @ w_up[:, FFN_DIM:]
    return (jax.nn.silu(gate) * val) @ w_down

def setup_inputs(seed: int = 0) -> dict:
    key = jax.random.key(seed)
    ks = jax.random.split(key, 28)
    f32 = jnp.float32
    L = DEPTH

    def dense(k, shape, fan_in):
        return jax.random.normal(k, shape, f32) * (fan_in ** -0.5)

    def gain(k, shape):
        return 1.0 + 0.02 * jax.random.normal(k, shape, f32)

    def small(k, shape, scale=0.02):
        return scale * jax.random.normal(k, shape, f32)

    a_pow = jax.random.uniform(ks[10], (L, LRU_WIDTH), f32, 0.9, 0.999)
    a_base = a_pow ** (1.0 / LRU_C)
    lru_lambda = jnp.log(a_base) - jnp.log1p(-a_base)
    return {
        "x": jax.random.normal(ks[0], (BATCH, SEQ, D_MODEL), f32),
        "mem": jax.random.normal(ks[1], (BATCH, MEM_LEN, D_MODEL), f32),
        "mem_norm_g": gain(ks[2], (D_MODEL,)),
        "norm_mix_g": gain(ks[3], (L, D_MODEL)),
        "w_in": dense(ks[4], (L, D_MODEL, IN_W), D_MODEL),
        "attn_sinks": small(ks[5], (L, SWA_Q_HEADS), 0.5),
        "lru_conv_w": dense(ks[6], (L, LRU_CONV, LRU_WIDTH), LRU_CONV),
        "lru_conv_b": small(ks[7], (L, LRU_WIDTH)),
        "lru_wa": dense(ks[8], (L, LRU_BLOCKS, LRU_BLOCK_DIM, LRU_BLOCK_DIM), LRU_BLOCK_DIM),
        "lru_ba": small(ks[9], (L, LRU_WIDTH), 0.1),
        "lru_wx": dense(ks[11], (L, LRU_BLOCKS, LRU_BLOCK_DIM, LRU_BLOCK_DIM), LRU_BLOCK_DIM),
        "lru_bx": small(ks[12], (L, LRU_WIDTH), 0.1),
        "lru_lambda": lru_lambda,
        "w_branch": dense(ks[13], (L, N_BRANCH, BRANCH_W, D_MODEL), BRANCH_W),
        "w_out": dense(ks[14], (L, D_MODEL, D_MODEL), D_MODEL),
        "norm_xattn_g": gain(ks[15], (L, D_MODEL)),
        "xattn_wq": dense(ks[16], (L, D_MODEL, D_MODEL), D_MODEL),
        "xattn_wkv": dense(ks[17], (L, D_MODEL, 2 * D_MODEL), D_MODEL),
        "xattn_wo": dense(ks[18], (L, D_MODEL, D_MODEL), D_MODEL),
        "norm_ffn_g": gain(ks[19], (L, D_MODEL)),
        "ffn_w_up": dense(ks[20], (L, D_MODEL, 2 * FFN_DIM), D_MODEL),
        "ffn_conv_w": dense(ks[21], (L, FFN_CONV, FFN_DIM), FFN_CONV),
        "ffn_conv_b": small(ks[22], (L, FFN_DIM)),
        "ffn_w_down": dense(ks[23], (L, FFN_DIM, D_MODEL), FFN_DIM),
        "final_norm_g": gain(ks[24], (D_MODEL,)),
    }

def reference(x, mem, mem_norm_g, norm_mix_g, w_in, attn_sinks, lru_conv_w, lru_conv_b, lru_wa,
              lru_ba, lru_wx, lru_bx, lru_lambda, w_branch, w_out, norm_xattn_g, xattn_wq,
              xattn_wkv, xattn_wo, norm_ffn_g, ffn_w_up, ffn_conv_w, ffn_conv_b, ffn_w_down,
              final_norm_g):
    mem_n = rms_norm(mem, mem_norm_g)
    for l in range(DEPTH):
        x = x + hybrid_mixer(rms_norm(x, norm_mix_g[l]), w_in[l], attn_sinks[l], lru_conv_w[l],
                             lru_conv_b[l], lru_wa[l], lru_ba[l], lru_wx[l], lru_bx[l],
                             lru_lambda[l], w_branch[l], w_out[l])
        x = x + memory_cross_attention(rms_norm(x, norm_xattn_g[l]), mem_n, xattn_wq[l],
                                       xattn_wkv[l], xattn_wo[l])
        x = x + conv_ffn(rms_norm(x, norm_ffn_g[l]), ffn_w_up[l], ffn_conv_w[l], ffn_conv_b[l],
                         ffn_w_down[l])
    return rms_norm(x, final_norm_g)


_drawn_inputs = setup_inputs


def setup_inputs(seed=0):
    import zlib

    import numpy as np

    out = dict(_drawn_inputs(seed))
    spreads = {}
    factors = {'mem_norm_g': 8.0,
     'norm_mix_g': 3.755,
     'attn_sinks': 8.0,
     'lru_ba': 8.0,
     'lru_bx': 8.0,
     'norm_xattn_g': 8.0,
     'norm_ffn_g': 4.096,
     'ffn_conv_b': 5.89,
     'final_norm_g': 2.839}
    for name, (base, spread) in spreads.items():
        noise = np.random.default_rng([zlib.crc32(name.encode()), seed]).standard_normal(out[name].shape)
        drawn = base * np.exp(spread * noise) if base else spread * noise
        out[name] = __import__('jax').numpy.asarray(drawn.astype(out[name].dtype))
    for name, factor in factors.items():
        out[name] = (out[name] * factor).astype(out[name].dtype)
    return out
```

```python
from contextlib import ExitStack

import numpy as np

import concourse.bass as bass
from concourse import mybir

P = 128
D = 2048
T = 256
KT = D // P
MEM = 256
EPS = 1e-6
BW = 1024
BT = BW // P
SWA_HEADS, SWA_KV, SWA_D = 16, 4, 64
RET_HEADS, RET_D = 8, 128
X_HEADS, X_D = 4, 512
F = 5504
FT = F // P
RING = 4
UT = 8
UW = UT * P

DOWN_K = [2] * 19 + [1] * 5
assert sum(DOWN_K) == FT and len(DOWN_K) % RING == 0
DOWN_BLOCKS = D // 512

G_CH = 26 * 2 // RING
G_VA = 1
G_RET = 8 * 8 // RING
G_BR = KT * 3 // RING
G_SQ = 4 * 8 // RING
G_UP = FT * 4 // RING
G0_VA = G_CH
G0_RET = G0_VA + G_VA
G0_BR = G0_RET + G_RET
G0_OUT = G0_BR + 3 * G_BR
G0_K = G0_OUT + G_SQ
G0_V = G0_K + G_SQ
G0_Q = G0_V + G_SQ
G0_O = G0_Q + G_SQ
G0_UP = G0_O + G_SQ
G0_DOWN = G0_UP + G_UP
G_DOWN = len(DOWN_K) // RING
FULL_ROWS = G0_DOWN * RING * P
DOWN_ROWS = FT * P

V_MEM, V_MIX, V_X, V_FFN = 0, 16, 32, 48
V_CW, V_CB, V_BA, V_BX, V_LAM = 64, 96, 104, 112, 120
V_FW, V_FB = 128, 128 + 3 * FT
NV = V_FB + FT
C_ID, C_COS, C_SIN, C_PREV, C_DIAG = 0, 128, 256, 384, 512
NC_ = 640
NDEC = 3 * P
GELU_1 = 2.0 * 0.7978845608028654
GELU_3 = GELU_1 * 0.044715


class Steps:

    def __init__(self, eng, sem):
        self.eng, self.sem, self.n, self.off = eng, sem, 0, 0

    def did(self, ins):
        ins.then_inc(self.sem, 1)
        self.n += 1
        return self.n + self.off

    def wait(self):
        self.eng.wait_ge(self.sem, self.n + self.off)

    def enter(self, i, per):
        self.off, self.start, self.per = i * per, self.n, per

    def leave(self, iters):
        assert self.n - self.start == self.per, (self.n - self.start, self.per)
        self.n, self.off = self.start + self.per * iters, 0


def trunk_kernel(nc, x_d, mem_d, stream_d, down_d, vecs_d, sinks_d, lru_w_d, final_g_d, consts_d, decay_d, out_d):
    f32, f32r = mybir.dt.float32, mybir.dt.float32r
    ALU, ACT, AX = mybir.AluOpType, mybir.ActivationFunctionType, mybir.AxisListType
    KB = 256

    ctx = ExitStack()
    with ctx:
        def sb(name, shape, dt=f32):
            return ctx.enter_context(nc.sbuf_tensor(name, shape, dt))

        def sem(name):
            return ctx.enter_context(nc.semaphore(name))

        raw = sb("raw", [P, RING, UW])
        whi = sb("whi", [P, RING, UW], f32r)
        wlo = sb("wlo", [P, RING, UW], f32r)
        xT = sb("xT", [P, KT, 2 * T], f32r)
        vecs = sb("vecs", [P, NV])
        consts = sb("consts", [P, NC_])
        sinks = sb("sinks", [P, SWA_HEADS])
        ss = sb("ss", [P, 10])
        rstd = sb("rstd", [P, 10])
        sp = sb("sp", [P, 8, BT])
        stat = sb("stat", [P, 6, 48])
        pw = sb("pw", [P, 2])
        ret_st = sb("ret_st", [P, 2, 8])
        ident = consts[:, C_ID:C_ID + P]

        def at(kib, name, shape, dt=f32):
            with ExitStack() as tmp:
                if kib:
                    tmp.enter_context(nc.sbuf_tensor(name + "_below", [P, int(kib * KB)], f32))
                return tmp.enter_context(nc.sbuf_tensor(name, shape, dt))

        xr = at(0, "xr", [P, 2, D])
        xn = at(16, "xn", [P, 2, D])
        chT = at(32, "chT", [P, 26, T])
        va = at(58, "va", [P, 2, SWA_KV * SWA_D])
        lru_t = at(60, "lru_t", [P, 2, 8, T])
        lru_w = at(76, "lru_w", [P, 2, BT, P])
        ocT = at(0, "ocT", [P, BT, 2 * T], f32r)
        oaT = at(16, "oaT", [P, BT, 2 * T], f32r)
        swa_s = at(92, "swa_s", [P, 2, 512])
        swa_p = at(96, "swa_p", [P, 2, 512])
        swa_pT = at(100, "swa_pT", [P, 2, 512])
        ret = at(60, "ret", [P, 8, 2, 512])
        decay = at(92, "decay", [P, RET_HEADS, NDEC])
        obT = at(32, "obT", [P, BT, 2 * T], f32r)
        rot = at(48, "rot", [P, 2, 2, 2, P])
        qkT = at(52, "qkT", [P, 2, 2 * T])
        rope_t = at(56, "rope_t", [P, 4, 2, 2, 64])
        sT = at(104, "sT", [P, 2, NDEC])
        ret_y = at(107, "ret_y", [P, 2, 4, 2, P])
        merged = at(64, "merged", [P, KT, T])
        br_t = at(80, "br_t", [P, 2, 4, T])
        mT = at(0, "mT", [P, KT, 2 * T], f32r)
        x1 = at(92, "x1", [P, 2, D])
        memr = at(64, "memr", [P, 2, D])
        memT = at(32, "memT", [P, KT, 2 * T], f32r)
        kT = at(0, "kT", [P, KT, MEM])
        v = at(64, "v", [P, 2, D])
        x1n = at(16, "x1n", [P, 2, D])
        qT = at(16, "qT", [P, KT, T])
        xp = at(80, "xp", [P, 2, 512])
        xpT = at(84, "xpT", [P, 2, 512])
        x2n = at(0, "x2n", [P, 2, D])
        actT = at(0, "actT", [P, FT, 2 * T], f32r)
        ffn_t = at(108, "ffn_t", [P, 4, T])
        outn = at(0, "outn", [P, 2, D])
        gfin = at(16, "gfin", [P, D])

        bank = [ctx.enter_context(nc.psum_tensor(f"bank{b}", [P, 512], f32)) for b in range(8)]

        raw_loaded = [sem(f"raw_loaded{s}") for s in range(RING)]
        hi_ready, lo_ready, unit_used = sem("hi_ready"), sem("lo_ready"), sem("unit_used")
        half0_done, prod_free = sem("half0_done"), sem("prod_free")
        x_loaded, c_loaded, lruw_loaded, dec_loaded = sem("x_loaded"), sem("c_loaded"), sem("lruw_loaded"), sem("dec_loaded")
        sinks_loaded = sem("sinks_loaded")
        x1_loaded, mem_loaded, gf_loaded, stored = sem("x1_loaded"), sem("mem_loaded"), sem("gf_loaded"), sem("stored")
        dve_step, act_step = sem("dve_step"), sem("act_step")
        n_sq, n_ms, n_rstd, n_xn, n_tr, n_hi, n_lo = (sem("norm_" + w) for w in ("sq", "ms", "rstd", "xn", "tr", "hi", "lo"))
        l_xc, l_ps, l_sig, l_q, l_gelu, l_done = (sem("lru_" + w) for w in ("xc", "ps", "sig", "q", "gelu", "done"))
        pow_ready, l_m, l_root, r_var, r_rstd = (sem(w) for w in (
            "pow_ready", "lru_m", "lru_root", "ret_var", "ret_rstd"))
        lru_abs, lru_z, lru_consts = sem("lru_abs"), sem("lru_z"), sem("lru_consts")
        s_sc, s_max, s_exp, s_p, s_tr, s_pT, s_pv, s_hi, s_lo = (
            sem("swa_" + w) for w in ("sc", "max", "exp", "p", "tr", "pT", "pv", "hi", "lo"))
        r_rot, r_tr, r_qkT, r_sc, r_sT, r_y, r_silu, r_o, r_otr, r_hi, r_lo = (
            sem("ret_" + w) for w in ("rot", "tr", "qkT", "sc", "sT", "y", "silu", "o", "otr", "hi", "lo"))
        g_tanh, merged_done = sem("gate_tanh"), sem("merged_done")
        x_sc, x_max, x_exp, x_p, x_tr, x_pT, x_pv, x_hi, x_lo = (
            sem("xa_" + w) for w in ("sc", "max", "exp", "p", "tr", "pT", "pv", "hi", "lo"))
        f_tanh = sem("ffn_tanh")
        out_ready, act_whole = sem("out_ready"), sem("act_whole")
        block = ctx.enter_context(nc.Block())

        NORM = [(xr, xn, xT, V_MIX), (memr, memr, memT, V_MEM), (x1, x1n, xT, V_X), (x1, x2n, xT, V_FFN)]
        NB = KT // 2
        P_CH = 0
        P_VA = 26
        P_RET = P_VA + 2
        P_BR = P_RET + 16
        P_OUT = P_BR + 3 * 2 * KT
        P_K = P_OUT + 8
        P_V = P_K + KT
        P_Q = P_V + 8
        P_O = P_Q + KT
        P_UP = P_O + 8
        P_DOWN = P_UP + 2 * FT
        B_VA, B_RET, B_OUT, B_V, B_O, B_DOWN = 0, 1, 9, 13, 17, 21

        def swa_groups():
            for big in range(2):
                for half in range(2):
                    yield big, half, 0, 4 * big, 4
                    yield big, half, 1, 4 * big, 2
                    yield big, half, 1, 4 * big + 2, 2

        SWA = list(swa_groups())

        def down_width(s):
            return DOWN_K[s] * 512

        @block.sync
        def _(sp_eng):
            def load(g, s):
                sp_eng.dma_start(raw[:, s, :], stream_d[bass.ds((g * RING + s) * P, P), :]).then_inc(raw_loaded[s], 16)

            for s in range(RING):
                load(0, s)
            with sp_eng.Fori(1, G0_DOWN) as g:
                for s in range(RING):
                    sp_eng.wait_ge(lo_ready, g * RING + (s + 1 - RING))
                    load(g, s)
            with sp_eng.Fori(0, DOWN_BLOCKS) as c:
                row = 0
                for u, k in enumerate(DOWN_K):
                    s = u % RING
                    sp_eng.wait_ge(lo_ready, c * len(DOWN_K) + (G0_DOWN * RING + u + 1 - RING))
                    src = down_d[bass.ds(c * DOWN_ROWS + row, k * P), :].rearrange("(p b) n -> p (b n)", p=P)
                    sp_eng.dma_start(raw[:, s, 0:512 * k], src).then_inc(raw_loaded[s], 16)
                    row += k * P
            for t in range(2):
                sp_eng.wait_ge(out_ready, t + 1)
                sp_eng.dma_start(out_d[t * P:(t + 1) * P, :], outn[:, t, :]).then_inc(stored, 16)
            sp_eng.wait_ge(stored, 32)

        @block.gpsimd
        def _(pool):
            def rsqrt_of_norm(which):
                for c in (2 * which, 2 * which + 1):
                    pool.wait_ge(n_ms, c + 1)
                    pool.tensor_tensor(rstd[:, c:c + 1], ss[:, c:c + 1], pw[:, 0:1], ALU.pow).then_inc(n_rstd, 1)

            pool.memset(pw[:, 0:1], -0.5).then_inc(pow_ready, 1)
            pool.memset(pw[:, 1:2], 0.5).then_inc(pow_ready, 1)
            pool.dma_start(lru_w[:, :, :, :], lru_w_d).then_inc(lruw_loaded, 16)
            pool.dma_start(sinks[:, :], sinks_d[None, :].broadcast_to([P, SWA_HEADS])).then_inc(sinks_loaded, 16)
            pool.wait_ge(pow_ready, 2)
            rsqrt_of_norm(0)
            for n in range(BT):
                th = lru_t[:, n % 2, 4, :]
                pool.wait_ge(l_m, n + 1)
                pool.tensor_tensor(th, th, pw[:, 1:2].broadcast_to([P, T]), ALU.pow).then_inc(l_root, 1)
            pool.wait_ge(s_lo, 4)
            pool.dma_start(decay[:, :, :], decay_d).then_inc(dec_loaded, 16)
            for h in range(RET_HEADS):
                pool.wait_ge(r_var, h + 1)
                for t in range(2):
                    pool.tensor_tensor(ret_st[:, t, 7:8], ret_st[:, t, 7:8], pw[:, 0:1], ALU.pow).then_inc(r_rstd, 1)
            pool.wait_ge(r_lo, RET_HEADS)
            pool.dma_start(x1[:, :, :], x_d.rearrange("(t p) d -> p t d", p=P)).then_inc(x1_loaded, 16)
            pool.wait_ge(prod_free, P_OUT)
            pool.dma_start(memr[:, :, :], mem_d.rearrange("(t p) d -> p t d", p=P)).then_inc(mem_loaded, 16)
            for which in (1, 2, 3):
                rsqrt_of_norm(which)
            pool.wait_ge(unit_used, RING * (G0_DOWN + DOWN_BLOCKS * G_DOWN))
            pool.dma_start(gfin[:, :], final_g_d[None, :].broadcast_to([P, D])).then_inc(gf_loaded, 16)
            rsqrt_of_norm(4)

        @block.scalar
        def _(act):
            step = Steps(act, act_step)
            act.dma_start(xr[:, :, :], x_d.rearrange("(t p) d -> p t d", p=P)).then_inc(x_loaded, 16)
            act.dma_start(vecs[:, :], vecs_d).then_inc(c_loaded, 16)
            act.dma_start(consts[:, :], consts_d).then_inc(c_loaded, 16)

            def hi_split(g, s, width=UW, first=False):
                act.wait_ge(raw_loaded[s], (g + 1) * 16)
                if not first:
                    act.wait_ge(unit_used, g * RING + (s + 1 - RING))
                act.activation(whi[:, s, 0:width], raw[:, s, 0:width], ACT.Copy).then_inc(hi_ready, 1)

            def stage(g0, body_groups, iters, evac=None):
                def body(i):
                    for u in range(RING * body_groups):
                        if evac:
                            evac(i, u)
                        hi_split(i * body_groups + (g0 + 1 + u // RING), u % RING)
                if iters == 1:
                    body(0)
                else:
                    with act.Fori(0, iters) as i:
                        body(i)

            def norm(which):
                src, dst, outT, g = NORM[which]
                for t in range(2):
                    if which == 0 and t == 0:
                        act.wait_ge(x_loaded, 16)
                    if which == 1 and t == 0:
                        act.wait_ge(mem_loaded, 16)
                    if which > 1 and t == 0:
                        act.wait_ge(prod_free, P_K if which == 2 else P_UP)
                    junk = outT[:, 4 * t:4 * t + 4, :].rearrange("p a b -> p (a b)")
                    act.activation(junk, src[:, t, :], ACT.Square,
                                   accum_out=ss[:, 2 * which + t:2 * which + t + 1]).then_inc(n_sq, 1)
                for t in range(2):
                    act.wait_ge(n_rstd, 2 * which + t + 1)
                    act.activation(dst[:, t, :], src[:, t, :], ACT.Copy,
                                   scale=rstd[:, 2 * which + t:2 * which + t + 1]).then_inc(n_xn, 1)
                for b in range(NB):
                    if which == 0 and b == 0:
                        act.wait_ge(c_loaded, 32)
                    act.wait_ge(n_tr, NB * which + b + 1)
                    for k in (2 * b, 2 * b + 1):
                        ins = act.activation(outT[:, k, 0:T], bank[4 + b % 4][:, (k % 2) * T:(k % 2) * T + T],
                                             ACT.Copy, scale=vecs[:, g + k:g + k + 1])
                    ins.then_inc(n_hi, 1)

            norm(0)
            for s in range(RING):
                hi_split(0, s, first=True)
            stage(0, 1, G_CH)
            stage(G0_VA, 1, 1)

            act.wait_ge(lru_abs, 1)
            act.activation(sp[:, 1, :], sp[:, 0, :], ACT.Exp).then_inc(lru_z, 1)
            act.wait_ge(lru_consts, 1)
            act.wait_ge(prod_free, P_VA)
            for n in range(BT):
                tr, ti, a, th, y2, tg = (lru_t[:, n % 2, j, :] for j in (1, 2, 3, 4, 5, 6))
                y = chT[:, BT + n, :]
                if n >= 2:
                    act.wait_ge(l_done, n - 1)
                act.activation(y2, y, ACT.Square).then_inc(l_sig, 1)
                act.wait_ge(l_ps, n + 1)
                act.activation(tr, bank[4 + n % 2][:, 0:T], ACT.Tanh, scale=0.5, bias=sp[:, 6, n:n + 1])
                step.did(act.activation(ti, bank[4 + n % 2][:, T:2 * T], ACT.Tanh, scale=0.5, bias=sp[:, 7, n:n + 1]))
                step.wait()
                act.activation(a, tr, ACT.Exp, scale=sp[:, 4, n:n + 1], bias=sp[:, 4, n:n + 1])
                act.activation(th, tr, ACT.Tanh, scale=sp[:, 5, n:n + 1], bias=sp[:, 5, n:n + 1]).then_inc(l_sig, 1)
                act.wait_ge(l_q, n + 1)
                act.activation(tg, lru_t[:, n % 2, 7, :], ACT.Tanh, scale=0.5).then_inc(l_gelu, 1)

            for n in range(len(SWA) + 1):
                if n < len(SWA):
                    tiles = SWA[n][4]
                    w = 512 // tiles
                    act.wait_ge(s_max, n + 1)
                    if n >= 2:
                        act.wait_ge(s_tr, n - 1)
                    for j in range(tiles):
                        act.activation(swa_p[:, n % 2, j * w:(j + 1) * w], swa_s[:, n % 2, j * w:(j + 1) * w],
                                       ACT.Exp, bias=stat[:, 1, 4 * n + j:4 * n + j + 1],
                                       accum_out=stat[:, 2, 4 * n + j:4 * n + j + 1])
                    act.activation(stat[:, 4, 4 * n:4 * n + tiles], stat[:, 3, 4 * n:4 * n + tiles],
                                   ACT.Exp).then_inc(s_exp, 1)
                if n >= 1:
                    m = n - 1
                    act.wait_ge(s_tr, m + 1)
                    if m >= 2:
                        act.wait_ge(s_pv, m - 1)
                    act.activation(swa_pT[:, m % 2, :], bank[6][:, :], ACT.Copy).then_inc(s_pT, 1)
                    if m % 6 == 5:
                        big = SWA[m][0]
                        act.wait_ge(s_pv, m + 1)
                        for j in range(2):
                            act.activation(oaT[:, 4 * big + 2 * j:4 * big + 2 * j + 2, 0:T],
                                           bank[2 + j][:, :].rearrange("p (a b) -> p a b", a=2),
                                           ACT.Copy).then_inc(s_hi, 1)

            stage(G0_RET, 2, 8)

            def ret_qkT(h):
                act.wait_ge(r_tr, h + 1)
                if h >= 2:
                    act.wait_ge(r_sc, h - 1)
                act.activation(qkT[:, h % 2, :], bank[4][:, :], ACT.Copy).then_inc(r_qkT, 1)

            act.wait_ge(prod_free, P_BR)
            ret_qkT(0)
            for h in range(RET_HEADS):
                if h >= 2:
                    act.wait_ge(r_o, h - 1)
                act.activation(ret_y[:, h % 2, 0, :, :], ret[:, 6 + h // 4, :, (h % 4) * P:(h % 4) * P + P],
                               ACT.Tanh, scale=0.5).then_inc(r_silu, 1)
                if h + 1 < RET_HEADS:
                    ret_qkT(h + 1)
                act.wait_ge(r_otr, h + 1)
                act.activation(obT[:, h, 0:T], bank[7][:, 0:T], ACT.Copy, scale=0.5).then_inc(r_hi, 1)

            def gate_evac(b):
                def evac(i, u):
                    if u % 3 == 1:
                        n = u // 3
                        act.wait_ge(unit_used, i * 12 + (RING * (G0_BR + G_BR * b) + u + 1))
                        act.wait_ge(prod_free, i * 8 + (P_BR + 2 * KT * b + 2 * n - 2))
                        act.activation(br_t[:, n % 2, 0, :], bank[2 * n % 4][:, 0:T], ACT.Tanh, scale=0.5).then_inc(g_tanh, 1)
                return evac
            for b in range(3):
                stage(G0_BR + G_BR * b, 3, 4, gate_evac(b))

            stage(G0_OUT, 2, 4)
            norm(1)
            stage(G0_K, 1, 8)
            stage(G0_V, 2, 4)
            norm(2)
            stage(G0_Q, 1, 8)

            for h in range(X_HEADS):
                act.wait_ge(x_max, h + 1)
                for t in range(2):
                    ins = act.activation(xp[:, t, 0:MEM], bank[4][:, t * MEM:(t + 1) * MEM], ACT.Exp,
                                         scale=X_D ** -0.5, bias=stat[:, 1, 2 * h + t:2 * h + t + 1],
                                         accum_out=stat[:, 2, 2 * h + t:2 * h + t + 1])
                ins.then_inc(x_exp, 1)
                act.wait_ge(x_tr, h + 1)
                act.activation(xpT[:, 0, :], bank[5][:, :], ACT.Copy).then_inc(x_pT, 1)
                for j in range(2):
                    act.wait_ge(x_pv, 2 * h + j + 1)
                    act.activation(xT[:, 4 * h + 2 * j:4 * h + 2 * j + 2, 0:T],
                                   bank[6 + j][:, :].rearrange("p (a b) -> p a b", a=2), ACT.Copy).then_inc(x_hi, 1)

            stage(G0_O, 2, 4)
            norm(3)

            def ffn_evac(i, u):
                if u == 2:
                    act.wait_ge(prod_free, i * 2 + (P_UP + 1))
                    act.activation(ffn_t[:, 1, :], ffn_t[:, 0, :], ACT.Tanh, scale=0.5).then_inc(f_tanh, 1)
            stage(G0_UP, 1, FT, ffn_evac)

            def down_splits(c, last):
                for u in range(len(DOWN_K)):
                    nxt = (u + RING) % len(DOWN_K)
                    if not (last and u + RING >= len(DOWN_K)):
                        hi_split(c * G_DOWN + (G0_DOWN + 1 + u // RING), u % RING, down_width(nxt))
            with act.Fori(0, DOWN_BLOCKS - 1) as c:
                down_splits(c, False)
            down_splits(DOWN_BLOCKS - 1, True)

            act.wait_ge(prod_free, P_DOWN + 2 * DOWN_BLOCKS)
            for t in range(2):
                act.activation(xT[:, 4 * t:4 * t + 4, :].rearrange("p a b -> p (a b)"), x1[:, t, :],
                               ACT.Square, accum_out=ss[:, 8 + t:9 + t]).then_inc(n_sq, 1)

        @block.vector
        def _(dve):
            step = Steps(dve, dve_step)

            def lo_split(g, s, width=UW):
                dve.wait_ge(hi_ready, g * RING + (s + 1))
                dve.tensor_tensor(wlo[:, s, 0:width], raw[:, s, 0:width], whi[:, s, 0:width].bitcast(f32),
                                  ALU.subtract).then_inc(lo_ready, 1)

            def stage(g0, body_groups, iters, evac=None, steps=0):
                def body(i):
                    for u in range(RING * body_groups):
                        if evac:
                            evac(i, u)
                        lo_split(i * body_groups + (g0 + 1 + u // RING), u % RING)
                if iters == 1:
                    body(0)
                else:
                    with dve.Fori(0, iters) as i:
                        step.enter(i, steps)
                        body(i)
                        step.leave(iters)

            def mean_squares(which):
                for c in (2 * which, 2 * which + 1):
                    dve.wait_ge(n_sq, c + 1)
                    dve.tensor_scalar(ss[:, c:c + 1], ss[:, c:c + 1], 1.0 / D, EPS, ALU.mult, ALU.add).then_inc(n_ms, 1)

            def norm(which):
                _, _, outT, g = NORM[which]
                mean_squares(which)
                for b in range(NB):
                    dve.wait_ge(n_hi, NB * which + b + 1)
                    for k in (2 * b, 2 * b + 1):
                        ins = dve.scalar_tensor_tensor(outT[:, k, T:2 * T], bank[4 + b % 4][:, (k % 2) * T:(k % 2) * T + T],
                                                       vecs[:, g + k:g + k + 1], outT[:, k, 0:T].bitcast(f32),
                                                       ALU.mult, ALU.subtract)
                    ins.then_inc(n_lo, 1)

            def copy_channels(g0, dest):
                def evac(i, u):
                    if u % 2 == 1:
                        dve.wait_ge(unit_used, i * 4 + (RING * g0 + u + 1))
                        out = dest(i, u // 2)
                        dve.tensor_copy(out, bank[u // 2][:, 0:T]).then_inc(prod_free, 1)
                return evac

            def wait_half(t, i, units, g0, b0):
                if t == 0:
                    dve.wait_ge(half0_done, i + (b0 + 1))
                else:
                    dve.wait_ge(unit_used, i * units + (RING * g0 + units))

            def copy_tokens(g0, b0, units, dest):
                def evac(i, u):
                    if u == units - 1:
                        for t in range(2):
                            wait_half(t, i, units, g0, b0)
                            out, src = dest(i, t)
                            dve.tensor_copy(out, src).then_inc(prod_free, 1)
                return evac

            dve.wait_ge(c_loaded, 32)
            lam = vecs[:, V_LAM:V_LAM + BT]
            s0, s1, s2, s3 = (sp[:, j, :] for j in range(4))
            dve.tensor_scalar(sp[:, 6, :], vecs[:, V_BA:V_BA + BT], 0.5, None, ALU.mult)
            dve.tensor_scalar(sp[:, 7, :], vecs[:, V_BX:V_BX + BT], 0.5, None, ALU.mult)
            step.did(dve.tensor_scalar(s1, lam, -1.0, None, ALU.mult))
            step.wait()
            step.did(dve.tensor_tensor(s0, lam, s1, ALU.max))
            step.wait()
            dve.tensor_scalar(s0, s0, -1.0, None, ALU.mult).then_inc(lru_abs, 1)
            norm(0)
            for s in range(RING):
                lo_split(0, s)
            stage(0, 1, G_CH, copy_channels(0, lambda i, j: (
                chT[:, bass.ds(i * 2 + j, 1), :].rearrange("p a b -> p (a b)"))))
            stage(G0_VA, 1, 1, copy_tokens(G0_VA, B_VA, 4, lambda i, j: (va[:, j, :], bank[j][:, 0:T])))

            dve.wait_ge(lru_z, 1)
            step.did(dve.tensor_scalar(s2, s1, 2.0, None, ALU.add))
            step.wait()
            step.did(dve.reciprocal(s2, s2))
            step.wait()
            step.did(dve.tensor_tensor(s1, s1, s2, ALU.mult))
            step.wait()
            step.did(dve.tensor_tensor(s2, s1, s1, ALU.mult))
            step.wait()
            step.did(dve.tensor_scalar(s3, s2, 2.0 / 19, 2.0 / 17, ALU.mult, ALU.add))
            for odd in (15, 13, 11, 9, 7, 5, 3, 1):
                step.wait()
                step.did(dve.tensor_tensor(s3, s3, s2, ALU.mult))
                step.wait()
                step.did(dve.tensor_scalar(s3, s3, 2.0 / odd, None, ALU.add))
            step.wait()
            step.did(dve.tensor_tensor(s3, s3, s1, ALU.mult))
            step.did(dve.tensor_scalar(s0, lam, -1.0, 0.0, ALU.mult, ALU.max))
            step.wait()
            step.did(dve.tensor_tensor(s3, s3, s0, ALU.add))
            step.wait()
            dve.tensor_scalar(sp[:, 5, :], s3, 4.0, None, ALU.mult)
            dve.tensor_scalar(sp[:, 4, :], s3, -4.0, None, ALU.mult).then_inc(lru_consts, 1)

            def lru_conv(n):
                xc, xin = lru_t[:, n % 2, 0, :], chT[:, n, :]
                w = [vecs[:, V_CW + BT * j + n:V_CW + BT * j + n + 1] for j in range(4)]
                if n >= 2:
                    dve.wait_ge(l_ps, n - 1)
                step.did(dve.tensor_scalar(xc, xin, w[3], vecs[:, V_CB + n:V_CB + n + 1], ALU.mult, ALU.add))
                for d in (1, 2, 3):
                    step.wait()
                    ins = dve.scalar_tensor_tensor(xc[:, d:], xin[:, :T - d], w[3 - d], xc[:, d:], ALU.mult, ALU.add)
                    if d < 3:
                        step.did(ins)
                ins.then_inc(l_xc, 1)

            def lru_input(n):
                xc, tr, ti, a, th, y2, tg, q = (lru_t[:, n % 2, j, :] for j in range(8))
                dve.wait_ge(l_sig, 2 * n + 1)
                step.did(dve.tensor_scalar(q, y2, GELU_3, GELU_1, ALU.mult, ALU.add))
                step.wait()
                dve.tensor_tensor(q, q, chT[:, BT + n, :], ALU.mult).then_inc(l_q, 1)
                dve.wait_ge(l_sig, 2 * n + 2)
                step.did(dve.tensor_tensor(y2, a, a, ALU.mult))
                step.did(dve.scalar_tensor_tensor(ti, ti, 1.0, xc, ALU.add, ALU.mult))
                step.wait()
                step.did(dve.scalar_tensor_tensor(th, y2, 1.0, th, ALU.add, ALU.mult))
                step.wait()
                dve.tensor_scalar(th, th, 0.0, None, ALU.max).then_inc(l_m, 1)

            def lru_scan(n):
                xc, tr, ti, a, th, y2, tg, q = (lru_t[:, n % 2, j, :] for j in range(8))
                dve.wait_ge(l_root, n + 1)
                step.did(dve.scalar_tensor_tensor(th, th, 0.5, ti, ALU.mult, ALU.mult))
                step.wait()
                step.did(dve.tensor_tensor_scan(y2, a, th, 0.0, ALU.mult, ALU.add))
                dve.wait_ge(l_gelu, n + 1)
                step.did(dve.scalar_tensor_tensor(tg, tg, 1.0, chT[:, BT + n, :], ALU.add, ALU.mult))
                step.wait()
                step.did(dve.scalar_tensor_tensor(q, tg, 0.5, y2, ALU.mult, ALU.mult))
                step.wait()
                step.did(dve.tensor_copy(ocT[:, n, 0:T], q))
                step.wait()
                dve.tensor_tensor(ocT[:, n, T:2 * T], q, ocT[:, n, 0:T].bitcast(f32), ALU.subtract).then_inc(l_done, 1)

            lru_conv(0)
            for n in range(BT + 1):
                if n + 1 < BT:
                    lru_conv(n + 1)
                if n < BT:
                    lru_input(n)
                if n >= 1:
                    lru_scan(n - 1)

            dve.wait_ge(sinks_loaded, 16)
            for n in range(len(SWA) + 1):
                if n < len(SWA):
                    big, half, blk, tile0, tiles = SWA[n]
                    w = 512 // tiles
                    head = 8 * big + 4 * half + tile0 % 4
                    cols = slice(4 * n, 4 * n + tiles)
                    scores = swa_s[:, n % 2, :].rearrange("p (a b) -> p a b", a=tiles)
                    mask = consts[:, C_DIAG + P - w:C_DIAG + P].unsqueeze(1).broadcast_to([P, tiles, w])
                    dve.wait_ge(s_sc, n + 1)
                    if n >= 2:
                        dve.wait_ge(s_exp, n - 1)
                    step.did(dve.scalar_tensor_tensor(scores, bank[4 + n % 2][:, :].rearrange("p (a b) -> p a b", a=tiles),
                                                      SWA_D ** -0.5, mask, ALU.mult, ALU.add))
                    step.wait()
                    step.did(dve.reduce_max(stat[:, 0, cols], scores, AX.X))
                    step.wait()
                    step.did(dve.tensor_tensor(stat[:, 0, cols], stat[:, 0, cols], sinks[:, head:head + tiles], ALU.max))
                    step.wait()
                    dve.tensor_scalar(stat[:, 1, cols], stat[:, 0, cols], -1.0, None, ALU.mult)
                    dve.tensor_tensor(stat[:, 3, cols], sinks[:, head:head + tiles], stat[:, 0, cols],
                                      ALU.subtract).then_inc(s_max, 1)
                if n >= 1:
                    m = n - 1
                    tiles = SWA[m][4]
                    cols = slice(4 * m, 4 * m + tiles)
                    dve.wait_ge(s_exp, m + 1)
                    step.did(dve.tensor_tensor(stat[:, 5, cols], stat[:, 2, cols], stat[:, 4, cols], ALU.add))
                    step.wait()
                    step.did(dve.reciprocal(stat[:, 5, cols], stat[:, 5, cols]))
                    step.wait()
                    probs = swa_p[:, m % 2, :].rearrange("p (a b) -> p a b", a=tiles)
                    dve.tensor_tensor(probs, probs, stat[:, 5, cols].unsqueeze(2).broadcast_to([P, tiles, 512 // tiles]),
                                      ALU.mult).then_inc(s_p, 1)
                    if m % 6 == 5:
                        big = SWA[m][0]
                        for j in range(2):
                            dve.wait_ge(s_hi, 2 * big + j + 1)
                            tl = slice(4 * big + 2 * j, 4 * big + 2 * j + 2)
                            dve.tensor_tensor(oaT[:, tl, T:2 * T], bank[2 + j][:, :].rearrange("p (a b) -> p a b", a=2),
                                              oaT[:, tl, 0:T].bitcast(f32), ALU.subtract).then_inc(s_lo, 1)

            stage(G0_RET, 2, 8, copy_tokens(G0_RET, B_RET, 8, lambda i, j: (
                ret[:, bass.ds(i, 1), j, :].rearrange("p a b -> p (a b)"), bank[j][:, :])))

            def rope(h):
                c = (h % 4) * P
                lo_half = ret[:, h // 4:h // 4 + 3:2, :, c:c + 64]
                hi_half = ret[:, h // 4:h // 4 + 3:2, :, c + 64:c + P]
                cos, sin = (consts[:, o:o + P].rearrange("p (t c) -> p t c", t=2).unsqueeze(1).broadcast_to([P, 2, 2, 64])
                            for o in (C_COS, C_SIN))
                if h >= 1:
                    dve.wait_ge(r_rot, h)
                dve.tensor_tensor(rope_t[:, 0], lo_half, cos, ALU.mult)
                dve.tensor_tensor(rope_t[:, 1], hi_half, sin, ALU.mult)
                dve.tensor_tensor(rope_t[:, 2], lo_half, sin, ALU.mult)
                step.did(dve.tensor_tensor(rope_t[:, 3], hi_half, cos, ALU.mult))
                step.wait()
                if h >= 2:
                    dve.wait_ge(r_tr, h - 1)
                dve.tensor_tensor(rot[:, h % 2, :, :, 0:64], rope_t[:, 0], rope_t[:, 1], ALU.subtract)
                dve.tensor_tensor(rot[:, h % 2, :, :, 64:P], rope_t[:, 2], rope_t[:, 3], ALU.add).then_inc(r_rot, 1)

            def ret_lo(h):
                dve.wait_ge(r_hi, h + 1)
                dve.scalar_tensor_tensor(obT[:, h, T:2 * T], bank[7][:, 0:T], 0.5, obT[:, h, 0:T].bitcast(f32),
                                         ALU.mult, ALU.subtract).then_inc(r_lo, 1)

            dve.wait_ge(dec_loaded, 16)
            rope(0)
            rope(1)
            for h in range(RET_HEADS):
                dve.wait_ge(r_sc, h + 1)
                if h >= 2:
                    dve.wait_ge(r_y, h - 1)
                dve.tensor_tensor(sT[:, h % 2, :], bank[5][:, 0:NDEC], decay[:, h, :], ALU.mult).then_inc(r_sT, 1)
                if h >= 1:
                    ret_lo(h - 1)
                if h + 2 < RET_HEADS:
                    rope(h + 2)
                dve.wait_ge(r_y, h + 1)
                for t in range(2):
                    step.did(dve.bn_stats(ret_st[:, t, 0:6], bank[6][:, t * P:(t + 1) * P]))
                step.wait()
                for t in range(2):
                    step.did(dve.bn_aggr(ret_st[:, t, 6:8], ret_st[:, t, 0:6]))
                step.wait()
                dve.tensor_scalar(ret_st[:, :, 7:8], ret_st[:, :, 7:8], EPS, None, ALU.add).then_inc(r_var, 1)
                dve.wait_ge(r_rstd, 2 * h + 2)
                for t in range(2):
                    step.did(dve.tensor_scalar(ret_y[:, h % 2, 1, t, :], bank[6][:, t * P:(t + 1) * P],
                                               ret_st[:, t, 6:7], ret_st[:, t, 7:8], ALU.subtract, ALU.mult))
                dve.wait_ge(r_silu, h + 1)
                step.did(dve.scalar_tensor_tensor(ret_y[:, h % 2, 2, :, :], ret_y[:, h % 2, 0, :, :], 1.0,
                                                  ret[:, 6 + h // 4, :, (h % 4) * P:(h % 4) * P + P], ALU.add, ALU.mult))
                step.wait()
                if h >= 2:
                    dve.wait_ge(r_otr, h - 1)
                dve.tensor_tensor(ret_y[:, h % 2, 3, :, :], ret_y[:, h % 2, 1, :, :], ret_y[:, h % 2, 2, :, :],
                                  ALU.mult).then_inc(r_o, 1)
            ret_lo(RET_HEADS - 1)

            def merge_evac(b):
                def evac(i, u):
                    if u % 3 != 2:
                        return
                    n = u // 3
                    tile = bass.ds(i * 4 + n, 1)
                    tanh, term, total = (br_t[:, n % 2, j, :] for j in range(3))
                    mrg = merged[:, tile, :].rearrange("p a b -> p (a b)")
                    dve.wait_ge(g_tanh, i * 4 + (KT * b + n + 1))
                    dve.wait_ge(unit_used, i * 12 + (RING * (G0_BR + G_BR * b) + u + 1))
                    src = bank[(2 * n + 1) % 4][:, 0:T]
                    if b == 0:
                        dve.scalar_tensor_tensor(mrg, tanh, 1.0, src, ALU.add, ALU.mult).then_inc(prod_free, 2)
                        return
                    step.did(dve.scalar_tensor_tensor(term, tanh, 1.0, src, ALU.add, ALU.mult))
                    step.wait()
                    if b == 1:
                        dve.tensor_tensor(mrg, mrg, term, ALU.add).then_inc(prod_free, 2)
                        return
                    step.did(dve.tensor_tensor(total, mrg, term, ALU.add))
                    step.wait()
                    hi = mT[:, tile, 0:T].rearrange("p a b -> p (a b)")
                    lo = mT[:, tile, T:2 * T].rearrange("p a b -> p (a b)")
                    step.did(dve.tensor_scalar(hi, total, 0.5, None, ALU.mult))
                    step.wait()
                    dve.scalar_tensor_tensor(lo, total, 0.5, hi.bitcast(f32), ALU.mult, ALU.subtract).then_inc(prod_free, 2)
                return evac
            for b in range(3):
                stage(G0_BR + G_BR * b, 3, 4, merge_evac(b), 4 * (0, 1, 3)[b])

            def add_tokens(g0, b0):
                def evac(i, u):
                    if u == 7:
                        for t in range(2):
                            wait_half(t, i, 8, g0, b0)
                            dst = x1[:, t, bass.ds(i * 512, 512)]
                            dve.tensor_tensor(dst, dst, bank[t][:, :], ALU.add).then_inc(prod_free, 1)
                return evac

            dve.wait_ge(x1_loaded, 16)
            stage(G0_OUT, 2, 4, add_tokens(G0_OUT, B_OUT))
            norm(1)
            stage(G0_K, 1, 8, copy_channels(G0_K, lambda i, j: (
                kT[:, bass.ds(i * 2 + j, 1), :].rearrange("p a b -> p (a b)"))))
            stage(G0_V, 2, 4, copy_tokens(G0_V, B_V, 8, lambda i, j: (v[:, j, bass.ds(i * 512, 512)], bank[j][:, :])))
            norm(2)
            stage(G0_Q, 1, 8, copy_channels(G0_Q, lambda i, j: (
                qT[:, bass.ds(i * 2 + j, 1), :].rearrange("p a b -> p (a b)"))))

            for h in range(X_HEADS):
                cols = slice(2 * h, 2 * h + 2)
                dve.wait_ge(x_sc, h + 1)
                step.did(dve.reduce_max(stat[:, 0, cols], bank[4][:, :].rearrange("p (a b) -> p a b", a=2), AX.X))
                step.wait()
                dve.tensor_scalar(stat[:, 1, cols], stat[:, 0, cols], -(X_D ** -0.5), None, ALU.mult).then_inc(x_max, 1)
                dve.wait_ge(x_exp, h + 1)
                step.did(dve.reciprocal(stat[:, 3, cols], stat[:, 2, cols]))
                step.wait()
                for t in range(2):
                    ins = dve.tensor_scalar(xp[:, t, 0:MEM], xp[:, t, 0:MEM], stat[:, 3, 2 * h + t:2 * h + t + 1],
                                            None, ALU.mult)
                ins.then_inc(x_p, 1)
                for j in range(2):
                    dve.wait_ge(x_hi, 2 * h + j + 1)
                    tl = slice(4 * h + 2 * j, 4 * h + 2 * j + 2)
                    dve.tensor_tensor(xT[:, tl, T:2 * T], bank[6 + j][:, :].rearrange("p (a b) -> p a b", a=2),
                                      xT[:, tl, 0:T].bitcast(f32), ALU.subtract).then_inc(x_lo, 1)

            stage(G0_O, 2, 4, add_tokens(G0_O, B_O))
            norm(3)

            def ffn_evac(i, u):
                conv, tanh, gated, full = (ffn_t[:, j, :] for j in range(4))
                if u == 1:
                    dve.wait_ge(unit_used, i * 4 + (RING * G0_UP + 2))
                    w = [vecs[:, bass.ds(i + (V_FW + FT * j), 1)] for j in range(3)]
                    step.did(dve.tensor_scalar(conv, bank[0][:, 0:T], w[2], vecs[:, bass.ds(i + V_FB, 1)],
                                               ALU.mult, ALU.add))
                    step.wait()
                    step.did(dve.scalar_tensor_tensor(conv[:, 1:], bank[0][:, 0:T - 1], w[1], conv[:, 1:],
                                                      ALU.mult, ALU.add))
                    step.wait()
                    dve.scalar_tensor_tensor(conv[:, 2:], bank[0][:, 0:T - 2], w[0], conv[:, 2:],
                                             ALU.mult, ALU.add).then_inc(prod_free, 1)
                if u == 3:
                    dve.wait_ge(f_tanh, i + 1)
                    step.did(dve.scalar_tensor_tensor(gated, tanh, 1.0, conv, ALU.add, ALU.mult))
                    step.wait()
                    dve.wait_ge(unit_used, i * 4 + (RING * G0_UP + 4))
                    dve.scalar_tensor_tensor(full, gated, 0.5, bank[1][:, 0:T], ALU.mult, ALU.mult).then_inc(prod_free, 1)
                    dve.wait_ge(prod_free, i * 2 + (P_UP + 2))
                    hi = actT[:, bass.ds(i, 1), 0:T].rearrange("p a b -> p (a b)")
                    lo = actT[:, bass.ds(i, 1), T:2 * T].rearrange("p a b -> p (a b)")
                    step.did(dve.tensor_copy(hi, full))
                    step.wait()
                    step.did(dve.tensor_tensor(lo, full, hi.bitcast(f32), ALU.subtract))
            stage(G0_UP, 1, FT, ffn_evac, 5)
            step.wait()
            dve.tensor_copy(stat[:, 0, 0:1], stat[:, 0, 0:1]).then_inc(act_whole, 1)

            def down(c, last):
                for u in range(len(DOWN_K)):
                    if u == len(DOWN_K) - 1:
                        for t in range(2):
                            wait_half(t, c, len(DOWN_K), G0_DOWN, B_DOWN)
                            dst = x1[:, t, c * 512:(c + 1) * 512] if last else x1[:, t, bass.ds(c * 512, 512)]
                            dve.tensor_tensor(dst, dst, bank[t][:, :], ALU.add).then_inc(prod_free, 1)
                    nxt = (u + RING) % len(DOWN_K)
                    if not (last and u + RING >= len(DOWN_K)):
                        lo_split(c * G_DOWN + (G0_DOWN + 1 + u // RING), u % RING, down_width(nxt))
            with dve.Fori(0, DOWN_BLOCKS - 1) as c:
                down(c, False)
            down(DOWN_BLOCKS - 1, True)

            mean_squares(4)
            dve.wait_ge(n_rstd, 10)
            dve.wait_ge(gf_loaded, 16)
            for t in range(2):
                dve.scalar_tensor_tensor(outn[:, t, :], x1[:, t, :], rstd[:, 8 + t:9 + t], gfin[:, :],
                                         ALU.mult, ALU.mult).then_inc(out_ready, 1)

        @block.tensor
        def _(pe):
            def passes(out, w_stationary, hi_w, lo_w, hi_x, lo_x, start, stop):
                pairs = ((hi_w, hi_x), (hi_w, lo_x), (lo_w, hi_x)) if w_stationary else \
                        ((hi_x, hi_w), (hi_x, lo_w), (lo_x, hi_w))
                for n, (st, mv) in enumerate(pairs):
                    ins = pe.matmul(out, st, mv, start=start and n == 0, stop=stop and n == 2)
                return ins

            def channel_unit(g, s, X, k0, out, first, last):
                pe.wait_ge(lo_ready, g * RING + (s + 1))
                for b in range(UT):
                    c = slice(b * P, (b + 1) * P)
                    ins = passes(out[:, 0:T], True, whi[:, s, c], wlo[:, s, c], X[:, k0 + b, 0:T], X[:, k0 + b, T:2 * T],
                                 first and b == 0, last and b == UT - 1)
                ins.then_inc(unit_used, 1)

            def token_unit(g, s, X, k0, nk, width, first, last):
                pe.wait_ge(lo_ready, g * RING + (s + 1))
                for t in range(2):
                    for b in range(nk):
                        c = slice(b * width, (b + 1) * width)
                        k = k0 + b
                        ins = passes(bank[t][:, 0:width], False, whi[:, s, c], wlo[:, s, c],
                                     X[:, k, t * P:(t + 1) * P], X[:, k, T + t * P:T + (t + 1) * P],
                                     first and b == 0, last and b == nk - 1)
                    if last and t == 0:
                        ins.then_inc(half0_done, 1)
                    if first and t == 0:
                        yield
                ins.then_inc(unit_used, 1)

            def channel_stage(g0, p0, pairs, X):
                with pe.Fori(0, pairs) as i:
                    for j in range(2):
                        pe.wait_ge(prod_free, i * 2 + (p0 + j - 1))
                        for u in range(2):
                            channel_unit(i + g0, 2 * j + u, X, UT * u, bank[j], u == 0, u == 1)

            def token_block(g, p, X, ks, width):
                k0 = 0
                pe.wait_ge(prod_free, p - 1)
                for u, nk in enumerate(ks):
                    for _ in token_unit(g + u // RING, u % RING, X, k0, nk, width, u == 0, u == len(ks) - 1):
                        pe.wait_ge(prod_free, p)
                    k0 += nk

            def token_stage(g0, p0, blocks, X, ks=(2,) * 8, width=512):
                with pe.Fori(0, blocks) as i:
                    token_block(i * (len(ks) // RING) + g0, i * 2 + p0, X, ks, width)

            def norm(which):
                _, xn_, _, _ = NORM[which]
                for b in range(NB):
                    if b == 0:
                        pe.wait_ge(n_xn, 2 * which + 2)
                        if which == 0:
                            pe.wait_ge(c_loaded, 32)
                    if NB * which + b >= 4:
                        pe.wait_ge(n_lo, NB * which + b - 3)
                    for k in (2 * b, 2 * b + 1):
                        for t in range(2):
                            c = (k % 2) * T + t * P
                            ins = pe.transpose(bank[4 + b % 4][:, c:c + P], xn_[:, t, k * P:(k + 1) * P], ident)
                    ins.then_inc(n_tr, 1)
                pe.wait_ge(n_lo, NB * (which + 1))

            norm(0)
            for j in range(2):
                for u in range(2):
                    channel_unit(0, 2 * j + u, xT, UT * u, bank[j], u == 0, u == 1)
            with pe.Fori(1, P_VA // 2) as i:
                for j in range(2):
                    pe.wait_ge(prod_free, i * 2 + (j - 1))
                    for u in range(2):
                        channel_unit(i, 2 * j + u, xT, UT * u, bank[j], u == 0, u == 1)
            token_block(G0_VA, P_VA, xT, (4,) * 4, SWA_KV * SWA_D)

            pe.wait_ge(lruw_loaded, 16)
            for n in range(BT):
                pe.wait_ge(l_xc, n + 1)
                if n >= 2:
                    pe.wait_ge(l_sig, 2 * (n - 1))
                for j in range(2):
                    ins = pe.matmul(bank[4 + n % 2][:, j * T:(j + 1) * T], lru_w[:, j, n, :], lru_t[:, n % 2, 0, :],
                                    start=True, stop=True)
                ins.then_inc(l_ps, 1)

            def swa_scores(n):
                big, half, blk, tile0, tiles = SWA[n]
                w = 512 // tiles
                rows = slice(64 * half, 64 * half + 64)
                if n >= 2:
                    pe.wait_ge(s_max, n - 1)
                for j in range(tiles):
                    ins = pe.matmul(bank[4 + n % 2][:, j * w:(j + 1) * w], chT[rows, 16 + tile0 + j, blk * P:blk * P + P],
                                    chT[rows, 24 + big, 0:w], start=True, stop=True)
                ins.then_inc(s_sc, 1)

            pe.wait_ge(prod_free, P_RET)
            pe.wait_ge(l_sig, 2 * BT)
            swa_scores(0)
            swa_scores(1)
            for n, (big, half, blk, tile0, tiles) in enumerate(SWA):
                pe.wait_ge(s_p, n + 1)
                if n >= 1:
                    pe.wait_ge(s_pT, n)
                for j in range(4):
                    ins = pe.transpose(bank[6][:, j * P:(j + 1) * P], swa_p[:, n % 2, j * P:(j + 1) * P], ident)
                ins.then_inc(s_tr, 1)
                if n + 2 < len(SWA):
                    swa_scores(n + 2)
                pe.wait_ge(s_pT, n + 1)
                if n == 6:
                    pe.wait_ge(s_lo, 2)
                kv = 2 * big + half
                for j in range(tiles):
                    local = (tile0 + j) % 4
                    c = (local % 2) * T + blk * P
                    out = bank[2 + local // 2][64 * half:64 * half + 64, c:c + P]
                    nb = 4 // tiles
                    for kb in range(nb):
                        at_ = (j * nb + kb) * P
                        ins = pe.matmul(out, va[:, kb, kv * 64:(kv + 1) * 64], swa_pT[:, n % 2, at_:at_ + P],
                                        start=kb == 0, stop=kb == nb - 1)
                ins.then_inc(s_pv, 1)

            token_stage(G0_RET, P_RET, 8, xT)

            def ret_transpose(h):
                pe.wait_ge(r_rot, h + 1)
                if h >= 1:
                    pe.wait_ge(r_qkT, h)
                for qk in range(2):
                    for t in range(2):
                        c = qk * T + t * P
                        ins = pe.transpose(bank[4][:, c:c + P], rot[:, h % 2, qk, t, :], ident)
                ins.then_inc(r_tr, 1)

            def ret_out(h):
                pe.wait_ge(r_o, h + 1)
                if h >= 1:
                    pe.wait_ge(r_lo, h)
                for t in range(2):
                    ins = pe.transpose(bank[7][:, t * P:(t + 1) * P], ret_y[:, h % 2, 3, t, :], ident)
                ins.then_inc(r_otr, 1)

            ret_transpose(0)
            for h in range(RET_HEADS):
                pe.wait_ge(r_qkT, h + 1)
                if h >= 1:
                    pe.wait_ge(r_sT, h)
                q_, k_ = qkT[:, h % 2, 0:T], qkT[:, h % 2, T:2 * T]
                pe.matmul(bank[5][:, 0:T], k_[:, 0:P], q_, start=True, stop=True)
                pe.matmul(bank[5][:, T:T + P], k_[:, P:T], q_[:, P:T], start=True, stop=True).then_inc(r_sc, 1)
                if h + 1 < RET_HEADS:
                    ret_transpose(h + 1)
                if h >= 1:
                    ret_out(h - 1)
                pe.wait_ge(r_sT, h + 1)
                if h >= 1:
                    pe.wait_ge(r_o, h)
                v_ = ret[:, 4 + h // 4, :, (h % 4) * P:(h % 4) * P + P]
                pe.matmul(bank[6][:, 0:P], sT[:, h % 2, 0:P], v_[:, 0, :], start=True, stop=True)
                pe.matmul(bank[6][:, P:T], sT[:, h % 2, P:T], v_[:, 0, :], start=True, stop=False)
                pe.matmul(bank[6][:, P:T], sT[:, h % 2, T:T + P], v_[:, 1, :], start=False, stop=True).then_inc(r_y, 1)
            ret_out(RET_HEADS - 1)

            pe.wait_ge(prod_free, P_BR)
            pe.wait_ge(s_lo, 4)
            pe.wait_ge(r_lo, RET_HEADS)
            pe.wait_ge(l_done, BT)
            for b, oT in enumerate((ocT, oaT, obT)):
                with pe.Fori(0, 4) as i:
                    for n in range(4):
                        p = i * 8 + (P_BR + 2 * KT * b + 2 * n)
                        g, units = i * 3 + (G0_BR + G_BR * b), [3 * n, 3 * n + 1, 3 * n + 2]
                        pe.wait_ge(prod_free, p - 2)
                        for j, u in enumerate(units[:2]):
                            channel_unit(g + u // RING, u % RING, xT, UT * j, bank[2 * n % 4], j == 0, j == 1)
                        u = units[2]
                        channel_unit(g + u // RING, u % RING, oT, 0, bank[(2 * n + 1) % 4], True, True)

            pe.wait_ge(prod_free, P_OUT)
            token_stage(G0_OUT, P_OUT, 4, mT)
            norm(1)
            channel_stage(G0_K, P_K, 8, memT)
            token_stage(G0_V, P_V, 4, memT)
            norm(2)
            channel_stage(G0_Q, P_Q, 8, xT)

            def x_scores(h):
                if h >= 1:
                    pe.wait_ge(x_exp, h)
                for t in range(2):
                    for j in range(4):
                        ins = pe.matmul(bank[4][:, t * MEM:(t + 1) * MEM], qT[:, 4 * h + j, t * P:(t + 1) * P],
                                        kT[:, 4 * h + j, :], start=j == 0, stop=j == 3)
                ins.then_inc(x_sc, 1)

            pe.wait_ge(prod_free, P_O)
            x_scores(0)
            for h in range(X_HEADS):
                pe.wait_ge(x_p, h + 1)
                if h >= 1:
                    pe.wait_ge(x_pT, h)
                for mb in range(2):
                    for t in range(2):
                        c = mb * T + t * P
                        ins = pe.transpose(bank[5][:, c:c + P], xp[:, t, mb * P:(mb + 1) * P], ident)
                ins.then_inc(x_tr, 1)
                if h + 1 < X_HEADS:
                    x_scores(h + 1)
                pe.wait_ge(x_pT, h + 1)
                for j in range(2):
                    if h >= 1:
                        pe.wait_ge(x_lo, 2 * h - 1 + j)
                    for d in range(2):
                        c0 = (4 * h + 2 * j + d) * P
                        for mb in range(2):
                            ins = pe.matmul(bank[6 + j][:, d * T:(d + 1) * T], v[:, mb, c0:c0 + P],
                                            xpT[:, 0, mb * T:(mb + 1) * T], start=mb == 0, stop=mb == 1)
                    ins.then_inc(x_pv, 1)
            pe.wait_ge(x_lo, 2 * X_HEADS)
            token_stage(G0_O, P_O, 4, xT)
            norm(3)
            channel_stage(G0_UP, P_UP, FT, xT)
            pe.wait_ge(act_whole, 1)
            token_stage(G0_DOWN, P_DOWN, DOWN_BLOCKS, actT, DOWN_K)


def channel_units(w):
    k, n = w.shape
    t = w.reshape(k // (UT * P), UT, P, n // P, P).transpose(3, 0, 2, 1, 4)
    return t.reshape(n // P, k // (UT * P), P, UW)


def token_units(w, nk, width):
    k, n = w.shape
    return w.reshape(k // (nk * P), nk, P, n // width, width).transpose(3, 0, 2, 1, 4).reshape(-1, UW)


def lay_out(a):
    w_in, wb = a["w_in"][0], a["w_branch"][0]
    sizes = (1024, 256, 256, 1024, 1024, 1024, 1024, 1024, 1024, D, D, D)
    at = np.cumsum((0,) + sizes)
    q_a, k_a, v_a, q_r, k_r, v_r, g_r, x_c, y_c, ga, gb, gc = (w_in[:, at[i]:at[i + 1]] for i in range(12))
    order = [h for m in range(8) for h in (m + 4 * (m // 4), m + 4 * (m // 4) + 4)]
    q_a = q_a.reshape(D, SWA_HEADS, SWA_D)[:, order].reshape(D, -1)
    wb_a = wb[0].reshape(SWA_HEADS, SWA_D, D)[order].reshape(BW, D)

    def branch(gate, w):
        return np.concatenate([channel_units(gate), channel_units(w)], axis=1).reshape(-1, UW)

    up = a["ffn_w_up"][0]
    wkv = a["xattn_wkv"][0]
    stream = np.concatenate([
        channel_units(np.concatenate([x_c, y_c, q_a, k_a], axis=1)).reshape(-1, UW),
        token_units(v_a, 4, 256),
        token_units(np.concatenate([q_r, k_r, v_r, g_r], axis=1), 2, 512),
        branch(gc, wb[2]), branch(ga, wb_a), branch(gb, wb[1]),
        token_units(a["w_out"][0], 2, 512),
        channel_units(wkv[:, :D]).reshape(-1, UW),
        token_units(wkv[:, D:], 2, 512),
        channel_units(a["xattn_wq"][0]).reshape(-1, UW),
        token_units(a["xattn_wo"][0], 2, 512),
        np.concatenate([channel_units(up[:, :F]), channel_units(up[:, F:])], axis=1).reshape(-1, UW),
    ], axis=0)
    down = []
    w_down = a["ffn_w_down"][0].reshape(FT, P, DOWN_BLOCKS, 512)
    for c in range(DOWN_BLOCKS):
        k0 = 0
        for k in DOWN_K:
            down.append(w_down[k0:k0 + k, :, c].transpose(1, 0, 2).reshape(-1, 512))
            k0 += k

    def tiles(v):
        return v.reshape(-1, P).T

    vecs = np.concatenate([tiles(a[n]) for n in (
        "mem_norm_g", "norm_mix_g", "norm_xattn_g", "norm_ffn_g", "lru_conv_w", "lru_conv_b", "lru_ba", "lru_bx",
        "lru_lambda", "ffn_conv_w", "ffn_conv_b")], axis=1)
    lru_w = np.stack([a["lru_wa"][0], a["lru_wx"][0]]).transpose(2, 0, 1, 3)
    return {"x": a["x"][0], "mem": a["mem"][0], "stream": stream, "down": np.concatenate(down, axis=0), "vecs": vecs,
            "sinks": a["attn_sinks"][0], "lru_w": lru_w, "final_g": a["final_norm_g"], **shape_constants()}


def shape_constants():
    f = np.float32
    theta = (f(10000.0) ** (-np.linspace(0.0, 1.0, RET_D // 2, dtype=f))).astype(f)
    ang = np.arange(T, dtype=f)[:, None] * theta[None, :]
    i, j = np.arange(P)[:, None], np.arange(P)[None, :]

    def half(t):
        return t.astype(f).reshape(2, P, RET_D // 2).transpose(1, 0, 2).reshape(P, P)

    consts = np.concatenate([np.eye(P, dtype=f), half(np.cos(ang)), half(np.sin(ang)),
                             np.where(j > i, 0.0, -1e30).astype(f), np.where(j <= i, 0.0, -1e30).astype(f)], axis=1)
    log_gamma = np.log1p(-np.exp2(-5.0 - np.arange(RET_HEADS)))
    gap = (np.arange(T)[None, :] - np.arange(P)[:, None]).astype(float)
    full = np.where(gap[:, None] >= 0, np.exp(np.maximum(gap, 0)[:, None] * log_gamma[None, :, None]), 0.0)
    full = full * RET_D ** -0.5
    decay = np.concatenate([full, full[:, :, 0:P]], axis=2).astype(f)
    return {"consts": consts, "decay": decay}


INPUTS = ["x", "mem", "stream", "down", "vecs", "sinks", "lru_w", "final_g", "consts", "decay"]


def kernel(**inputs):
    import concourse.bacc as bacc
    from concourse.bass_utils import run_bass_kernel_spmd

    nc = bacc.Bacc("TRN2", target_bir_lowering=False, num_devices=1)
    laid = lay_out({k: np.asarray(v) for k, v in inputs.items()})
    arrays, args = {}, []
    for name in INPUTS:
        arr = np.ascontiguousarray(laid[name])
        arrays[f"in_{name}"] = arr
        args.append(nc.dram_tensor(f"in_{name}", arr.shape, mybir.dt.from_np(arr.dtype), kind="ExternalInput").ap())
    out = nc.dram_tensor("out_y", (T, D), mybir.dt.float32, kind="ExternalOutput").ap()
    trunk_kernel(nc, *args, out)
    r = run_bass_kernel_spmd(nc, [arrays], core_ids=[0])
    return r.results[0]["out_y"].reshape(1, T, D)
```

```python
from contextlib import ExitStack

import numpy as np

import concourse.bass as bass
from concourse import mybir

P = 128
D = 2048
T = 256
KT = D // P
MEM = 256
EPS = 1e-6
BW = 1024
BT = BW // P
SWA_HEADS, SWA_KV, SWA_D = 16, 4, 64
RET_HEADS, RET_D = 8, 128
X_HEADS, X_D = 4, 512
F = 5504
FT = F // P
RING = 4
UT = 8
UW = UT * P

DOWN_K = [2] * 8 + [1] * 5 + [2] * 11
assert sum(DOWN_K) == FT and len(DOWN_K) % RING == 0
DOWN_BLOCKS = D // 512

G_CH = 26 * 2 // RING
G_VA = 1
G_RET = 8 * 8 // RING
G_BR = KT * 3 // RING
G_SQ = 4 * 8 // RING
G_UP = FT * 4 // RING
G0_VA = G_CH
G0_RET = G0_VA + G_VA
G0_BR = G0_RET + G_RET
G0_OUT = G0_BR + 3 * G_BR
G0_K = G0_OUT + G_SQ
G0_Q = G0_K + G_SQ
G0_V = G0_Q + G_SQ
G0_O = G0_V + G_SQ
G0_UP = G0_O + G_SQ
G0_DOWN = G0_UP + G_UP
G_DOWN = len(DOWN_K) // RING
FULL_ROWS = G0_DOWN * RING * P
DOWN_ROWS = FT * P

V_MEM, V_MIX, V_X, V_FFN = 0, 16, 32, 48
V_CW, V_CB, V_BA, V_BX, V_LAM = 64, 96, 104, 112, 120
V_FW, V_FB = 128, 128 + 3 * FT
NV = V_FB + FT
C_ID, C_COS, C_SIN, C_PREV, C_DIAG = 0, 128, 256, 384, 512
NC_ = 640
NDEC = 3 * P
GELU_1 = 2.0 * 0.7978845608028654
GELU_3 = GELU_1 * 0.044715
RSQRT_SEED = 0x5F3759DF


class Steps:

    def __init__(self, eng, sem):
        self.eng, self.sem, self.n, self.off = eng, sem, 0, 0

    def did(self, ins):
        ins.then_inc(self.sem, 1)
        self.n += 1
        return self.n + self.off

    def wait(self):
        self.eng.wait_ge(self.sem, self.n + self.off)

    def enter(self, i, per, first=0):
        self.start, self.per, self.first = self.n, per, first
        self.n -= first * per
        self.off = i * per

    def leave(self, iters):
        assert self.n + self.first * self.per - self.start == self.per, (self.n, self.start, self.per)
        self.n, self.off = self.start + self.per * (iters - self.first), 0


def trunk_kernel(nc, x_d, mem_d, stream_d, down_d, vecs_d, sinks_d, lru_w_d, final_g_d, consts_d, decay_d, out_d):
    f32, f32r, i32 = mybir.dt.float32, mybir.dt.float32r, mybir.dt.int32
    ALU, ACT, AX = mybir.AluOpType, mybir.ActivationFunctionType, mybir.AxisListType
    KB = 256

    ctx = ExitStack()
    with ctx:
        def sb(name, shape, dt=f32):
            return ctx.enter_context(nc.sbuf_tensor(name, shape, dt))

        def sem(name):
            return ctx.enter_context(nc.semaphore(name))

        raw = sb("raw", [P, RING, UW])
        whi = sb("whi", [P, RING, UW], f32r)
        wlo = sb("wlo", [P, RING, UW], f32r)
        xT = sb("xT", [P, KT, 2 * T], f32r)
        vecs = sb("vecs", [P, NV])
        consts = sb("consts", [P, NC_])
        sinks = sb("sinks", [P, SWA_HEADS])
        ss = sb("ss", [P, 5, 2, 4])
        ms = sb("ms", [P, 2, 2])
        rstd = sb("rstd", [P, 10])
        sp = sb("sp", [P, 8, BT])
        stat = sb("stat", [P, 6, 48])
        ret_st = sb("ret_st", [P, 2, 8])
        ret_nw = sb("ret_nw", [P, 3, 2])
        ident = consts[:, C_ID:C_ID + P]

        def at(kib, name, shape, dt=f32):
            with ExitStack() as tmp:
                if kib:
                    tmp.enter_context(nc.sbuf_tensor(name + "_below", [P, int(kib * KB)], f32))
                return tmp.enter_context(nc.sbuf_tensor(name, shape, dt))

        xr = at(0, "xr", [P, 2, D])
        xn = at(16, "xn", [P, 2, D])
        chT = at(32, "chT", [P, 26, T])
        va = at(58, "va", [P, 2, SWA_KV * SWA_D])
        lru_w = at(92, "lru_w", [P, 2, BT, P])
        lru_t = at(104, "lru_t", [P, 2, 8, T])
        ocT = at(0, "ocT", [P, BT, 2 * T], f32r)
        oaT = at(16, "oaT", [P, BT, 2 * T], f32r)
        obT = at(0, "obT", [P, BT, 2 * T], f32r)
        ret = at(60, "ret", [P, 2, 4, RET_HEADS * P])
        swa_s = at(92, "swa_s", [P, 2, 512])
        swa_p = at(96, "swa_p", [P, 2, 512])
        swa_pT = at(100, "swa_pT", [P, 2, 512])
        decay = at(92, "decay", [P, RET_HEADS, NDEC])
        rot = at(48, "rot", [P, 2, 2, 2, P])
        qkT = at(52, "qkT", [P, 2, 2 * T])
        rope_t = at(56, "rope_t", [P, 4, 2, 2, 64])
        sT = at(104, "sT", [P, 2, NDEC])
        ret_y = at(107, "ret_y", [P, 2, 4, 2, P])
        br_t = at(115, "br_t", [P, 2, 3, T])
        merged = at(32, "merged", [P, KT, T])
        mT = at(60, "mT", [P, KT, 2 * T], f32r)
        x1 = at(92, "x1", [P, 2, D])
        memr = at(0, "memr", [P, 2, D])
        memT = at(16, "memT", [P, KT, 2 * T], f32r)
        kT = at(48, "kT", [P, KT, MEM])
        x1n = at(64, "x1n", [P, 2, D])
        qT = at(0, "qT", [P, KT, T])
        v = at(64, "v", [P, 2, D])
        xp = at(80, "xp", [P, 2, 512])
        xpT = at(84, "xpT", [P, X_HEADS, 512])
        x2n = at(0, "x2n", [P, 2, D])
        actT = at(0, "actT", [P, FT, 2 * T], f32r)
        ffn_t = at(108, "ffn_t", [P, 4, T])
        gfin = at(112, "gfin", [P, D])
        junk = at(120, "junk", [P, 512])

        bank = [ctx.enter_context(nc.psum_tensor(f"bank{b}", [P, 512], f32)) for b in range(8)]

        raw_loaded = [sem(f"raw_loaded{s}") for s in range(RING)]
        hi_ready, lo_ready, unit_used = sem("hi_ready"), sem("lo_ready"), sem("unit_used")
        half0_done, prod_free = sem("half0_done"), sem("prod_free")
        x_loaded = [sem(f"x_loaded{b}") for b in range(4)]
        c_loaded, lruw_loaded, dec_loaded = sem("c_loaded"), sem("lruw_loaded"), sem("dec_loaded")
        sinks_loaded = sem("sinks_loaded")
        x1_loaded, mem_loaded, gf_loaded, stored = sem("x1_loaded"), sem("mem_loaded"), sem("gf_loaded"), sem("stored")
        dve_step, act_step = sem("dve_step"), sem("act_step")
        n_sq, n_xn, n_tr, n_hi, n_lo = (sem("norm_" + w) for w in ("sq", "xn", "tr", "hi", "lo"))
        l_xc, l_ps, l_sig, l_q, l_gelu, l_done = (sem("lru_" + w) for w in ("xc", "ps", "sig", "q", "gelu", "done"))
        r_prod = sem("ret_rope_prod")
        l_m, l_root, r_sg, r_stat, r_yn = (sem(w) for w in (
            "lru_m", "lru_root", "ret_silu_g", "ret_stat", "ret_yn"))
        lru_abs, lru_z, lru_consts = sem("lru_abs"), sem("lru_z"), sem("lru_consts")
        s_sc, s_max, s_exp, s_p, s_tr, s_pT, s_pv, s_hi, s_lo = (
            sem("swa_" + w) for w in ("sc", "max", "exp", "p", "tr", "pT", "pv", "hi", "lo"))
        r_rot, r_tr, r_qkT, r_sc, r_sT, r_y, r_silu, r_o, r_otr, r_hi, r_lo = (
            sem("ret_" + w) for w in ("rot", "tr", "qkT", "sc", "sT", "y", "silu", "o", "otr", "hi", "lo"))
        g_tanh, merged_done = sem("gate_tanh"), sem("merged_done")
        x_sc, x_max, x_exp, x_p, x_tr, x_pT, x_pv, x_hi, x_lo = (
            sem("xa_" + w) for w in ("sc", "max", "exp", "p", "tr", "pT", "pv", "hi", "lo"))
        f_tanh = sem("ffn_tanh")
        out_ready, act_whole = sem("out_ready"), sem("act_whole")
        block = ctx.enter_context(nc.Block())

        NORM = [(xr, xn, xT, V_MIX), (memr, memr, memT, V_MEM), (x1, x1n, xT, V_X), (x1, x2n, xT, V_FFN),
                (x1, None, None, None)]
        NB = KT // 2
        P_CH = 0
        P_VA = 26
        P_RET = P_VA + 2
        P_BR = P_RET + 16
        P_OUT = P_BR + 3 * 2 * KT
        P_K = P_OUT + 8
        P_Q = P_K + KT
        P_V = P_Q + KT
        P_O = P_V + 8
        P_UP = P_O + 8
        P_DOWN = P_UP + 2 * FT
        B_VA, B_RET, B_OUT, B_V, B_O, B_DOWN = 0, 1, 9, 13, 17, 21

        def swa_groups():
            for big in range(2):
                for half in range(2):
                    yield big, half, 0, 4 * big, 4
                    yield big, half, 1, 4 * big, 2
                    yield big, half, 1, 4 * big + 2, 2

        SWA = list(swa_groups())

        LRU_PERIOD = 7
        RET_PERIOD = 5
        RET_FROM = 4
        SWA_FROM = 60

        def down_width(s):
            return DOWN_K[s] * 512

        @block.sync
        def _(sp_eng):
            def load(g, s):
                sp_eng.dma_start(raw[:, s, :], stream_d[bass.ds((g * RING + s) * P, P), :]).then_inc(raw_loaded[s], 16)

            for b in range(4):
                sp_eng.dma_start(xr[:, :, b * 512:(b + 1) * 512],
                                 x_d[:, b * 512:(b + 1) * 512].rearrange("(t p) d -> p t d", p=P)).then_inc(x_loaded[b], 16)
            for s in range(RING):
                load(0, s)
            with sp_eng.Fori(1, G0_DOWN) as g:
                for s in range(RING):
                    sp_eng.wait_ge(lo_ready, g * RING + (s + 1 - RING))
                    load(g, s)
            with sp_eng.Fori(0, DOWN_BLOCKS) as c:
                row = 0
                for u, k in enumerate(DOWN_K):
                    s = u % RING
                    sp_eng.wait_ge(lo_ready, c * len(DOWN_K) + (G0_DOWN * RING + u + 1 - RING))
                    src = down_d[bass.ds(c * DOWN_ROWS + row, k * P), :].rearrange("(p b) n -> p (b n)", p=P)
                    sp_eng.dma_start(raw[:, s, 0:512 * k], src).then_inc(raw_loaded[s], 16)
                    row += k * P
            for t in range(2):
                sp_eng.wait_ge(out_ready, t + 1)
                sp_eng.dma_start(out_d[t * P:(t + 1) * P, :], x1[:, t, :]).then_inc(stored, 16)
            sp_eng.wait_ge(stored, 32)

        @block.gpsimd
        def _(pool):
            pool.dma_start(lru_w[:, :, :, :], lru_w_d).then_inc(lruw_loaded, 16)
            pool.dma_start(sinks[:, :], sinks_d[None, :].broadcast_to([P, SWA_HEADS])).then_inc(sinks_loaded, 16)
            pool.wait_ge(s_lo, 4)
            pool.dma_start(decay[:, :, :], decay_d).then_inc(dec_loaded, 16)

            for h in range(RET_HEADS):
                c = h * P
                lo_half = ret[:, :, 0:2, c:c + 64].rearrange("p t k c -> p k t c")
                hi_half = ret[:, :, 0:2, c + 64:c + P].rearrange("p t k c -> p k t c")
                cos, sin = (consts[:, o:o + P].rearrange("p (t c) -> p t c", t=2).unsqueeze(1).broadcast_to([P, 2, 2, 64])
                            for o in (C_COS, C_SIN))
                if h == 0:
                    pool.wait_ge(prod_free, P_BR)
                if h >= 1:
                    pool.wait_ge(r_rot, 2 * h)
                for j, (half, ang) in enumerate(((lo_half, cos), (hi_half, sin), (lo_half, sin), (hi_half, cos))):
                    pool.tensor_tensor(rope_t[:, j], half, ang, ALU.mult).then_inc(r_prod, 1)
                pool.wait_ge(r_prod, 4 * h + 4)
                if h >= 2:
                    pool.wait_ge(r_tr, h - 1)
                pool.tensor_tensor(rot[:, h % 2, :, :, 0:64], rope_t[:, 0], rope_t[:, 1], ALU.subtract).then_inc(r_rot, 1)
                pool.tensor_tensor(rot[:, h % 2, :, :, 64:P], rope_t[:, 2], rope_t[:, 3], ALU.add).then_inc(r_rot, 1)
                gate = ret[:, :, 3, c:c + P]
                pool.wait_ge(r_silu, h + 1)
                pool.tensor_tensor(ret_y[:, h % 2, 1, :, :], ret_y[:, h % 2, 0, :, :], gate, ALU.mult).then_inc(r_sg, 1)
                pool.wait_ge(r_sg, 2 * h + 1)
                pool.tensor_tensor(ret_y[:, h % 2, 1, :, :], ret_y[:, h % 2, 1, :, :], gate, ALU.add).then_inc(r_sg, 1)

            pool.wait_ge(r_lo, RET_HEADS)
            pool.dma_start(x1[:, :, :], x_d.rearrange("(t p) d -> p t d", p=P)).then_inc(x1_loaded, 16)
            pool.wait_ge(prod_free, P_OUT)
            pool.dma_start(memr[:, :, :], mem_d.rearrange("(t p) d -> p t d", p=P)).then_inc(mem_loaded, 16)
            pool.wait_ge(prod_free, P_UP)
            pool.dma_start(gfin[:, :], final_g_d[None, :].broadcast_to([P, D])).then_inc(gf_loaded, 16)

        @block.scalar
        def _(act):
            step = Steps(act, act_step)
            act.dma_start(vecs[:, :], vecs_d).then_inc(c_loaded, 16)
            act.dma_start(consts[:, :], consts_d).then_inc(c_loaded, 16)

            def hi_split(g, s, width=UW, first=False):
                act.wait_ge(raw_loaded[s], (g + 1) * 16)
                if not first:
                    act.wait_ge(unit_used, g * RING + (s + 1 - RING))
                act.activation(whi[:, s, 0:width], raw[:, s, 0:width], ACT.Copy).then_inc(hi_ready, 1)

            def stage(g0, body_groups, iters, evac=None, first=0, side=None, after=None):
                def body(i):
                    for u in range(RING * body_groups):
                        if evac:
                            evac(i, u)
                        if side:
                            side(i * RING * body_groups + u)
                        hi_split(i * body_groups + (g0 + 1 + u // RING), u % RING)
                    if after:
                        after(i)
                if side or iters - first == 1:
                    for i in range(first, iters):
                        body(i)
                else:
                    with act.Fori(first, iters) as i:
                        body(i)

            def squares(which, b, p0=None):
                for t in range(2):
                    if p0 is not None:
                        act.wait_ge(prod_free, b * 2 + (p0 + 1 + t))
                    src = NORM[which][0][:, t, b * 512:(b + 1) * 512]
                    if which or b or t:
                        act.wait_ge(n_sq, b * 2 + (8 * which + t))
                    act.activation(junk[:, :], src, ACT.Square, accum_out=ss[:, which, t, b:b + 1]).then_inc(n_sq, 1)

            def norm_hi(which, b):
                _, _, outT, g = NORM[which]
                act.wait_ge(n_tr, NB * which + b + 1)
                for k in (2 * b, 2 * b + 1):
                    ins = act.activation(outT[:, k, 0:T], bank[4 + b % 4][:, (k % 2) * T:(k % 2) * T + T],
                                         ACT.Copy, scale=vecs[:, g + k:g + k + 1])
                ins.then_inc(n_hi, 1)

            for b in range(4):
                act.wait_ge(x_loaded[b], 16)
                squares(0, b)
            for s in range(RING):
                hi_split(0, s, first=True)
            act.wait_ge(c_loaded, 32)
            for b in range(NB):
                norm_hi(0, b)
            act.wait_ge(lru_abs, 1)
            act.activation(sp[:, 1, :], sp[:, 0, :], ACT.Exp).then_inc(lru_z, 1)
            stage(0, 1, G_CH)
            stage(G0_VA, 1, 1)

            def lru_gates(n):
                tr, ti, a, th, y2 = (lru_t[:, n % 2, j, :] for j in (1, 2, 3, 4, 5))
                if n == 0:
                    act.wait_ge(lru_consts, 1)
                    act.wait_ge(prod_free, P_VA)
                if n >= 2:
                    act.wait_ge(l_done, n - 1)
                act.activation(y2, chT[:, BT + n, :], ACT.Square).then_inc(l_sig, 1)
                act.wait_ge(l_ps, n + 1)
                act.activation(tr, bank[4 + n % 2][:, 0:T], ACT.Tanh, scale=0.5, bias=sp[:, 6, n:n + 1])
                step.did(act.activation(ti, bank[4 + n % 2][:, T:2 * T], ACT.Tanh, scale=0.5, bias=sp[:, 7, n:n + 1]))
                step.wait()
                act.activation(a, tr, ACT.Exp, scale=sp[:, 4, n:n + 1], bias=sp[:, 4, n:n + 1])
                act.activation(th, tr, ACT.Tanh, scale=sp[:, 5, n:n + 1], bias=sp[:, 5, n:n + 1]).then_inc(l_sig, 1)

            def lru_root(n):
                th, tg, q = (lru_t[:, n % 2, j, :] for j in (4, 6, 7))
                act.wait_ge(l_q, n + 1)
                act.activation(tg, q, ACT.Tanh, scale=0.5).then_inc(l_gelu, 1)
                act.wait_ge(l_m, n + 1)
                act.activation(th, th, ACT.Sqrt).then_inc(l_root, 1)

            def swa_exp(n):
                tiles = SWA[n][4]
                w = 512 // tiles
                act.wait_ge(s_max, n + 1)
                if n >= 2:
                    act.wait_ge(s_tr, n - 1)
                for j in range(tiles):
                    act.activation(swa_p[:, n % 2, j * w:(j + 1) * w], swa_s[:, n % 2, j * w:(j + 1) * w],
                                   ACT.Exp, bias=stat[:, 1, 4 * n + j:4 * n + j + 1],
                                   accum_out=stat[:, 2, 4 * n + j:4 * n + j + 1])
                act.activation(stat[:, 4, 4 * n:4 * n + tiles], stat[:, 3, 4 * n:4 * n + tiles],
                               ACT.Exp).then_inc(s_exp, 1)

            def swa_copy(n):
                act.wait_ge(s_tr, n + 1)
                if n >= 2:
                    act.wait_ge(s_pv, n - 1)
                act.activation(swa_pT[:, n % 2, :], bank[5][:, :], ACT.Copy).then_inc(s_pT, 1)

            def swa_hi(big):
                act.wait_ge(s_pv, 6 * big + 6)
                for j in range(2):
                    act.activation(oaT[:, 4 * big + 2 * j:4 * big + 2 * j + 2, 0:T],
                                   bank[6 + j][:, :].rearrange("p (a b) -> p a b", a=2), ACT.Copy).then_inc(s_hi, 1)

            def swa_side(u):
                n = u // 4
                if u % 4 == 0 and 1 <= n <= len(SWA):
                    swa_copy(n - 1)
                if u % 4 == 2 and n < len(SWA):
                    swa_exp(n)
                if u in (25, 49):
                    swa_hi(u // 24 - 1)

            def ret_side(u):
                n = u // LRU_PERIOD
                if n < BT and u % LRU_PERIOD == 2:
                    lru_gates(n)
                if n < BT and u % LRU_PERIOD == 5:
                    lru_root(n)
                if u >= SWA_FROM:
                    swa_side(u - SWA_FROM)

            stage(G0_RET, 2, 8, side=ret_side)

            def gate_evac(b):
                def evac(i, u):
                    if u % 3 == 1:
                        n = u // 3
                        act.wait_ge(unit_used, i * 12 + (RING * (G0_BR + G_BR * b) + u + 1))
                        act.wait_ge(prod_free, i * 8 + (P_BR + 2 * KT * b + 2 * n - 2))
                        act.activation(br_t[:, n % 2, 0, :], bank[2 * n % 4][:, 0:T], ACT.Tanh, scale=0.5).then_inc(g_tanh, 1)
                return evac

            def retention_side(u):
                if u < 0:
                    return
                h, phase = u // RET_PERIOD, u % RET_PERIOD
                if h < RET_HEADS and phase == 0:
                    act.wait_ge(r_tr, h + 1)
                    if h >= 2:
                        act.wait_ge(r_sc, h - 1)
                    act.activation(qkT[:, h % 2, :], bank[4][:, :], ACT.Copy).then_inc(r_qkT, 1)
                    if h >= 2:
                        act.wait_ge(r_o, h - 1)
                    act.activation(ret_y[:, h % 2, 0, :, :], ret[:, :, 3, h * P:(h + 1) * P],
                                   ACT.Tanh, scale=0.5).then_inc(r_silu, 1)
                if 1 <= h <= RET_HEADS and phase == 1:
                    act.wait_ge(r_otr, h)
                    act.activation(obT[:, h - 1, 0:T], bank[7][:, 0:T], ACT.Copy, scale=0.5).then_inc(r_hi, 1)

            stage(G0_BR, 3, 4, gate_evac(0), side=lambda u: swa_side(u + 64 - SWA_FROM))
            stage(G0_BR + G_BR, 3, 4, gate_evac(1), side=lambda u: retention_side(u - RET_FROM))
            stage(G0_BR + 2 * G_BR, 3, 4, gate_evac(2))

            def mem_side(u):
                if u in (5, 6):
                    if u == 5:
                        act.wait_ge(mem_loaded, 16)
                    squares(1, 2 * (u - 5))
                    squares(1, 2 * (u - 5) + 1)
                if 11 <= u < 11 + NB:
                    norm_hi(1, u - 11)
            stage(G0_OUT, 2, 4, side=mem_side)

            def x1_side(u):
                if u < 4:
                    act.wait_ge(prod_free, P_K)
                    squares(2, u)
                if 8 <= u < 8 + NB:
                    norm_hi(2, u - 8)
            stage(G0_K, 1, 4, side=x1_side)
            stage(G0_K, 1, 8, first=4)
            stage(G0_Q, 1, 8)

            def x_exp_(h):
                act.wait_ge(x_max, h + 1)
                if h >= 2:
                    act.wait_ge(x_tr, h - 1)
                for t in range(2):
                    ins = act.activation(xp[:, h % 2, t * MEM:(t + 1) * MEM], bank[4][:, t * MEM:(t + 1) * MEM], ACT.Exp,
                                         scale=X_D ** -0.5, bias=stat[:, 1, 2 * h + t:2 * h + t + 1],
                                         accum_out=stat[:, 2, 2 * h + t:2 * h + t + 1])
                act.activation(stat[:, 4, 2 * h:2 * h + 2], stat[:, 1, 2 * h:2 * h + 2], ACT.Copy).then_inc(x_exp, 1)

            def x_hi_(h):
                for j in range(2):
                    act.wait_ge(x_pv, 2 * h + j + 1)
                    act.activation(xT[:, 4 * h + 2 * j:4 * h + 2 * j + 2, 0:T],
                                   bank[6 + j][:, :].rearrange("p (a b) -> p a b", a=2), ACT.Copy).then_inc(x_hi, 1)

            def x_side(u):
                h = u // 6
                if h < X_HEADS and u % 6 == 3:
                    x_exp_(h)
                if h < X_HEADS and u % 6 == 5:
                    act.wait_ge(x_tr, h + 1)
                    act.activation(xpT[:, h, :], bank[5][:, :], ACT.Copy).then_inc(x_pT, 1)
                if u in (11, 19, 27):
                    x_hi_(u // 8 - 1)
            stage(G0_V, 2, 4, side=x_side)
            stage(G0_O, 2, 4, side=lambda u: x_hi_(3) if u == 3 else None, after=lambda i: squares(3, i, P_O))
            for b in range(NB):
                norm_hi(3, b)

            def ffn_evac(i, u):
                if u == 2:
                    act.wait_ge(prod_free, i * 2 + (P_UP + 1))
                    act.activation(ffn_t[:, 1, :], ffn_t[:, 0, :], ACT.Tanh, scale=0.5).then_inc(f_tanh, 1)
            stage(G0_UP, 1, FT, ffn_evac)

            def down_splits(c, last):
                for u in range(len(DOWN_K)):
                    nxt = (u + RING) % len(DOWN_K)
                    if not (last and u + RING >= len(DOWN_K)):
                        hi_split(c * G_DOWN + (G0_DOWN + 1 + u // RING), u % RING, down_width(nxt))
                squares(4, c, P_DOWN)
            for c in range(DOWN_BLOCKS):
                down_splits(c, c == DOWN_BLOCKS - 1)

        @block.vector
        def _(dve):
            step = Steps(dve, dve_step)

            def lo_split(g, s, width=UW):
                dve.wait_ge(hi_ready, g * RING + (s + 1))
                dve.tensor_tensor(wlo[:, s, 0:width], raw[:, s, 0:width], whi[:, s, 0:width].bitcast(f32),
                                  ALU.subtract).then_inc(lo_ready, 1)

            def stage(g0, body_groups, iters, evac=None, steps=0, first=0, side=None):
                def body(i):
                    for u in range(RING * body_groups):
                        if evac:
                            evac(i, u)
                        if side:
                            side(i * RING * body_groups + u)
                        lo_split(i * body_groups + (g0 + 1 + u // RING), u % RING)
                if side or iters - first == 1:
                    for i in range(first, iters):
                        body(i)
                else:
                    with dve.Fori(first, iters) as i:
                        step.enter(i, steps, first)
                        body(i)
                        step.leave(iters)

            def rsqrt(y, x, t):
                step.wait()
                step.did(dve.tensor_scalar(t.bitcast(i32), x.bitcast(i32), 1, None, ALU.logical_shift_right))
                step.wait()
                step.did(dve.tensor_scalar(y.bitcast(i32), t.bitcast(i32), -1, RSQRT_SEED, ALU.mult, ALU.add))
                for _ in range(3):
                    step.wait()
                    step.did(dve.tensor_tensor(t, y, y, ALU.mult))
                    step.wait()
                    step.did(dve.scalar_tensor_tensor(t, t, -0.5, x, ALU.mult, ALU.mult))
                    step.wait()
                    step.did(dve.scalar_tensor_tensor(y, t, 1.5, y, ALU.add, ALU.mult))
                step.wait()

            def norm_rstd(which):
                dve.wait_ge(n_sq, 8 * (which + 1))
                step.did(dve.reduce_sum(ms[:, 0, :], ss[:, which, :, :], AX.X))
                step.wait()
                step.did(dve.tensor_scalar(ms[:, 0, :], ms[:, 0, :], 1.0 / D, EPS, ALU.mult, ALU.add))
                rsqrt(rstd[:, 2 * which:2 * which + 2], ms[:, 0, :], ms[:, 1, :])

            def norm_scale(which, b):
                src, dst, _, _ = NORM[which]
                for t in range(2):
                    ins = dve.tensor_scalar(dst[:, t, b * 512:(b + 1) * 512], src[:, t, b * 512:(b + 1) * 512],
                                            rstd[:, 2 * which + t:2 * which + t + 1], None, ALU.mult)
                ins.then_inc(n_xn, 1)

            def norm_lo(which, b):
                _, _, outT, g = NORM[which]
                dve.wait_ge(n_hi, NB * which + b + 1)
                for k in (2 * b, 2 * b + 1):
                    ins = dve.scalar_tensor_tensor(outT[:, k, T:2 * T], bank[4 + b % 4][:, (k % 2) * T:(k % 2) * T + T],
                                                   vecs[:, g + k:g + k + 1], outT[:, k, 0:T].bitcast(f32),
                                                   ALU.mult, ALU.subtract)
                ins.then_inc(n_lo, 1)

            def norm_alone(which):
                norm_rstd(which)
                norm_scale(which, 0)
                norm_scale(which, 1)
                for b in range(NB):
                    norm_lo(which, b)
                    if b in (0, 2):
                        norm_scale(which, 2 + b // 2)

            def copy_channels(g0, dest):
                def evac(i, u):
                    if u % 2 == 1:
                        dve.wait_ge(unit_used, i * 4 + (RING * g0 + u + 1))
                        out = dest(i, u // 2)
                        dve.tensor_copy(out, bank[u // 2][:, 0:T]).then_inc(prod_free, 1)
                return evac

            def wait_half(t, i, units, g0, b0):
                if t == 0:
                    dve.wait_ge(half0_done, i + (b0 + 1))
                else:
                    dve.wait_ge(unit_used, i * units + (RING * g0 + units))

            def copy_tokens(g0, b0, units, dest, width=512, pair=0):
                def evac(i, u):
                    if u == units - 1:
                        for t in range(2):
                            wait_half(t, i, units, g0, b0)
                            dve.tensor_copy(dest(i, t), bank[(2 * i + pair) % 4 + t][:, 0:width]).then_inc(prod_free, 1)
                return evac

            dve.wait_ge(c_loaded, 32)
            lam = vecs[:, V_LAM:V_LAM + BT]
            s0, s1, s2, s3 = (sp[:, j, :] for j in range(4))
            dve.tensor_scalar(sp[:, 6, :], vecs[:, V_BA:V_BA + BT], 0.5, None, ALU.mult)
            dve.tensor_scalar(sp[:, 7, :], vecs[:, V_BX:V_BX + BT], 0.5, None, ALU.mult)
            step.did(dve.tensor_scalar(s1, lam, -1.0, None, ALU.mult))
            step.wait()
            step.did(dve.tensor_tensor(s0, lam, s1, ALU.max))
            step.wait()
            dve.tensor_scalar(s0, s0, -1.0, None, ALU.mult).then_inc(lru_abs, 1)
            norm_rstd(0)
            norm_scale(0, 0)
            norm_scale(0, 1)
            for s in range(RING):
                lo_split(0, s)
            norm_scale(0, 2)
            norm_scale(0, 3)
            for b in range(NB):
                norm_lo(0, b)
            def to_chT(i, j):
                return chT[:, bass.ds(i * 2 + j, 1), :].rearrange("p a b -> p (a b)")
            stage(0, 1, G_CH - 1, copy_channels(0, to_chT))

            dve.wait_ge(lru_z, 1)
            step.did(dve.tensor_scalar(s2, s1, 2.0, None, ALU.add))
            step.wait()
            step.did(dve.reciprocal(s2, s2))
            step.wait()
            step.did(dve.tensor_tensor(s1, s1, s2, ALU.mult))
            step.wait()
            step.did(dve.tensor_tensor(s2, s1, s1, ALU.mult))
            step.wait()
            step.did(dve.tensor_scalar(s3, s2, 2.0 / 19, 2.0 / 17, ALU.mult, ALU.add))
            for odd in (15, 13, 11, 9, 7, 5, 3, 1):
                step.wait()
                step.did(dve.tensor_tensor(s3, s3, s2, ALU.mult))
                step.wait()
                step.did(dve.tensor_scalar(s3, s3, 2.0 / odd, None, ALU.add))
            step.wait()
            step.did(dve.tensor_tensor(s3, s3, s1, ALU.mult))
            step.did(dve.tensor_scalar(s0, lam, -1.0, 0.0, ALU.mult, ALU.max))
            step.wait()
            step.did(dve.tensor_tensor(s3, s3, s0, ALU.add))
            step.wait()
            dve.tensor_scalar(sp[:, 5, :], s3, 4.0, None, ALU.mult)
            dve.tensor_scalar(sp[:, 4, :], s3, -4.0, None, ALU.mult).then_inc(lru_consts, 1)

            stage(0, 1, G_CH, copy_channels(0, to_chT), first=G_CH - 1)
            stage(G0_VA, 1, 1, copy_tokens(G0_VA, B_VA, 4, lambda i, t: va[:, t, :], T, 2))

            def lru_conv(n):
                xc, xin = lru_t[:, n % 2, 0, :], chT[:, n, :]
                w = [vecs[:, V_CW + BT * j + n:V_CW + BT * j + n + 1] for j in range(4)]
                if n >= 2:
                    dve.wait_ge(l_ps, n - 1)
                step.did(dve.tensor_scalar(xc, xin, w[3], vecs[:, V_CB + n:V_CB + n + 1], ALU.mult, ALU.add))
                for d in (1, 2, 3):
                    step.wait()
                    ins = dve.scalar_tensor_tensor(xc[:, d:], xin[:, :T - d], w[3 - d], xc[:, d:], ALU.mult, ALU.add)
                    if d < 3:
                        step.did(ins)
                ins.then_inc(l_xc, 1)

            def lru_input(n):
                xc, tr, ti, a, th, y2, tg, q = (lru_t[:, n % 2, j, :] for j in range(8))
                dve.wait_ge(l_sig, 2 * n + 1)
                step.did(dve.tensor_scalar(q, y2, GELU_3, GELU_1, ALU.mult, ALU.add))
                step.wait()
                dve.tensor_tensor(q, q, chT[:, BT + n, :], ALU.mult).then_inc(l_q, 1)
                dve.wait_ge(l_sig, 2 * n + 2)
                step.did(dve.tensor_tensor(y2, a, a, ALU.mult))
                step.did(dve.scalar_tensor_tensor(ti, ti, 1.0, xc, ALU.add, ALU.mult))
                step.wait()
                step.did(dve.scalar_tensor_tensor(th, y2, 1.0, th, ALU.add, ALU.mult))
                step.wait()
                dve.tensor_scalar(th, th, 0.0, None, ALU.max).then_inc(l_m, 1)

            def lru_scan(n):
                xc, tr, ti, a, th, y2, tg, q = (lru_t[:, n % 2, j, :] for j in range(8))
                dve.wait_ge(l_root, n + 1)
                step.did(dve.scalar_tensor_tensor(th, th, 0.5, ti, ALU.mult, ALU.mult))
                step.wait()
                step.did(dve.tensor_tensor_scan(y2, a, th, 0.0, ALU.mult, ALU.add))
                dve.wait_ge(l_gelu, n + 1)
                step.did(dve.scalar_tensor_tensor(tg, tg, 1.0, chT[:, BT + n, :], ALU.add, ALU.mult))
                step.wait()
                step.did(dve.scalar_tensor_tensor(q, tg, 0.5, y2, ALU.mult, ALU.mult))
                step.wait()
                step.did(dve.tensor_copy(ocT[:, n, 0:T], q))
                step.wait()
                dve.tensor_tensor(ocT[:, n, T:2 * T], q, ocT[:, n, 0:T].bitcast(f32), ALU.subtract).then_inc(l_done, 1)

            def swa_mask(n):
                big, half, blk, tile0, tiles = SWA[n]
                w = 512 // tiles
                head = 8 * big + 4 * half + tile0 % 4
                cols = slice(4 * n, 4 * n + tiles)
                scores = swa_s[:, n % 2, :].rearrange("p (a b) -> p a b", a=tiles)
                mask = consts[:, C_DIAG + P - w:C_DIAG + P].unsqueeze(1).broadcast_to([P, tiles, w])
                if n == 0:
                    dve.wait_ge(sinks_loaded, 16)
                dve.wait_ge(s_sc, n + 1)
                if n >= 2:
                    dve.wait_ge(s_exp, n - 1)
                step.did(dve.scalar_tensor_tensor(scores, bank[4][:, :].rearrange("p (a b) -> p a b", a=tiles),
                                                  SWA_D ** -0.5, mask, ALU.mult, ALU.add))
                step.wait()
                step.did(dve.reduce_max(stat[:, 0, cols], scores, AX.X))
                step.wait()
                step.did(dve.tensor_tensor(stat[:, 0, cols], stat[:, 0, cols], sinks[:, head:head + tiles], ALU.max))
                step.wait()
                dve.tensor_scalar(stat[:, 1, cols], stat[:, 0, cols], -1.0, None, ALU.mult)
                dve.tensor_tensor(stat[:, 3, cols], sinks[:, head:head + tiles], stat[:, 0, cols],
                                  ALU.subtract).then_inc(s_max, 1)

            def swa_normalise(n):
                tiles = SWA[n][4]
                cols = slice(4 * n, 4 * n + tiles)
                dve.wait_ge(s_exp, n + 1)
                step.did(dve.tensor_tensor(stat[:, 5, cols], stat[:, 2, cols], stat[:, 4, cols], ALU.add))
                step.wait()
                step.did(dve.reciprocal(stat[:, 5, cols], stat[:, 5, cols]))
                step.wait()
                probs = swa_p[:, n % 2, :].rearrange("p (a b) -> p a b", a=tiles)
                dve.tensor_tensor(probs, probs, stat[:, 5, cols].unsqueeze(2).broadcast_to([P, tiles, 512 // tiles]),
                                  ALU.mult).then_inc(s_p, 1)

            def swa_lo(big):
                for j in range(2):
                    dve.wait_ge(s_hi, 2 * big + j + 1)
                    tl = slice(4 * big + 2 * j, 4 * big + 2 * j + 2)
                    dve.tensor_tensor(oaT[:, tl, T:2 * T], bank[6 + j][:, :].rearrange("p (a b) -> p a b", a=2),
                                      oaT[:, tl, 0:T].bitcast(f32), ALU.subtract).then_inc(s_lo, 1)

            def swa_side(u):
                n = u // 4
                if n < len(SWA) and u % 4 == 0:
                    swa_mask(n)
                if n < len(SWA) and u % 4 == 2:
                    swa_normalise(n)
                if u in (26, 50):
                    swa_lo(u // 24 - 1)

            def ret_side(u):
                n = u // LRU_PERIOD
                if n < BT and u % LRU_PERIOD == 0:
                    lru_conv(n)
                if n < BT and u % LRU_PERIOD == 3:
                    lru_input(n)
                if n < BT and u % LRU_PERIOD == 6:
                    lru_scan(n)
                if u >= SWA_FROM:
                    swa_side(u - SWA_FROM)

            def ret_evac(i, u):
                if u == 7:
                    for t in range(2):
                        wait_half(t, i, 8, G0_RET, B_RET)
                        dve.tensor_copy(ret[:, t, i // 2, (i % 2) * 512:(i % 2) * 512 + 512],
                                        bank[2 * (i % 2) + t][:, :]).then_inc(prod_free, 1)
            stage(G0_RET, 2, 8, ret_evac, side=ret_side)

            def ret_stats(h):
                dve.wait_ge(r_y, h + 1)
                for t in range(2):
                    step.did(dve.bn_stats(ret_st[:, t, 0:6], bank[6][:, t * P:(t + 1) * P]))
                step.wait()
                for t in range(2):
                    step.did(dve.bn_aggr(ret_st[:, t, 6:8], ret_st[:, t, 0:6]))
                step.wait()
                var, root, place = ret_nw[:, 0, :], ret_nw[:, 1, :], ret_nw[:, 2, :]
                step.did(dve.tensor_scalar(var, ret_st[:, :, 7], EPS, None, ALU.add))
                rsqrt(root, var, place)
                if h >= 2:
                    dve.wait_ge(r_o, h - 1)
                for t in range(2):
                    step.did(dve.tensor_scalar(ret_y[:, h % 2, 2, t, :], bank[6][:, t * P:(t + 1) * P],
                                               ret_st[:, t, 6:7], ret_nw[:, 1, t:t + 1], ALU.subtract, ALU.mult))
                step.wait()
                dve.wait_ge(r_sg, 2 * h + 2)
                if h >= 2:
                    dve.wait_ge(r_otr, h - 1)
                dve.tensor_tensor(ret_y[:, h % 2, 3, :, :], ret_y[:, h % 2, 2, :, :], ret_y[:, h % 2, 1, :, :],
                                  ALU.mult).then_inc(r_o, 1)

            def retention_side(u):
                if u < 0:
                    return
                h, phase = u // RET_PERIOD, u % RET_PERIOD
                if 1 <= h <= RET_HEADS and phase == 1:
                    dve.wait_ge(r_hi, h)
                    dve.scalar_tensor_tensor(obT[:, h - 1, T:2 * T], bank[7][:, 0:T], 0.5,
                                             obT[:, h - 1, 0:T].bitcast(f32), ALU.mult, ALU.subtract).then_inc(r_lo, 1)
                if h < RET_HEADS and phase == 1:
                    if h == 0:
                        dve.wait_ge(dec_loaded, 16)
                    dve.wait_ge(r_sc, h + 1)
                    if h >= 2:
                        dve.wait_ge(r_y, h - 1)
                    dve.tensor_tensor(sT[:, h % 2, :], bank[5][:, 0:NDEC], decay[:, h, :], ALU.mult).then_inc(r_sT, 1)
                if h < RET_HEADS and phase == 3:
                    ret_stats(h)

            def merge_evac(b):
                def evac(i, u):
                    if u % 3 != 2:
                        return
                    n = u // 3
                    tile = bass.ds(i * 4 + n, 1)
                    tanh, term, total = (br_t[:, n % 2, j, :] for j in range(3))
                    mrg = merged[:, tile, :].rearrange("p a b -> p (a b)")
                    dve.wait_ge(g_tanh, i * 4 + (KT * b + n + 1))
                    dve.wait_ge(unit_used, i * 12 + (RING * (G0_BR + G_BR * b) + u + 1))
                    src = bank[(2 * n + 1) % 4][:, 0:T]
                    if b == 0:
                        dve.scalar_tensor_tensor(mrg, tanh, 1.0, src, ALU.add, ALU.mult).then_inc(prod_free, 2)
                        return
                    step.did(dve.scalar_tensor_tensor(term, tanh, 1.0, src, ALU.add, ALU.mult))
                    step.wait()
                    if b == 1:
                        dve.tensor_tensor(mrg, mrg, term, ALU.add).then_inc(prod_free, 2)
                        return
                    step.did(dve.tensor_tensor(total, mrg, term, ALU.add))
                    step.wait()
                    hi = mT[:, tile, 0:T].rearrange("p a b -> p (a b)")
                    lo = mT[:, tile, T:2 * T].rearrange("p a b -> p (a b)")
                    step.did(dve.tensor_scalar(hi, total, 0.5, None, ALU.mult))
                    step.wait()
                    dve.scalar_tensor_tensor(lo, total, 0.5, hi.bitcast(f32), ALU.mult, ALU.subtract).then_inc(prod_free, 2)
                return evac
            stage(G0_BR, 3, 4, merge_evac(0), side=lambda u: swa_side(u + 64 - SWA_FROM))
            stage(G0_BR + G_BR, 3, 4, merge_evac(1), side=lambda u: retention_side(u - RET_FROM))
            stage(G0_BR + 2 * G_BR, 3, 4, merge_evac(2), 12)

            def add_tokens(g0, b0):
                def evac(i, u):
                    if u == 7:
                        for t in range(2):
                            wait_half(t, i, 8, g0, b0)
                            dst = x1[:, t, i * 512:(i + 1) * 512]
                            dve.tensor_tensor(dst, dst, bank[2 * (i % 2) + t][:, :], ALU.add).then_inc(prod_free, 1)
                return evac

            dve.wait_ge(x1_loaded, 16)

            def mem_side(u):
                if u == 8:
                    norm_rstd(1)
                if 9 <= u < 13:
                    norm_scale(1, u - 9)
                if 12 <= u < 12 + NB:
                    norm_lo(1, u - 12)
            stage(G0_OUT, 2, 4, add_tokens(G0_OUT, B_OUT), side=mem_side)

            def x1_side(u):
                if u == 4:
                    norm_rstd(2)
                if 5 <= u < 9:
                    norm_scale(2, u - 5)
                if 9 <= u < 16:
                    norm_lo(2, u - 9)
                if u == 15:
                    norm_lo(2, 7)

            def to_kT(i, j):
                return kT[:, bass.ds(i * 2 + j, 1), :].rearrange("p a b -> p (a b)")
            stage(G0_K, 1, 4, copy_channels(G0_K, to_kT), side=x1_side)
            stage(G0_K, 1, 8, copy_channels(G0_K, to_kT), first=4)
            stage(G0_Q, 1, 8, copy_channels(G0_Q, lambda i, j: (
                qT[:, bass.ds(i * 2 + j, 1), :].rearrange("p a b -> p (a b)"))))

            def x_lo_(h):
                for j in range(2):
                    dve.wait_ge(x_hi, 2 * h + j + 1)
                    tl = slice(4 * h + 2 * j, 4 * h + 2 * j + 2)
                    dve.tensor_tensor(xT[:, tl, T:2 * T], bank[6 + j][:, :].rearrange("p (a b) -> p a b", a=2),
                                      xT[:, tl, 0:T].bitcast(f32), ALU.subtract).then_inc(x_lo, 1)

            def x_side(u):
                h = u // 6
                cols = slice(2 * h, 2 * h + 2)
                if h < X_HEADS and u % 6 == 1:
                    dve.wait_ge(x_sc, h + 1)
                    step.did(dve.reduce_max(stat[:, 0, cols], bank[4][:, :].rearrange("p (a b) -> p a b", a=2), AX.X))
                    step.wait()
                    dve.tensor_scalar(stat[:, 1, cols], stat[:, 0, cols], -(X_D ** -0.5), None,
                                      ALU.mult).then_inc(x_max, 1)
                if h < X_HEADS and u % 6 == 4:
                    dve.wait_ge(x_exp, h + 1)
                    step.did(dve.reciprocal(stat[:, 3, cols], stat[:, 2, cols]))
                    step.wait()
                    for t in range(2):
                        part = xp[:, h % 2, t * MEM:(t + 1) * MEM]
                        ins = dve.tensor_scalar(part, part, stat[:, 3, 2 * h + t:2 * h + t + 1], None, ALU.mult)
                    ins.then_inc(x_p, 1)
                if u in (12, 20, 28):
                    x_lo_(u // 8 - 1)
            stage(G0_V, 2, 4, copy_tokens(G0_V, B_V, 8, lambda i, t: v[:, t, i * 512:(i + 1) * 512]),
                  side=x_side)
            stage(G0_O, 2, 4, add_tokens(G0_O, B_O), side=lambda u: x_lo_(3) if u == 4 else None)
            norm_alone(3)

            def ffn_evac(i, u):
                conv, tanh, gated, full = (ffn_t[:, j, :] for j in range(4))
                if u == 1:
                    dve.wait_ge(unit_used, i * 4 + (RING * G0_UP + 2))
                    w = [vecs[:, bass.ds(i + (V_FW + FT * j), 1)] for j in range(3)]
                    step.did(dve.tensor_scalar(conv, bank[0][:, 0:T], w[2], vecs[:, bass.ds(i + V_FB, 1)],
                                               ALU.mult, ALU.add))
                    step.wait()
                    step.did(dve.scalar_tensor_tensor(conv[:, 1:], bank[0][:, 0:T - 1], w[1], conv[:, 1:],
                                                      ALU.mult, ALU.add))
                    step.wait()
                    dve.scalar_tensor_tensor(conv[:, 2:], bank[0][:, 0:T - 2], w[0], conv[:, 2:],
                                             ALU.mult, ALU.add).then_inc(prod_free, 1)
                if u == 3:
                    dve.wait_ge(f_tanh, i + 1)
                    step.did(dve.scalar_tensor_tensor(gated, tanh, 1.0, conv, ALU.add, ALU.mult))
                    step.wait()
                    dve.wait_ge(unit_used, i * 4 + (RING * G0_UP + 4))
                    dve.scalar_tensor_tensor(full, gated, 0.5, bank[1][:, 0:T], ALU.mult, ALU.mult).then_inc(prod_free, 1)
                    dve.wait_ge(prod_free, i * 2 + (P_UP + 2))
                    hi = actT[:, bass.ds(i, 1), 0:T].rearrange("p a b -> p (a b)")
                    lo = actT[:, bass.ds(i, 1), T:2 * T].rearrange("p a b -> p (a b)")
                    step.did(dve.tensor_copy(hi, full))
                    step.wait()
                    step.did(dve.tensor_tensor(lo, full, hi.bitcast(f32), ALU.subtract))
            stage(G0_UP, 1, FT, ffn_evac, 5)
            step.wait()
            dve.tensor_copy(stat[:, 0, 0:1], stat[:, 0, 0:1]).then_inc(act_whole, 1)

            def down(c, last):
                for u in range(len(DOWN_K)):
                    if u == len(DOWN_K) - 1:
                        for t in range(2):
                            wait_half(t, c, len(DOWN_K), G0_DOWN, B_DOWN)
                            dst = x1[:, t, c * 512:(c + 1) * 512]
                            dve.tensor_tensor(dst, dst, bank[2 * (c % 2) + t][:, :], ALU.add).then_inc(prod_free, 1)
                    nxt = (u + RING) % len(DOWN_K)
                    if not (last and u + RING >= len(DOWN_K)):
                        lo_split(c * G_DOWN + (G0_DOWN + 1 + u // RING), u % RING, down_width(nxt))
            for c in range(DOWN_BLOCKS):
                down(c, c == DOWN_BLOCKS - 1)

            norm_rstd(4)
            dve.wait_ge(gf_loaded, 16)
            for t in range(2):
                dve.scalar_tensor_tensor(x1[:, t, :], x1[:, t, :], rstd[:, 8 + t:9 + t], gfin[:, :],
                                         ALU.mult, ALU.mult).then_inc(out_ready, 1)

        @block.tensor
        def _(pe):
            def passes(out, w_stationary, hi_w, lo_w, hi_x, lo_x, start, stop):
                pairs = ((hi_w, hi_x), (hi_w, lo_x), (lo_w, hi_x)) if w_stationary else \
                        ((hi_x, hi_w), (hi_x, lo_w), (lo_x, hi_w))
                for n, (st, mv) in enumerate(pairs):
                    ins = pe.matmul(out, st, mv, start=start and n == 0, stop=stop and n == 2)
                return ins

            def channel_unit(g, s, X, k0, out, first, last):
                pe.wait_ge(lo_ready, g * RING + (s + 1))
                for b in range(UT):
                    c = slice(b * P, (b + 1) * P)
                    ins = passes(out[:, 0:T], True, whi[:, s, c], wlo[:, s, c], X[:, k0 + b, 0:T], X[:, k0 + b, T:2 * T],
                                 first and b == 0, last and b == UT - 1)
                ins.then_inc(unit_used, 1)

            def token_unit(g, s, X, k0, nk, width, first, last, pair):
                pe.wait_ge(lo_ready, g * RING + (s + 1))
                for t in range(2):
                    for b in range(nk):
                        c = slice(b * width, (b + 1) * width)
                        k = k0 + b
                        ins = passes(bank[pair + t][:, 0:width], False, whi[:, s, c], wlo[:, s, c],
                                     X[:, k, t * P:(t + 1) * P], X[:, k, T + t * P:T + (t + 1) * P],
                                     first and b == 0, last and b == nk - 1)
                    if last and t == 0:
                        ins.then_inc(half0_done, 1)
                    if first and t == 0:
                        yield
                ins.then_inc(unit_used, 1)

            def channel_stage(g0, p0, pairs, X, first=0, before=None):
                def body(i):
                    for j in range(2):
                        pe.wait_ge(prod_free, i * 2 + (p0 + j - 1))
                        for u in range(2):
                            if before:
                                before(4 * i + 2 * j + u)
                            channel_unit(i + g0, 2 * j + u, X, UT * u, bank[j], u == 0, u == 1)
                if before:
                    for i in range(first, pairs):
                        body(i)
                else:
                    with pe.Fori(first, pairs) as i:
                        body(i)

            def token_block(g, p, X, ks, width, pair=0, before=None):
                k0 = 0
                pe.wait_ge(prod_free, p - 3)
                for u, nk in enumerate(ks):
                    if before:
                        before(u)
                    for _ in token_unit(g + u // RING, u % RING, X, k0, nk, width, u == 0, u == len(ks) - 1,
                                        pair):
                        pe.wait_ge(prod_free, p - 2)
                    k0 += nk

            def token_stage(g0, p0, blocks, X, ks=(2,) * 8, width=512, first=0, before=None):
                if p0 != P_RET:
                    pe.wait_ge(prod_free, p0 + 2 * first)
                if before:
                    for i in range(first, blocks):
                        token_block(i * (len(ks) // RING) + g0, i * 2 + p0, X, ks, width, 2 * (i % 2),
                                    lambda u, i=i: before(i * len(ks) + u))
                else:
                    with pe.Fori(first // 2, blocks // 2) as i:
                        for j in range(2):
                            token_block(i * (len(ks) // RING * 2) + (g0 + j * (len(ks) // RING)), i * 4 + (p0 + 2 * j),
                                        X, ks, width, 2 * j)

            def norm_transpose(which, b):
                _, xn_, _, _ = NORM[which]
                pe.wait_ge(n_xn, 4 * which + b // 2 + 1)
                if NB * which + b >= 4:
                    pe.wait_ge(n_lo, NB * which + b - 3)
                for k in (2 * b, 2 * b + 1):
                    for t in range(2):
                        c = (k % 2) * T + t * P
                        ins = pe.transpose(bank[4 + b % 4][:, c:c + P], xn_[:, t, k * P:(k + 1) * P], ident)
                ins.then_inc(n_tr, 1)

            pe.wait_ge(c_loaded, 32)
            for b in range(NB):
                norm_transpose(0, b)
            for j in range(2):
                for u in range(2):
                    if j == 0:
                        pe.wait_ge(n_lo, NB // 2 * (u + 1))
                    channel_unit(0, 2 * j + u, xT, UT * u, bank[j], u == 0, u == 1)
            with pe.Fori(1, P_VA // 2) as i:
                for j in range(2):
                    pe.wait_ge(prod_free, i * 2 + (j - 1))
                    for u in range(2):
                        channel_unit(i, 2 * j + u, xT, UT * u, bank[j], u == 0, u == 1)
            token_block(G0_VA, P_VA, xT, (4,) * 4, SWA_KV * SWA_D, 2)

            def lru_product(n):
                if n == 0:
                    pe.wait_ge(lruw_loaded, 16)
                pe.wait_ge(l_xc, n + 1)
                if n >= 2:
                    pe.wait_ge(l_sig, 2 * (n - 1))
                for j in range(2):
                    ins = pe.matmul(bank[4 + n % 2][:, j * T:(j + 1) * T], lru_w[:, j, n, :], lru_t[:, n % 2, 0, :],
                                    start=True, stop=True)
                ins.then_inc(l_ps, 1)

            def swa_scores(n):
                big, half, blk, tile0, tiles = SWA[n]
                w = 512 // tiles
                rows = slice(64 * half, 64 * half + 64)
                if n == 0:
                    pe.wait_ge(l_sig, 2 * BT)
                else:
                    pe.wait_ge(s_max, n)
                for j in range(tiles):
                    ins = pe.matmul(bank[4][:, j * w:(j + 1) * w], chT[rows, 16 + tile0 + j, blk * P:blk * P + P],
                                    chT[rows, 24 + big, 0:w], start=True, stop=True)
                ins.then_inc(s_sc, 1)

            def swa_transpose(n):
                pe.wait_ge(s_p, n + 1)
                if n >= 1:
                    pe.wait_ge(s_pT, n)
                for j in range(4):
                    ins = pe.transpose(bank[5][:, j * P:(j + 1) * P], swa_p[:, n % 2, j * P:(j + 1) * P], ident)
                ins.then_inc(s_tr, 1)

            def swa_values(n):
                big, half, blk, tile0, tiles = SWA[n]
                pe.wait_ge(s_pT, n + 1)
                if n == 6:
                    pe.wait_ge(s_lo, 2)
                kv = 2 * big + half
                for j in range(tiles):
                    local = (tile0 + j) % 4
                    c = (local % 2) * T + blk * P
                    out = bank[6 + local // 2][64 * half:64 * half + 64, c:c + P]
                    nb = 4 // tiles
                    for kb in range(nb):
                        at_ = (j * nb + kb) * P
                        ins = pe.matmul(out, va[:, kb, kv * 64:(kv + 1) * 64], swa_pT[:, n % 2, at_:at_ + P],
                                        start=kb == 0, stop=kb == nb - 1)
                ins.then_inc(s_pv, 1)

            def swa_side(u):
                n = u // 4
                if u % 4 == 0 and 1 <= n <= len(SWA):
                    swa_transpose(n - 1)
                if u % 4 == 0 and n < len(SWA):
                    swa_scores(n)
                if u % 4 == 1 and 1 <= n <= len(SWA):
                    swa_values(n - 1)

            def ret_side(u):
                n = u // LRU_PERIOD
                if n < BT and u % LRU_PERIOD == 2:
                    lru_product(n)
                if u >= SWA_FROM:
                    swa_side(u - SWA_FROM)
            token_stage(G0_RET, P_RET, 8, xT, before=ret_side)

            def retention_side(u):
                if u < 0:
                    return
                h, phase = u // RET_PERIOD, u % RET_PERIOD
                if 1 <= h <= RET_HEADS and phase == 1:
                    pe.wait_ge(r_o, h)
                    if h >= 2:
                        pe.wait_ge(r_lo, h - 1)
                    for t in range(2):
                        ins = pe.transpose(bank[7][:, t * P:(t + 1) * P], ret_y[:, (h - 1) % 2, 3, t, :], ident)
                    ins.then_inc(r_otr, 1)
                if h >= RET_HEADS:
                    return
                if phase == 0:
                    pe.wait_ge(r_rot, 2 * h + 2)
                    if h >= 1:
                        pe.wait_ge(r_qkT, h)
                    for qk in range(2):
                        for t in range(2):
                            c = qk * T + t * P
                            ins = pe.transpose(bank[4][:, c:c + P], rot[:, h % 2, qk, t, :], ident)
                    ins.then_inc(r_tr, 1)
                if phase == 1:
                    pe.wait_ge(r_qkT, h + 1)
                    if h >= 1:
                        pe.wait_ge(r_sT, h)
                    q_, k_ = qkT[:, h % 2, 0:T], qkT[:, h % 2, T:2 * T]
                    pe.matmul(bank[5][:, 0:T], k_[:, 0:P], q_, start=True, stop=True)
                    pe.matmul(bank[5][:, T:T + P], k_[:, P:T], q_[:, P:T], start=True, stop=True).then_inc(r_sc, 1)
                if phase == 3:
                    pe.wait_ge(r_sT, h + 1)
                    if h >= 1:
                        pe.wait_ge(r_o, h)
                    v_ = ret[:, :, 2, h * P:(h + 1) * P]
                    pe.matmul(bank[6][:, 0:P], sT[:, h % 2, 0:P], v_[:, 0, :], start=True, stop=True)
                    pe.matmul(bank[6][:, P:T], sT[:, h % 2, P:T], v_[:, 0, :], start=True, stop=False)
                    pe.matmul(bank[6][:, P:T], sT[:, h % 2, T:T + P], v_[:, 1, :], start=False, stop=True).then_inc(r_y, 1)

            def branch_body(b, i, oT, before=None):
                for n in range(4):
                    p = i * 8 + (P_BR + 2 * KT * b + 2 * n)
                    g = i * 3 + (G0_BR + G_BR * b)
                    pe.wait_ge(prod_free, p - 2)
                    for j in range(3):
                        u = 3 * n + j
                        if before:
                            before(12 * i + u)
                        if j < 2:
                            channel_unit(g + u // RING, u % RING, xT, UT * j, bank[2 * n % 4], j == 0, j == 1)
                        else:
                            if before and i == 0 and n == 0:
                                pe.wait_ge(*((l_done, BT), (s_lo, 4))[b])
                            channel_unit(g + u // RING, u % RING, oT, 0, bank[(2 * n + 1) % 4], True, True)

            pe.wait_ge(prod_free, P_BR)
            for i in range(4):
                branch_body(0, i, ocT, lambda u: swa_side(u + 64 - SWA_FROM))
            for i in range(4):
                branch_body(1, i, oaT, lambda u: retention_side(u - RET_FROM))
            pe.wait_ge(r_lo, RET_HEADS)
            with pe.Fori(0, 4) as i:
                branch_body(2, i, obT)

            pe.wait_ge(prod_free, P_OUT)
            token_stage(G0_OUT, P_OUT, 4, mT, before=lambda u: norm_transpose(1, u - 11) if 11 <= u < 11 + NB else None)
            pe.wait_ge(n_lo, 2 * NB)
            channel_stage(G0_K, P_K, 4, memT, before=lambda u: norm_transpose(2, u - 8) if 8 <= u < 8 + NB else None)
            channel_stage(G0_K, P_K, 8, memT, first=4)
            pe.wait_ge(n_lo, 3 * NB)
            channel_stage(G0_Q, P_Q, 8, xT)

            def x_scores(h):
                if h == 0:
                    pe.wait_ge(prod_free, P_V)
                else:
                    pe.wait_ge(x_exp, h)
                for t in range(2):
                    for j in range(4):
                        ins = pe.matmul(bank[4][:, t * MEM:(t + 1) * MEM], qT[:, 4 * h + j, t * P:(t + 1) * P],
                                        kT[:, 4 * h + j, :], start=j == 0, stop=j == 3)
                ins.then_inc(x_sc, 1)

            def x_transpose(h):
                pe.wait_ge(x_p, h + 1)
                if h >= 1:
                    pe.wait_ge(x_pT, h)
                for mb in range(2):
                    for t in range(2):
                        c = mb * T + t * P
                        ins = pe.transpose(bank[5][:, c:c + P], xp[:, h % 2, t * MEM + mb * P:t * MEM + (mb + 1) * P],
                                           ident)
                ins.then_inc(x_tr, 1)

            def x_values(h):
                pe.wait_ge(x_pT, h + 1)
                pe.wait_ge(prod_free, P_V + 2 * h + 2)
                for j in range(2):
                    if h >= 1:
                        pe.wait_ge(x_lo, 2 * h - 1 + j)
                    for d in range(2):
                        c0 = (4 * h + 2 * j + d) * P
                        for mb in range(2):
                            ins = pe.matmul(bank[6 + j][:, d * T:(d + 1) * T], v[:, mb, c0:c0 + P],
                                            xpT[:, h, mb * T:(mb + 1) * T], start=mb == 0, stop=mb == 1)
                    ins.then_inc(x_pv, 1)

            def x_side(u):
                h = u // 6
                if h < X_HEADS and u % 6 == 1:
                    x_scores(h)
                if h < X_HEADS and u % 6 == 5:
                    x_transpose(h)
                if u in (10, 18, 26):
                    x_values(u // 8 - 1)
            token_stage(G0_V, P_V, 4, memT, before=x_side)

            def o_side(u):
                if u == 0:
                    pe.wait_ge(x_lo, 6)
                if u == 2:
                    x_values(3)
                if u == 6:
                    pe.wait_ge(x_lo, 8)
            token_stage(G0_O, P_O, 2, xT, before=o_side)
            token_stage(G0_O, P_O, 4, xT, first=2)
            for b in range(NB):
                norm_transpose(3, b)
            pe.wait_ge(n_lo, 4 * NB)
            channel_stage(G0_UP, P_UP, FT, xT)
            pe.wait_ge(act_whole, 1)
            token_stage(G0_DOWN, P_DOWN, DOWN_BLOCKS, actT, DOWN_K)


def channel_units(w):
    k, n = w.shape
    t = w.reshape(k // (UT * P), UT, P, n // P, P).transpose(3, 0, 2, 1, 4)
    return t.reshape(n // P, k // (UT * P), P, UW)


def token_units(w, nk, width):
    k, n = w.shape
    return w.reshape(k // (nk * P), nk, P, n // width, width).transpose(3, 0, 2, 1, 4).reshape(-1, UW)


def lay_out(a):
    w_in, wb = a["w_in"][0], a["w_branch"][0]
    sizes = (1024, 256, 256, 1024, 1024, 1024, 1024, 1024, 1024, D, D, D)
    at = np.cumsum((0,) + sizes)
    q_a, k_a, v_a, q_r, k_r, v_r, g_r, x_c, y_c, ga, gb, gc = (w_in[:, at[i]:at[i + 1]] for i in range(12))
    order = [h for m in range(8) for h in (m + 4 * (m // 4), m + 4 * (m // 4) + 4)]
    q_a = q_a.reshape(D, SWA_HEADS, SWA_D)[:, order].reshape(D, -1)
    wb_a = wb[0].reshape(SWA_HEADS, SWA_D, D)[order].reshape(BW, D)

    def branch(gate, w):
        return np.concatenate([channel_units(gate), channel_units(w)], axis=1).reshape(-1, UW)

    up = a["ffn_w_up"][0]
    wkv = a["xattn_wkv"][0]
    stream = np.concatenate([
        channel_units(np.concatenate([x_c, y_c, q_a, k_a], axis=1)).reshape(-1, UW),
        token_units(v_a, 4, 256),
        token_units(np.concatenate([q_r, k_r, v_r, g_r], axis=1), 2, 512),
        branch(gc, wb[2]), branch(ga, wb_a), branch(gb, wb[1]),
        token_units(a["w_out"][0], 2, 512),
        channel_units(wkv[:, :D]).reshape(-1, UW),
        channel_units(a["xattn_wq"][0]).reshape(-1, UW),
        token_units(wkv[:, D:], 2, 512),
        token_units(a["xattn_wo"][0], 2, 512),
        np.concatenate([channel_units(up[:, :F]), channel_units(up[:, F:])], axis=1).reshape(-1, UW),
    ], axis=0)
    down = []
    w_down = a["ffn_w_down"][0].reshape(FT, P, DOWN_BLOCKS, 512)
    for c in range(DOWN_BLOCKS):
        k0 = 0
        for k in DOWN_K:
            down.append(w_down[k0:k0 + k, :, c].transpose(1, 0, 2).reshape(-1, 512))
            k0 += k

    def tiles(v):
        return v.reshape(-1, P).T

    vecs = np.concatenate([tiles(a[n]) for n in (
        "mem_norm_g", "norm_mix_g", "norm_xattn_g", "norm_ffn_g", "lru_conv_w", "lru_conv_b", "lru_ba", "lru_bx",
        "lru_lambda", "ffn_conv_w", "ffn_conv_b")], axis=1)
    lru_w = np.stack([a["lru_wa"][0], a["lru_wx"][0]]).transpose(2, 0, 1, 3)
    return {"x": a["x"][0], "mem": a["mem"][0], "stream": stream, "down": np.concatenate(down, axis=0), "vecs": vecs,
            "sinks": a["attn_sinks"][0], "lru_w": lru_w, "final_g": a["final_norm_g"], **shape_constants()}


def shape_constants():
    f = np.float32
    theta = (f(10000.0) ** (-np.linspace(0.0, 1.0, RET_D // 2, dtype=f))).astype(f)
    ang = np.arange(T, dtype=f)[:, None] * theta[None, :]
    i, j = np.arange(P)[:, None], np.arange(P)[None, :]

    def half(t):
        return t.astype(f).reshape(2, P, RET_D // 2).transpose(1, 0, 2).reshape(P, P)

    consts = np.concatenate([np.eye(P, dtype=f), half(np.cos(ang)), half(np.sin(ang)),
                             np.where(j > i, 0.0, -1e30).astype(f), np.where(j <= i, 0.0, -1e30).astype(f)], axis=1)
    log_gamma = np.log1p(-np.exp2(-5.0 - np.arange(RET_HEADS)))
    gap = (np.arange(T)[None, :] - np.arange(P)[:, None]).astype(float)
    full = np.where(gap[:, None] >= 0, np.exp(np.maximum(gap, 0)[:, None] * log_gamma[None, :, None]), 0.0)
    full = full * RET_D ** -0.5
    decay = np.concatenate([full, full[:, :, 0:P]], axis=2).astype(f)
    return {"consts": consts, "decay": decay}


INPUTS = ["x", "mem", "stream", "down", "vecs", "sinks", "lru_w", "final_g", "consts", "decay"]


def kernel(**inputs):
    import concourse.bacc as bacc
    from concourse.bass_utils import run_bass_kernel_spmd

    nc = bacc.Bacc("TRN2", target_bir_lowering=False, num_devices=1)
    laid = lay_out({k: np.asarray(v) for k, v in inputs.items()})
    arrays, args = {}, []
    for name in INPUTS:
        arr = np.ascontiguousarray(laid[name])
        arrays[f"in_{name}"] = arr
        args.append(nc.dram_tensor(f"in_{name}", arr.shape, mybir.dt.from_np(arr.dtype), kind="ExternalInput").ap())
    out = nc.dram_tensor("out_y", (T, D), mybir.dt.float32, kind="ExternalOutput").ap()
    trunk_kernel(nc, *args, out)
    r = run_bass_kernel_spmd(nc, [arrays], core_ids=[0])
    return r.results[0]["out_y"].reshape(1, T, D)
```

```python
from contextlib import ExitStack

import numpy as np

import concourse.bass as bass
from concourse import mybir

P = 128
D = 2048
T = 256
KT = D // P
MEM = 256
EPS = 1e-6
BW = 1024
BT = BW // P
SWA_HEADS, SWA_KV, SWA_D = 16, 4, 64
RET_HEADS, RET_D = 8, 128
X_HEADS, X_D = 4, 512
F = 5504
FT = F // P
RING = 4
UT = 8
UW = UT * P

DOWN_K = [2] * 8 + [1] * 5 + [2] * 11
assert sum(DOWN_K) == FT and len(DOWN_K) % RING == 0
DOWN_BLOCKS = D // 512

G_CH = 26 * 2 // RING
G_VA = 1
G_RET = 8 * 8 // RING
G_BR = KT * 3 // RING
G_SQ = 4 * 8 // RING
G_UP = FT * 4 // RING
G0_VA = G_CH
G0_RET = G0_VA + G_VA
G0_BR = G0_RET + G_RET
G0_OUT = G0_BR + 3 * G_BR
G0_K = G0_OUT + G_SQ
G0_Q = G0_K + G_SQ
G0_V = G0_Q + G_SQ
G0_O = G0_V + G_SQ
G0_UP = G0_O + G_SQ
G0_DOWN = G0_UP + G_UP
G_DOWN = len(DOWN_K) // RING
DOWN_ROWS = FT * P

V_MEM, V_MIX, V_X, V_FFN = 0, 16, 32, 48
V_CW, V_CB, V_BA, V_BX, V_LAM = 64, 96, 104, 112, 120
V_FW, V_FB = 128, 128 + 3 * FT
NV = V_FB + FT
C_ID, C_COS, C_SIN, C_PREV, C_DIAG = 0, 128, 256, 384, 512
NC_ = 640
NDEC = 3 * P
GELU_1 = 2.0 * 0.7978845608028654
GELU_3 = GELU_1 * 0.044715
RSQRT_SEED = 0x5F3759DF


class Steps:

    def __init__(self, eng, sem):
        self.eng, self.sem, self.n, self.off = eng, sem, 0, 0

    def did(self, ins):
        ins.then_inc(self.sem, 1)
        self.n += 1
        return self.n + self.off

    def wait(self):
        self.eng.wait_ge(self.sem, self.n + self.off)

    def enter(self, i, per, first=0):
        self.start, self.per, self.first = self.n, per, first
        self.n -= first * per
        self.off = i * per

    def leave(self, iters):
        assert self.n + self.first * self.per - self.start == self.per, (self.n, self.start, self.per)
        self.n, self.off = self.start + self.per * (iters - self.first), 0


def trunk_kernel(nc, x_d, mem_d, stream_d, down_d, vecs_d, sinks_d, lru_w_d, final_g_d, consts_d, decay_d, out_d):
    f32, f32r, i32 = mybir.dt.float32, mybir.dt.float32r, mybir.dt.int32
    ALU, ACT, AX = mybir.AluOpType, mybir.ActivationFunctionType, mybir.AxisListType
    KB = 256

    ctx = ExitStack()
    with ctx:
        def sb(name, shape, dt=f32):
            return ctx.enter_context(nc.sbuf_tensor(name, shape, dt))

        def sem(name):
            return ctx.enter_context(nc.semaphore(name))

        raw = sb("raw", [P, RING, UW])
        whi = sb("whi", [P, RING, UW], f32r)
        wlo = sb("wlo", [P, RING, UW], f32r)
        xT = sb("xT", [P, KT, 2 * T], f32r)
        vecs = sb("vecs", [P, NV])
        consts = sb("consts", [P, NC_])
        sinks = sb("sinks", [P, SWA_HEADS])
        ss = sb("ss", [P, 5, 2, 4])
        ms = sb("ms", [P, 2, 2])
        rstd = sb("rstd", [P, 10])
        sp = sb("sp", [P, 8, BT])
        stat = sb("stat", [P, 6, 48])
        ret_st = sb("ret_st", [P, 2, 8])
        ret_nw = sb("ret_nw", [P, 3, 2])
        ident = consts[:, C_ID:C_ID + P]

        def at(kib, name, shape, dt=f32):
            with ExitStack() as tmp:
                if kib:
                    tmp.enter_context(nc.sbuf_tensor(name + "_below", [P, int(kib * KB)], f32))
                return tmp.enter_context(nc.sbuf_tensor(name, shape, dt))

        xr = at(0, "xr", [P, 2, D])
        xn = at(16, "xn", [P, 2, D])
        chT = at(32, "chT", [P, 26, T])
        va = at(58, "va", [P, 2, SWA_KV * SWA_D])
        lru_w = at(92, "lru_w", [P, 2, BT, P])
        lru_t = at(104, "lru_t", [P, 2, 8, T])
        ocT = at(0, "ocT", [P, BT, 2 * T], f32r)
        oaT = at(16, "oaT", [P, BT, 2 * T], f32r)
        obT = at(0, "obT", [P, BT, 2 * T], f32r)
        ret = at(60, "ret", [P, 2, 4, RET_HEADS * P])
        swa_s = at(92, "swa_s", [P, 2, 512])
        swa_p = at(96, "swa_p", [P, 2, 512])
        swa_pT = at(100, "swa_pT", [P, 2, 512])
        decay = at(92, "decay", [P, RET_HEADS, NDEC])
        rot = at(48, "rot", [P, 2, 2, 2, P])
        qkT = at(52, "qkT", [P, 2, 2 * T])
        rope_t = at(56, "rope_t", [P, 4, 2, 2, 64])
        sT = at(104, "sT", [P, 2, NDEC])
        ret_y = at(107, "ret_y", [P, 2, 4, 2, P])
        br_t = at(115, "br_t", [P, 2, 3, T])
        merged = at(32, "merged", [P, KT, T])
        mT = at(60, "mT", [P, KT, 2 * T], f32r)
        x1 = at(92, "x1", [P, 2, D])
        memr = at(0, "memr", [P, 2, D])
        memT = at(16, "memT", [P, KT, 2 * T], f32r)
        kT = at(48, "kT", [P, KT, MEM])
        x1n = at(64, "x1n", [P, 2, D])
        qT = at(0, "qT", [P, KT, T])
        v = at(64, "v", [P, 2, D])
        xp = at(80, "xp", [P, 2, 512])
        xpT = at(84, "xpT", [P, X_HEADS, 512])
        x2n = at(0, "x2n", [P, 2, D])
        actT = at(0, "actT", [P, FT, 2 * T], f32r)
        ffn_t = at(108, "ffn_t", [P, 4, T])
        y_last = at(108, "y_last", [P, 2, 512])
        gfin = at(112, "gfin", [P, D])
        junk = at(120, "junk", [P, 512])

        bank = [ctx.enter_context(nc.psum_tensor(f"bank{b}", [P, 512], f32)) for b in range(8)]

        raw_loaded = [sem(f"raw_loaded{s}") for s in range(RING)]
        hi_ready, lo_ready, unit_used = sem("hi_ready"), sem("lo_ready"), sem("unit_used")
        half0_done, prod_free = sem("half0_done"), sem("prod_free")
        x_loaded = [sem(f"x_loaded{b}") for b in range(4)]
        c_loaded, lruw_loaded, dec_loaded = sem("c_loaded"), sem("lruw_loaded"), sem("dec_loaded")
        sinks_loaded = sem("sinks_loaded")
        x1_loaded, mem_loaded, gf_loaded, stored = sem("x1_loaded"), sem("mem_loaded"), sem("gf_loaded"), sem("stored")
        dve_step, act_step = sem("dve_step"), sem("act_step")
        n_sq, n_rstd, n_xn, n_xn_act, n_tr, n_hi, n_lo = (
            sem("norm_" + w) for w in ("sq", "rstd", "xn", "xn_act", "tr", "hi", "lo"))
        l_xc, l_ps, l_sig, l_q, l_gelu, l_done = (sem("lru_" + w) for w in ("xc", "ps", "sig", "q", "gelu", "done"))
        r_prod = sem("ret_rope_prod")
        l_m, l_root, r_sg = sem("lru_m"), sem("lru_root"), sem("ret_silu_g")
        lru_abs, lru_z, lru_consts = sem("lru_abs"), sem("lru_z"), sem("lru_consts")
        s_sc, s_max, s_exp, s_p, s_tr, s_pT, s_pv, s_hi, s_lo = (
            sem("swa_" + w) for w in ("sc", "max", "exp", "p", "tr", "pT", "pv", "hi", "lo"))
        r_rot, r_tr, r_qkT, r_sc, r_sT, r_y, r_silu, r_o, r_otr, r_hi, r_lo = (
            sem("ret_" + w) for w in ("rot", "tr", "qkT", "sc", "sT", "y", "silu", "o", "otr", "hi", "lo"))
        g_sum, g_tanh = sem("gate_sum"), sem("gate_tanh")
        x_sc, x_max, x_exp, x_p, x_tr, x_pT, x_pv, x_hi, x_lo = (
            sem("xa_" + w) for w in ("sc", "max", "exp", "p", "tr", "pT", "pv", "hi", "lo"))
        f_conv, f_tanh = sem("ffn_conv"), sem("ffn_tanh")
        out_ready, act_whole = [sem(f"out_ready{t}") for t in range(2)], sem("act_whole")
        block = ctx.enter_context(nc.Block())

        NORM = [(xr, xn, xT, V_MIX), (memr, memr, memT, V_MEM), (x1, x1n, xT, V_X), (x1, x2n, xT, V_FFN),
                (x1, None, None, None)]
        NB = KT // 2
        ALONE = (0, 3)
        XN_DVE, XN_ACT = (0, 2, 6, 10), (0, None, None, 2)

        def norm_bank(which, b):
            return bank[2 + b % 6] if which in ALONE else bank[4 + b % 4]

        P_CH = 0
        P_VA = 26
        P_RET = P_VA + 2
        P_BR = P_RET + 16
        P_OUT = P_BR + 3 * 2 * KT
        P_K = P_OUT + 8
        P_Q = P_K + KT
        P_V = P_Q + KT
        P_O = P_V + 8
        P_UP = P_O + 8
        P_DOWN = P_UP + 2 * FT
        B_VA, B_RET, B_OUT, B_V, B_O, B_DOWN = 0, 1, 9, 13, 17, 21

        def swa_groups():
            for big in range(2):
                for half in range(2):
                    yield big, half, 0, 4 * big, 4
                    yield big, half, 1, 4 * big, 2
                    yield big, half, 1, 4 * big + 2, 2

        SWA = list(swa_groups())

        LRU_PERIOD = 7
        RET_PERIOD = 5
        RET_FROM = 3
        SWA_FROM = 60

        def down_width(s):
            return DOWN_K[s] * 512

        @block.sync
        def _(sp_eng):
            def load(g, s):
                sp_eng.dma_start(raw[:, s, :], stream_d[bass.ds((g * RING + s) * P, P), :]).then_inc(raw_loaded[s], 16)

            for b in range(4):
                sp_eng.dma_start(xr[:, :, b * 512:(b + 1) * 512],
                                 x_d[:, b * 512:(b + 1) * 512].rearrange("(t p) d -> p t d", p=P)
                                 ).then_inc(x_loaded[b], 16)
            sp_eng.dma_start(consts[:, :], consts_d).then_inc(c_loaded, 16)
            sp_eng.dma_start(vecs[:, :], vecs_d).then_inc(c_loaded, 16)
            for s in range(RING):
                load(0, s)
            with sp_eng.Fori(1, G0_DOWN) as g:
                for s in range(RING):
                    sp_eng.wait_ge(lo_ready, g * RING + (s + 1 - RING))
                    load(g, s)
            with sp_eng.Fori(0, DOWN_BLOCKS) as c:
                row = 0
                for u, k in enumerate(DOWN_K):
                    s = u % RING
                    sp_eng.wait_ge(lo_ready, c * len(DOWN_K) + (G0_DOWN * RING + u + 1 - RING))
                    src = down_d[bass.ds(c * DOWN_ROWS + row, k * P), :].rearrange("(p b) n -> p (b n)", p=P)
                    sp_eng.dma_start(raw[:, s, 0:512 * k], src).then_inc(raw_loaded[s], 16)
                    row += k * P
            for t in range(2):
                for n, (src, c0, c1) in enumerate(((y_last, D - 512, D), (x1, 0, D - 512))):
                    sp_eng.wait_ge(out_ready[t], n + 1)
                    sp_eng.dma_start(out_d[t * P:(t + 1) * P, c0:c1], src[:, t, 0:c1 - c0]).then_inc(stored, 16)
            sp_eng.wait_ge(stored, 64)

        @block.gpsimd
        def _(pool):
            pool.wait_ge(raw_loaded[RING - 1], 16)
            pool.dma_start(lru_w[:, :, :, :], lru_w_d).then_inc(lruw_loaded, 16)
            pool.dma_start(sinks[:, :], sinks_d[None, :].broadcast_to([P, SWA_HEADS])).then_inc(sinks_loaded, 16)
            pool.wait_ge(s_lo, 4)
            pool.dma_start(decay[:, :, :], decay_d).then_inc(dec_loaded, 16)

            for h in range(RET_HEADS):
                c = h * P
                lo_half = ret[:, :, 0:2, c:c + 64].rearrange("p t k c -> p k t c")
                hi_half = ret[:, :, 0:2, c + 64:c + P].rearrange("p t k c -> p k t c")
                cos, sin = (consts[:, o:o + P].rearrange("p (t c) -> p t c", t=2).unsqueeze(1).broadcast_to([P, 2, 2, 64])
                            for o in (C_COS, C_SIN))
                if h == 0:
                    pool.wait_ge(prod_free, P_BR)
                if h >= 1:
                    pool.wait_ge(r_rot, 2 * h)
                for j, (half, ang) in enumerate(((lo_half, cos), (hi_half, sin), (lo_half, sin), (hi_half, cos))):
                    pool.tensor_tensor(rope_t[:, j], half, ang, ALU.mult).then_inc(r_prod, 1)
                pool.wait_ge(r_prod, 4 * h + 4)
                if h >= 2:
                    pool.wait_ge(r_tr, h - 1)
                pool.tensor_tensor(rot[:, h % 2, :, :, 0:64], rope_t[:, 0], rope_t[:, 1], ALU.subtract).then_inc(r_rot, 1)
                pool.tensor_tensor(rot[:, h % 2, :, :, 64:P], rope_t[:, 2], rope_t[:, 3], ALU.add).then_inc(r_rot, 1)
                gate = ret[:, :, 3, c:c + P]
                pool.wait_ge(r_silu, h + 1)
                pool.tensor_tensor(ret_y[:, h % 2, 1, :, :], ret_y[:, h % 2, 0, :, :], gate, ALU.mult).then_inc(r_sg, 1)
                pool.wait_ge(r_sg, 2 * h + 1)
                pool.tensor_tensor(ret_y[:, h % 2, 1, :, :], ret_y[:, h % 2, 1, :, :], gate, ALU.add).then_inc(r_sg, 1)

            pool.wait_ge(r_lo, RET_HEADS)
            pool.dma_start(x1[:, :, :], x_d.rearrange("(t p) d -> p t d", p=P)).then_inc(x1_loaded, 16)
            pool.wait_ge(prod_free, P_OUT)
            pool.dma_start(memr[:, :, :], mem_d.rearrange("(t p) d -> p t d", p=P)).then_inc(mem_loaded, 16)
            pool.wait_ge(prod_free, P_UP)
            pool.dma_start(gfin[:, :], final_g_d[None, :].broadcast_to([P, D])).then_inc(gf_loaded, 16)

        @block.scalar
        def _(act):
            step = Steps(act, act_step)

            def hi_split(g, s, width=UW, first=False):
                act.wait_ge(raw_loaded[s], (g + 1) * 16)
                if not first:
                    act.wait_ge(unit_used, g * RING + (s + 1 - RING))
                act.activation(whi[:, s, 0:width], raw[:, s, 0:width], ACT.Copy).then_inc(hi_ready, 1)

            def stage(g0, body_groups, iters, evac=None, first=0, side=None, after=None):
                def body(i):
                    for u in range(RING * body_groups):
                        if evac:
                            evac(i, u)
                        if side:
                            side(i * RING * body_groups + u)
                        hi_split(i * body_groups + (g0 + 1 + u // RING), u % RING)
                    if after:
                        after(i)
                if side or iters - first == 1:
                    for i in range(first, iters):
                        body(i)
                else:
                    with act.Fori(first, iters) as i:
                        body(i)

            def squares(which, b, p0=None):
                for t in range(2):
                    if p0 is not None:
                        act.wait_ge(prod_free, b * 2 + (p0 + 1 + t))
                    src = NORM[which][0][:, t, b * 512:(b + 1) * 512]
                    if which or b or t:
                        act.wait_ge(n_sq, b * 2 + (8 * which + t))
                    act.activation(junk[:, :], src, ACT.Square, accum_out=ss[:, which, t, b:b + 1]).then_inc(n_sq, 1)

            def norm_scale(which, b):
                src, dst, _, _ = NORM[which]
                act.wait_ge(n_rstd, ALONE.index(which) + 1)
                for t in range(2):
                    ins = act.activation(dst[:, t, b * 512:(b + 1) * 512], src[:, t, b * 512:(b + 1) * 512],
                                         ACT.Copy, scale=rstd[:, 2 * which + t:2 * which + t + 1])
                ins.then_inc(n_xn_act, 1)

            def norm_hi(which, b):
                _, _, outT, g = NORM[which]
                act.wait_ge(n_tr, NB * which + b + 1)
                for k in (2 * b, 2 * b + 1):
                    ins = act.activation(outT[:, k, 0:T], norm_bank(which, b)[:, (k % 2) * T:(k % 2) * T + T],
                                         ACT.Copy, scale=vecs[:, g + k:g + k + 1])
                ins.then_inc(n_hi, 1)

            for b in range(4):
                act.wait_ge(x_loaded[b], 16)
                squares(0, b)
            hi_split(0, 0, first=True)
            act.wait_ge(c_loaded, 32)
            norm_scale(0, 2)
            norm_scale(0, 3)
            for b in range(NB):
                norm_hi(0, b)
                if b in (1, 3, 5):
                    hi_split(0, (b + 1) // 2, first=True)
            act.wait_ge(lru_abs, 1)
            act.activation(sp[:, 1, :], sp[:, 0, :], ACT.Exp).then_inc(lru_z, 1)
            stage(0, 1, G_CH)
            stage(G0_VA, 1, 1)

            def lru_gates(n):
                tr, ti, a, th, y2 = (lru_t[:, n % 2, j, :] for j in (1, 2, 3, 4, 5))
                if n == 0:
                    act.wait_ge(lru_consts, 1)
                    act.wait_ge(prod_free, P_VA)
                if n >= 2:
                    act.wait_ge(l_done, n - 1)
                act.activation(y2, chT[:, BT + n, :], ACT.Square).then_inc(l_sig, 1)
                act.wait_ge(l_ps, n + 1)
                act.activation(tr, bank[4 + n % 2][:, 0:T], ACT.Tanh, scale=0.5, bias=sp[:, 6, n:n + 1])
                step.did(act.activation(ti, bank[4 + n % 2][:, T:2 * T], ACT.Tanh, scale=0.5, bias=sp[:, 7, n:n + 1]))
                step.wait()
                act.activation(a, tr, ACT.Exp, scale=sp[:, 4, n:n + 1], bias=sp[:, 4, n:n + 1])
                act.activation(th, tr, ACT.Tanh, scale=sp[:, 5, n:n + 1], bias=sp[:, 5, n:n + 1]).then_inc(l_sig, 1)

            def lru_root(n):
                th, tg, q = (lru_t[:, n % 2, j, :] for j in (4, 6, 7))
                act.wait_ge(l_q, n + 1)
                act.activation(tg, q, ACT.Tanh, scale=0.5).then_inc(l_gelu, 1)
                act.wait_ge(l_m, n + 1)
                act.activation(th, th, ACT.Sqrt).then_inc(l_root, 1)

            def swa_exp(n):
                tiles = SWA[n][4]
                w = 512 // tiles
                act.wait_ge(s_max, n + 1)
                if n >= 2:
                    act.wait_ge(s_tr, n - 1)
                for j in range(tiles):
                    act.activation(swa_p[:, n % 2, j * w:(j + 1) * w], swa_s[:, n % 2, j * w:(j + 1) * w],
                                   ACT.Exp, bias=stat[:, 1, 4 * n + j:4 * n + j + 1],
                                   accum_out=stat[:, 2, 4 * n + j:4 * n + j + 1])
                act.activation(stat[:, 4, 4 * n:4 * n + tiles], stat[:, 3, 4 * n:4 * n + tiles],
                               ACT.Exp).then_inc(s_exp, 1)

            def swa_copy(n):
                act.wait_ge(s_tr, n + 1)
                if n >= 2:
                    act.wait_ge(s_pv, n - 1)
                act.activation(swa_pT[:, n % 2, :], bank[5][:, :], ACT.Copy).then_inc(s_pT, 1)

            def swa_hi(big):
                act.wait_ge(s_pv, 6 * big + 6)
                for j in range(2):
                    act.activation(oaT[:, 4 * big + 2 * j:4 * big + 2 * j + 2, 0:T],
                                   bank[6 + j][:, :].rearrange("p (a b) -> p a b", a=2), ACT.Copy).then_inc(s_hi, 1)

            def swa_side(u):
                n = u // 4
                if u % 4 == 0 and 1 <= n <= len(SWA):
                    swa_copy(n - 1)
                if u % 4 == 2 and n < len(SWA):
                    swa_exp(n)
                if u in (25, 49):
                    swa_hi(u // 24 - 1)

            def ret_side(u):
                n = u // LRU_PERIOD
                if n < BT and u % LRU_PERIOD == 3:
                    lru_gates(n)
                if n < BT and u % LRU_PERIOD == 6:
                    lru_root(n)
                if u >= SWA_FROM:
                    swa_side(u - SWA_FROM)

            stage(G0_RET, 2, 8, side=ret_side)

            def gate_evac(b):
                def evac(i, u):
                    if u % 3 == 2:
                        n = u // 3
                        act.wait_ge(g_sum, i * 4 + (KT * b + n + 1))
                        gate = br_t[:, n % 2, 0, :]
                        act.activation(gate, gate, ACT.Tanh, scale=0.5).then_inc(g_tanh, 1)
                return evac

            def retention_side(u):
                if u < 0:
                    return
                h, phase = u // RET_PERIOD, u % RET_PERIOD
                if h < RET_HEADS and phase == 0:
                    act.wait_ge(r_tr, h + 1)
                    if h >= 2:
                        act.wait_ge(r_sc, h - 1)
                    act.activation(qkT[:, h % 2, :], bank[4][:, :], ACT.Copy).then_inc(r_qkT, 1)
                    if h >= 2:
                        act.wait_ge(r_o, h - 1)
                    act.activation(ret_y[:, h % 2, 0, :, :], ret[:, :, 3, h * P:(h + 1) * P],
                                   ACT.Tanh, scale=0.5).then_inc(r_silu, 1)
                if 1 <= h <= RET_HEADS and phase == 3:
                    act.wait_ge(r_otr, h)
                    act.activation(obT[:, h - 1, 0:T], bank[7][:, 0:T], ACT.Copy, scale=0.5).then_inc(r_hi, 1)

            stage(G0_BR, 3, 4, gate_evac(0), side=lambda u: swa_side(u + 64 - SWA_FROM))
            stage(G0_BR + G_BR, 3, 4, gate_evac(1), side=lambda u: retention_side(u - RET_FROM))
            stage(G0_BR + 2 * G_BR, 3, 4, gate_evac(2))

            def mem_side(u):
                if u in (5, 6):
                    if u == 5:
                        act.wait_ge(mem_loaded, 16)
                    squares(1, 2 * (u - 5))
                    squares(1, 2 * (u - 5) + 1)
                if 13 <= u < 13 + NB:
                    norm_hi(1, u - 13)
            stage(G0_OUT, 2, 4, side=mem_side)

            def x1_side(u):
                if u < 4:
                    act.wait_ge(prod_free, P_K)
                    squares(2, u)
                if 8 <= u < 8 + NB:
                    norm_hi(2, u - 8)
            stage(G0_K, 1, 4, side=x1_side)
            stage(G0_K, 1, 8, first=4)
            stage(G0_Q, 1, 8)

            def x_exp_(h):
                act.wait_ge(x_max, h + 1)
                if h >= 2:
                    act.wait_ge(x_tr, h - 1)
                for t in range(2):
                    ins = act.activation(xp[:, h % 2, t * MEM:(t + 1) * MEM], bank[4][:, t * MEM:(t + 1) * MEM], ACT.Exp,
                                         scale=X_D ** -0.5, bias=stat[:, 1, 2 * h + t:2 * h + t + 1],
                                         accum_out=stat[:, 2, 2 * h + t:2 * h + t + 1])
                act.activation(stat[:, 4, 2 * h:2 * h + 2], stat[:, 1, 2 * h:2 * h + 2], ACT.Copy).then_inc(x_exp, 1)

            def x_hi_(h):
                for j in range(2):
                    act.wait_ge(x_pv, 2 * h + j + 1)
                    act.activation(xT[:, 4 * h + 2 * j:4 * h + 2 * j + 2, 0:T],
                                   bank[6 + j][:, :].rearrange("p (a b) -> p a b", a=2), ACT.Copy).then_inc(x_hi, 1)

            def x_side(u):
                h = u // 6
                if h < X_HEADS and u % 6 == 2:
                    x_exp_(h)
                if h < X_HEADS and u % 6 == 5:
                    act.wait_ge(x_tr, h + 1)
                    act.activation(xpT[:, h, :], bank[5][:, :], ACT.Copy).then_inc(x_pT, 1)
                if u in (11, 19, 27):
                    x_hi_(u // 8 - 1)
            stage(G0_V, 2, 4, side=x_side)
            stage(G0_O, 2, 4, side=lambda u: x_hi_(3) if u == 3 else None, after=lambda i: squares(3, i, P_O))
            norm_scale(3, 2)
            norm_scale(3, 3)
            for b in range(NB):
                norm_hi(3, b)

            def ffn_evac(i, u):
                if u == 3:
                    act.wait_ge(f_conv, i + 1)
                    act.activation(ffn_t[:, 1, :], ffn_t[:, 0, :], ACT.Tanh, scale=0.5).then_inc(f_tanh, 1)
            stage(G0_UP, 1, FT, ffn_evac)

            def down_splits(c, last):
                for u in range(len(DOWN_K)):
                    nxt = (u + RING) % len(DOWN_K)
                    if not (last and u + RING >= len(DOWN_K)):
                        hi_split(c * G_DOWN + (G0_DOWN + 1 + u // RING), u % RING, down_width(nxt))
                squares(4, c, P_DOWN)
            for c in range(DOWN_BLOCKS):
                down_splits(c, c == DOWN_BLOCKS - 1)
            act.wait_ge(n_rstd, 3)
            for src, cols in ((y_last, 512), (x1, D - 512)):
                act.activation(src[:, 1, 0:cols], src[:, 1, 0:cols], ACT.Copy,
                               scale=rstd[:, 9:10]).then_inc(out_ready[1], 1)

        @block.vector
        def _(dve):
            step = Steps(dve, dve_step)

            def lo_split(g, s, width=UW):
                dve.wait_ge(hi_ready, g * RING + (s + 1))
                dve.tensor_tensor(wlo[:, s, 0:width], raw[:, s, 0:width], whi[:, s, 0:width].bitcast(f32),
                                  ALU.subtract).then_inc(lo_ready, 1)

            def stage(g0, body_groups, iters, evac=None, steps=0, first=0, side=None):
                def body(i):
                    for u in range(RING * body_groups):
                        if evac:
                            evac(i, u)
                        if side:
                            side(i * RING * body_groups + u)
                        lo_split(i * body_groups + (g0 + 1 + u // RING), u % RING)
                if side or iters - first == 1:
                    for i in range(first, iters):
                        body(i)
                else:
                    with dve.Fori(first, iters) as i:
                        step.enter(i, steps, first)
                        body(i)
                        step.leave(iters)

            def rsqrt(y, x, t):
                step.wait()
                step.did(dve.tensor_scalar(t.bitcast(i32), x.bitcast(i32), 1, None, ALU.logical_shift_right))
                step.wait()
                step.did(dve.tensor_scalar(y.bitcast(i32), t.bitcast(i32), -1, RSQRT_SEED, ALU.mult, ALU.add))
                for _ in range(3):
                    step.wait()
                    step.did(dve.tensor_tensor(t, y, y, ALU.mult))
                    step.wait()
                    step.did(dve.scalar_tensor_tensor(t, t, -0.5, x, ALU.mult, ALU.mult))
                    step.wait()
                    step.did(dve.scalar_tensor_tensor(y, t, 1.5, y, ALU.add, ALU.mult))
                step.wait()

            def norm_rstd(which):
                dve.wait_ge(n_sq, 8 * (which + 1))
                step.did(dve.reduce_sum(ms[:, 0, :], ss[:, which, :, :], AX.X))
                step.wait()
                step.did(dve.tensor_scalar(ms[:, 0, :], ms[:, 0, :], 1.0 / D, EPS, ALU.mult, ALU.add))
                rsqrt(rstd[:, 2 * which:2 * which + 2], ms[:, 0, :], ms[:, 1, :])
                if which == 4:
                    dve.tensor_copy(ms[:, 1, :], ms[:, 0, :]).then_inc(n_rstd, 1)

            def norm_scale(which, b):
                src, dst, _, _ = NORM[which]
                for t in range(2):
                    ins = dve.tensor_scalar(dst[:, t, b * 512:(b + 1) * 512], src[:, t, b * 512:(b + 1) * 512],
                                            rstd[:, 2 * which + t:2 * which + t + 1], None, ALU.mult)
                    if which in ALONE and b == 0 and t == 0:
                        ins.then_inc(n_rstd, 1)
                ins.then_inc(n_xn, 1)

            def norm_lo(which, b):
                _, _, outT, g = NORM[which]
                dve.wait_ge(n_hi, NB * which + b + 1)
                for k in (2 * b, 2 * b + 1):
                    ins = dve.scalar_tensor_tensor(outT[:, k, T:2 * T],
                                                   norm_bank(which, b)[:, (k % 2) * T:(k % 2) * T + T],
                                                   vecs[:, g + k:g + k + 1], outT[:, k, 0:T].bitcast(f32),
                                                   ALU.mult, ALU.subtract)
                ins.then_inc(n_lo, 1)

            def sum_parts(out, from_bank):
                return dve.reduce_sum(out, from_bank[:, :].rearrange("p (a t) -> p t a", a=2), AX.X)

            def copy_channels(g0, dest):
                def evac(i, u):
                    if u >= 2:
                        dve.wait_ge(unit_used, i * 4 + (RING * g0 + u + 1))
                        sum_parts(dest(i, u - 2), bank[u - 2]).then_inc(prod_free, 1)
                return evac

            def wait_half(t, i, units, g0, b0):
                if t == 0:
                    dve.wait_ge(half0_done, i + (b0 + 1))
                else:
                    dve.wait_ge(unit_used, i * units + (RING * g0 + units))

            def copy_tokens(g0, b0, units, dest, width=512, flip=0):
                def evac(i, u):
                    if u == units - 1:
                        for t in range(2):
                            wait_half(t, i, units, g0, b0)
                            dve.tensor_copy(dest(i, t), bank[2 * ((i + flip) % 2) + t][:, 0:width]).then_inc(prod_free, 1)
                return evac

            norm_rstd(0)
            norm_scale(0, 0)
            norm_scale(0, 1)
            lo_split(0, 0)
            dve.wait_ge(c_loaded, 32)
            for b in range(NB):
                norm_lo(0, b)
                if b in (3, 7):
                    lo_split(0, (b + 1) // 4)
            lo_split(0, 3)

            lam = vecs[:, V_LAM:V_LAM + BT]
            s0, s1, s2, s3 = (sp[:, j, :] for j in range(4))
            dve.tensor_scalar(sp[:, 6, :], vecs[:, V_BA:V_BA + BT], 0.5, None, ALU.mult)
            dve.tensor_scalar(sp[:, 7, :], vecs[:, V_BX:V_BX + BT], 0.5, None, ALU.mult)
            step.did(dve.tensor_scalar(s1, lam, -1.0, None, ALU.mult))
            step.wait()
            step.did(dve.tensor_tensor(s0, lam, s1, ALU.max))
            step.wait()
            dve.tensor_scalar(s0, s0, -1.0, None, ALU.mult).then_inc(lru_abs, 1)

            def to_chT(i, j):
                return chT[:, bass.ds(i * 2 + j, 1), :].rearrange("p a b -> p (a b)")
            stage(0, 1, G_CH - 1, copy_channels(0, to_chT))

            dve.wait_ge(lru_z, 1)
            step.did(dve.tensor_scalar(s2, s1, 2.0, None, ALU.add))
            step.wait()
            step.did(dve.reciprocal(s2, s2))
            step.wait()
            step.did(dve.tensor_tensor(s1, s1, s2, ALU.mult))
            step.wait()
            step.did(dve.tensor_tensor(s2, s1, s1, ALU.mult))
            step.wait()
            step.did(dve.tensor_scalar(s3, s2, 2.0 / 19, 2.0 / 17, ALU.mult, ALU.add))
            for odd in (15, 13, 11, 9, 7, 5, 3, 1):
                step.wait()
                step.did(dve.tensor_tensor(s3, s3, s2, ALU.mult))
                step.wait()
                step.did(dve.tensor_scalar(s3, s3, 2.0 / odd, None, ALU.add))
            step.wait()
            step.did(dve.tensor_tensor(s3, s3, s1, ALU.mult))
            step.did(dve.tensor_scalar(s0, lam, -1.0, 0.0, ALU.mult, ALU.max))
            step.wait()
            step.did(dve.tensor_tensor(s3, s3, s0, ALU.add))
            step.wait()
            dve.tensor_scalar(sp[:, 5, :], s3, 4.0, None, ALU.mult)
            dve.tensor_scalar(sp[:, 4, :], s3, -4.0, None, ALU.mult).then_inc(lru_consts, 1)

            stage(0, 1, G_CH, copy_channels(0, to_chT), first=G_CH - 1)
            stage(G0_VA, 1, 1, copy_tokens(G0_VA, B_VA, 4, lambda i, t: va[:, t, :], T, 1))

            def lru_conv(n):
                xc, xin = lru_t[:, n % 2, 0, :], chT[:, n, :]
                w = [vecs[:, V_CW + BT * j + n:V_CW + BT * j + n + 1] for j in range(4)]
                if n >= 2:
                    dve.wait_ge(l_ps, n - 1)
                step.did(dve.tensor_scalar(xc, xin, w[3], vecs[:, V_CB + n:V_CB + n + 1], ALU.mult, ALU.add))
                for d in (1, 2, 3):
                    step.wait()
                    ins = dve.scalar_tensor_tensor(xc[:, d:], xin[:, :T - d], w[3 - d], xc[:, d:], ALU.mult, ALU.add)
                    if d < 3:
                        step.did(ins)
                ins.then_inc(l_xc, 1)

            def lru_input(n):
                xc, tr, ti, a, th, y2, tg, q = (lru_t[:, n % 2, j, :] for j in range(8))
                dve.wait_ge(l_sig, 2 * n + 1)
                step.did(dve.tensor_scalar(q, y2, GELU_3, GELU_1, ALU.mult, ALU.add))
                step.wait()
                dve.tensor_tensor(q, q, chT[:, BT + n, :], ALU.mult).then_inc(l_q, 1)
                dve.wait_ge(l_sig, 2 * n + 2)
                step.did(dve.tensor_tensor(y2, a, a, ALU.mult))
                step.did(dve.scalar_tensor_tensor(ti, ti, 1.0, xc, ALU.add, ALU.mult))
                step.wait()
                step.did(dve.scalar_tensor_tensor(th, y2, 1.0, th, ALU.add, ALU.mult))
                step.wait()
                dve.tensor_scalar(th, th, 0.0, None, ALU.max).then_inc(l_m, 1)

            def lru_scan(n):
                xc, tr, ti, a, th, y2, tg, q = (lru_t[:, n % 2, j, :] for j in range(8))
                dve.wait_ge(l_root, n + 1)
                step.did(dve.scalar_tensor_tensor(th, th, 0.5, ti, ALU.mult, ALU.mult))
                step.wait()
                step.did(dve.tensor_tensor_scan(y2, a, th, 0.0, ALU.mult, ALU.add))
                dve.wait_ge(l_gelu, n + 1)
                step.did(dve.scalar_tensor_tensor(tg, tg, 1.0, chT[:, BT + n, :], ALU.add, ALU.mult))
                step.wait()
                step.did(dve.scalar_tensor_tensor(q, tg, 0.5, y2, ALU.mult, ALU.mult))
                step.wait()
                step.did(dve.tensor_copy(ocT[:, n, 0:T], q))
                step.wait()
                dve.tensor_tensor(ocT[:, n, T:2 * T], q, ocT[:, n, 0:T].bitcast(f32), ALU.subtract).then_inc(l_done, 1)

            def swa_mask(n):
                big, half, blk, tile0, tiles = SWA[n]
                w = 512 // tiles
                head = 8 * big + 4 * half + tile0 % 4
                cols = slice(4 * n, 4 * n + tiles)
                scores = swa_s[:, n % 2, :].rearrange("p (a b) -> p a b", a=tiles)
                mask = consts[:, C_DIAG + P - w:C_DIAG + P].unsqueeze(1).broadcast_to([P, tiles, w])
                if n == 0:
                    dve.wait_ge(sinks_loaded, 16)
                dve.wait_ge(s_sc, n + 1)
                if n >= 2:
                    dve.wait_ge(s_exp, n - 1)
                step.did(dve.scalar_tensor_tensor(scores, bank[4][:, :].rearrange("p (a b) -> p a b", a=tiles),
                                                  SWA_D ** -0.5, mask, ALU.mult, ALU.add))
                step.wait()
                step.did(dve.reduce_max(stat[:, 0, cols], scores, AX.X))
                step.wait()
                step.did(dve.tensor_tensor(stat[:, 0, cols], stat[:, 0, cols], sinks[:, head:head + tiles], ALU.max))
                step.wait()
                dve.tensor_scalar(stat[:, 1, cols], stat[:, 0, cols], -1.0, None, ALU.mult)
                dve.tensor_tensor(stat[:, 3, cols], sinks[:, head:head + tiles], stat[:, 0, cols],
                                  ALU.subtract).then_inc(s_max, 1)

            def swa_normalise(n):
                tiles = SWA[n][4]
                cols = slice(4 * n, 4 * n + tiles)
                dve.wait_ge(s_exp, n + 1)
                step.did(dve.tensor_tensor(stat[:, 5, cols], stat[:, 2, cols], stat[:, 4, cols], ALU.add))
                step.wait()
                step.did(dve.reciprocal(stat[:, 5, cols], stat[:, 5, cols]))
                step.wait()
                probs = swa_p[:, n % 2, :].rearrange("p (a b) -> p a b", a=tiles)
                dve.tensor_tensor(probs, probs, stat[:, 5, cols].unsqueeze(2).broadcast_to([P, tiles, 512 // tiles]),
                                  ALU.mult).then_inc(s_p, 1)

            def swa_lo(big):
                for j in range(2):
                    dve.wait_ge(s_hi, 2 * big + j + 1)
                    tl = slice(4 * big + 2 * j, 4 * big + 2 * j + 2)
                    dve.tensor_tensor(oaT[:, tl, T:2 * T], bank[6 + j][:, :].rearrange("p (a b) -> p a b", a=2),
                                      oaT[:, tl, 0:T].bitcast(f32), ALU.subtract).then_inc(s_lo, 1)

            def swa_side(u):
                n = u // 4
                if n < len(SWA) and u % 4 == 0:
                    swa_mask(n)
                if n < len(SWA) and u % 4 == 2:
                    swa_normalise(n)
                if u in (26, 50):
                    swa_lo(u // 24 - 1)

            def ret_side(u):
                n = u // LRU_PERIOD
                if n < BT and u % LRU_PERIOD == 0:
                    lru_conv(n)
                if n < BT and u % LRU_PERIOD == 4:
                    lru_input(n)
                if n < BT and u % LRU_PERIOD == 6:
                    lru_scan(n)
                if u >= SWA_FROM:
                    swa_side(u - SWA_FROM)

            def ret_evac(i, u):
                if u == 7:
                    for t in range(2):
                        wait_half(t, i, 8, G0_RET, B_RET)
                        dve.tensor_copy(ret[:, t, i // 2, (i % 2) * 512:(i % 2) * 512 + 512],
                                        bank[2 * (i % 2) + t][:, :]).then_inc(prod_free, 1)
            stage(G0_RET, 2, 8, ret_evac, side=ret_side)

            def ret_stats(h):
                dve.wait_ge(r_y, h + 1)
                for t in range(2):
                    step.did(dve.bn_stats(ret_st[:, t, 0:6], bank[6][:, t * P:(t + 1) * P]))
                step.wait()
                for t in range(2):
                    step.did(dve.bn_aggr(ret_st[:, t, 6:8], ret_st[:, t, 0:6]))
                step.wait()
                var, root, place = ret_nw[:, 0, :], ret_nw[:, 1, :], ret_nw[:, 2, :]
                step.did(dve.tensor_scalar(var, ret_st[:, :, 7], EPS, None, ALU.add))
                rsqrt(root, var, place)
                if h >= 2:
                    dve.wait_ge(r_o, h - 1)
                for t in range(2):
                    step.did(dve.tensor_scalar(ret_y[:, h % 2, 2, t, :], bank[6][:, t * P:(t + 1) * P],
                                               ret_st[:, t, 6:7], ret_nw[:, 1, t:t + 1], ALU.subtract, ALU.mult))
                step.wait()
                dve.wait_ge(r_sg, 2 * h + 2)
                if h >= 2:
                    dve.wait_ge(r_otr, h - 1)
                dve.tensor_tensor(ret_y[:, h % 2, 3, :, :], ret_y[:, h % 2, 2, :, :], ret_y[:, h % 2, 1, :, :],
                                  ALU.mult).then_inc(r_o, 1)

            def retention_side(u):
                if u < 0:
                    return
                h, phase = u // RET_PERIOD, u % RET_PERIOD
                if 1 <= h <= RET_HEADS and phase == 3:
                    dve.wait_ge(r_hi, h)
                    dve.scalar_tensor_tensor(obT[:, h - 1, T:2 * T], bank[7][:, 0:T], 0.5,
                                             obT[:, h - 1, 0:T].bitcast(f32), ALU.mult, ALU.subtract).then_inc(r_lo, 1)
                if h < RET_HEADS and phase == 2:
                    if h == 0:
                        dve.wait_ge(dec_loaded, 16)
                    dve.wait_ge(r_sc, h + 1)
                    if h >= 2:
                        dve.wait_ge(r_y, h - 1)
                    dve.tensor_tensor(sT[:, h % 2, :], bank[5][:, 0:NDEC], decay[:, h, :], ALU.mult).then_inc(r_sT, 1)
                if h < RET_HEADS and phase == 4:
                    ret_stats(h)

            def merge_evac(b):
                def evac(i, u):
                    n = u // 3
                    if u % 3 == 1:
                        dve.wait_ge(unit_used, i * 12 + (RING * (G0_BR + G_BR * b) + u + 1))
                        dve.wait_ge(prod_free, i * 8 + (P_BR + 2 * KT * b + 2 * n - 2))
                        sum_parts(br_t[:, n % 2, 0, :], bank[2 * n % 4]).then_inc(g_sum, 1)
                    if u % 3 != 2:
                        return
                    tile = bass.ds(i * 4 + n, 1)
                    tanh, part, term = (br_t[:, n % 2, j, :] for j in range(3))
                    mrg = merged[:, tile, :].rearrange("p a b -> p (a b)")
                    dve.wait_ge(unit_used, i * 12 + (RING * (G0_BR + G_BR * b) + u + 1))
                    step.did(sum_parts(part, bank[(2 * n + 1) % 4]))
                    step.wait()
                    dve.wait_ge(g_tanh, i * 4 + (KT * b + n + 1))
                    if b == 0:
                        dve.scalar_tensor_tensor(mrg, tanh, 1.0, part, ALU.add, ALU.mult).then_inc(prod_free, 2)
                        return
                    step.did(dve.scalar_tensor_tensor(term, tanh, 1.0, part, ALU.add, ALU.mult))
                    step.wait()
                    if b == 1:
                        dve.tensor_tensor(mrg, mrg, term, ALU.add).then_inc(prod_free, 2)
                        return
                    total = part
                    step.did(dve.tensor_tensor(total, mrg, term, ALU.add))
                    step.wait()
                    hi = mT[:, tile, 0:T].rearrange("p a b -> p (a b)")
                    lo = mT[:, tile, T:2 * T].rearrange("p a b -> p (a b)")
                    step.did(dve.tensor_scalar(hi, total, 0.5, None, ALU.mult))
                    step.wait()
                    dve.scalar_tensor_tensor(lo, total, 0.5, hi.bitcast(f32),
                                             ALU.mult, ALU.subtract).then_inc(prod_free, 2)
                return evac
            stage(G0_BR, 3, 4, merge_evac(0), side=lambda u: swa_side(u + 64 - SWA_FROM))
            stage(G0_BR + G_BR, 3, 4, merge_evac(1), side=lambda u: retention_side(u - RET_FROM))
            stage(G0_BR + 2 * G_BR, 3, 4, merge_evac(2), 16)

            def add_tokens(g0, b0, flip):
                def evac(i, u):
                    if u == 7:
                        for t in range(2):
                            wait_half(t, i, 8, g0, b0)
                            dst = x1[:, t, i * 512:(i + 1) * 512]
                            dve.tensor_tensor(dst, dst, bank[2 * ((i + flip) % 2) + t][:, :],
                                              ALU.add).then_inc(prod_free, 1)
                return evac

            dve.wait_ge(x1_loaded, 16)

            def mem_side(u):
                if u == 8:
                    norm_rstd(1)
                if 9 <= u < 13:
                    norm_scale(1, u - 9)
                if 14 <= u < 14 + NB:
                    norm_lo(1, u - 14)
            stage(G0_OUT, 2, 4, add_tokens(G0_OUT, B_OUT, 0), side=mem_side)

            def x1_side(u):
                if u == 4:
                    norm_rstd(2)
                if 5 <= u < 9:
                    norm_scale(2, u - 5)
                if 9 <= u < 16:
                    norm_lo(2, u - 9)
                if u == 15:
                    norm_lo(2, 7)

            def to_kT(i, j):
                return kT[:, bass.ds(i * 2 + j, 1), :].rearrange("p a b -> p (a b)")
            stage(G0_K, 1, 4, copy_channels(G0_K, to_kT), side=x1_side)
            stage(G0_K, 1, 8, copy_channels(G0_K, to_kT), first=4)
            stage(G0_Q, 1, 8, copy_channels(G0_Q, lambda i, j: (
                qT[:, bass.ds(i * 2 + j, 1), :].rearrange("p a b -> p (a b)"))))

            def x_lo_(h):
                for j in range(2):
                    dve.wait_ge(x_hi, 2 * h + j + 1)
                    tl = slice(4 * h + 2 * j, 4 * h + 2 * j + 2)
                    dve.tensor_tensor(xT[:, tl, T:2 * T], bank[6 + j][:, :].rearrange("p (a b) -> p a b", a=2),
                                      xT[:, tl, 0:T].bitcast(f32), ALU.subtract).then_inc(x_lo, 1)

            def x_side(u):
                h = u // 6
                cols = slice(2 * h, 2 * h + 2)
                if h < X_HEADS and u % 6 == 1:
                    dve.wait_ge(x_sc, h + 1)
                    step.did(dve.reduce_max(stat[:, 0, cols], bank[4][:, :].rearrange("p (a b) -> p a b", a=2), AX.X))
                    step.wait()
                    dve.tensor_scalar(stat[:, 1, cols], stat[:, 0, cols], -(X_D ** -0.5), None,
                                      ALU.mult).then_inc(x_max, 1)
                if h < X_HEADS and u % 6 == 3:
                    dve.wait_ge(x_exp, h + 1)
                    step.did(dve.reciprocal(stat[:, 3, cols], stat[:, 2, cols]))
                    step.wait()
                    for t in range(2):
                        part = xp[:, h % 2, t * MEM:(t + 1) * MEM]
                        ins = dve.tensor_scalar(part, part, stat[:, 3, 2 * h + t:2 * h + t + 1], None, ALU.mult)
                    ins.then_inc(x_p, 1)
                if u in (12, 20, 28):
                    x_lo_(u // 8 - 1)
            stage(G0_V, 2, 4, copy_tokens(G0_V, B_V, 8, lambda i, t: v[:, t, i * 512:(i + 1) * 512], flip=1),
                  side=x_side)
            stage(G0_O, 2, 4, add_tokens(G0_O, B_O, 1), side=lambda u: x_lo_(3) if u == 4 else None)
            norm_rstd(3)
            norm_scale(3, 0)
            norm_scale(3, 1)
            for b in range(NB):
                norm_lo(3, b)

            def ffn_evac(i, u):
                conv, tanh, gate, value = (ffn_t[:, j, :] for j in range(4))
                if u == 2:
                    dve.wait_ge(unit_used, i * 4 + (RING * G0_UP + 3))
                    step.wait()
                    sum_parts(gate, bank[0]).then_inc(prod_free, 1)
                    dve.wait_ge(prod_free, i * 2 + (P_UP + 1))
                    w = [vecs[:, bass.ds(i + (V_FW + FT * j), 1)] for j in range(3)]
                    step.did(dve.tensor_scalar(conv, gate, w[2], vecs[:, bass.ds(i + V_FB, 1)], ALU.mult, ALU.add))
                    step.wait()
                    step.did(dve.scalar_tensor_tensor(conv[:, 1:], gate[:, 0:T - 1], w[1], conv[:, 1:],
                                                      ALU.mult, ALU.add))
                    step.wait()
                    dve.scalar_tensor_tensor(conv[:, 2:], gate[:, 0:T - 2], w[0], conv[:, 2:],
                                             ALU.mult, ALU.add).then_inc(f_conv, 1)
                if u == 3:
                    dve.wait_ge(f_tanh, i + 1)
                    step.did(dve.scalar_tensor_tensor(gate, tanh, 1.0, conv, ALU.add, ALU.mult))
                    dve.wait_ge(unit_used, i * 4 + (RING * G0_UP + 4))
                    sum_parts(value, bank[1]).then_inc(prod_free, 1)
                    dve.wait_ge(prod_free, i * 2 + (P_UP + 2))
                    step.wait()
                    step.did(dve.scalar_tensor_tensor(value, gate, 0.5, value, ALU.mult, ALU.mult))
                    step.wait()
                    hi = actT[:, bass.ds(i, 1), 0:T].rearrange("p a b -> p (a b)")
                    lo = actT[:, bass.ds(i, 1), T:2 * T].rearrange("p a b -> p (a b)")
                    step.did(dve.tensor_copy(hi, value))
                    step.wait()
                    step.did(dve.tensor_tensor(lo, value, hi.bitcast(f32), ALU.subtract))
            stage(G0_UP, 1, FT, ffn_evac, 6)
            step.wait()
            dve.tensor_copy(stat[:, 0, 0:1], stat[:, 0, 0:1]).then_inc(act_whole, 1)

            def times_gain(c):
                if c < DOWN_BLOCKS - 1:
                    dve.wait_ge(n_sq, 8 * 4 + 2 * (c + 1))
                dve.wait_ge(prod_free, P_DOWN + 2 * (c + 1))
                for t in range(2):
                    src = x1[:, t, c * 512:(c + 1) * 512]
                    dst = src if c < DOWN_BLOCKS - 1 else y_last[:, t, :]
                    step.did(dve.tensor_tensor(dst, src, gfin[:, c * 512:(c + 1) * 512], ALU.mult))

            def down(c, last):
                for u in range(len(DOWN_K)):
                    if u == len(DOWN_K) - 1:
                        for t in range(2):
                            wait_half(t, c, len(DOWN_K), G0_DOWN, B_DOWN)
                            dst = x1[:, t, c * 512:(c + 1) * 512]
                            dve.tensor_tensor(dst, dst, bank[2 * ((c + 1) % 2) + t][:, :],
                                              ALU.add).then_inc(prod_free, 1)
                        if last:
                            times_gain(c)
                    if u == 4 and c:
                        times_gain(c - 1)
                    nxt = (u + RING) % len(DOWN_K)
                    if not (last and u + RING >= len(DOWN_K)):
                        lo_split(c * G_DOWN + (G0_DOWN + 1 + u // RING), u % RING, down_width(nxt))
            dve.wait_ge(gf_loaded, 16)
            for c in range(DOWN_BLOCKS):
                down(c, c == DOWN_BLOCKS - 1)

            norm_rstd(4)
            for n, (src, cols) in enumerate(((y_last, 512), (x1, D - 512))):
                dve.tensor_scalar(src[:, 0, 0:cols], src[:, 0, 0:cols], rstd[:, 8:9], None,
                                  ALU.mult).then_inc(out_ready[0], 1)

        @block.tensor
        def _(pe):
            def channel_unit(g, s, X, k0, out, first, last):
                pe.wait_ge(lo_ready, g * RING + (s + 1))
                for b in range(UT):
                    c = slice(b * P, (b + 1) * P)
                    end = last and b == UT - 1
                    if end:
                        pe.matmul(out[:, T:2 * T], wlo[:, s, c], X[:, k0 + b, 0:T], start=False, stop=False)
                    ins = pe.matmul(out[:, :], whi[:, s, c], X[:, k0 + b, :], start=first and b == 0, stop=end)
                    if not end:
                        ins = pe.matmul(out[:, T:2 * T], wlo[:, s, c], X[:, k0 + b, 0:T], start=False, stop=False)
                ins.then_inc(unit_used, 1)

            def token_unit(g, s, X, k0, nk, width, first, last, pair):
                pe.wait_ge(lo_ready, g * RING + (s + 1))
                for t in range(2):
                    for b in range(nk):
                        c = slice(b * width, (b + 1) * width)
                        k = k0 + b
                        hi_x, lo_x = X[:, k, t * P:(t + 1) * P], X[:, k, T + t * P:T + (t + 1) * P]
                        for n, (x_, w_) in enumerate(((hi_x, whi), (hi_x, wlo), (lo_x, whi))):
                            ins = pe.matmul(bank[pair + t][:, 0:width], x_, w_[:, s, c],
                                            start=first and b == 0 and n == 0, stop=last and b == nk - 1 and n == 2)
                    if last and t == 0:
                        ins.then_inc(half0_done, 1)
                    if first and t == 0:
                        yield
                ins.then_inc(unit_used, 1)

            def channel_stage(g0, p0, pairs, X, first=0, before=None, older=0):
                def body(i):
                    for u in range(RING):
                        half, j = divmod(u, 2)
                        if half == 0 and (p0 or not before):
                            pe.wait_ge(prod_free, i * 2 + (p0 + j - 1 - older))
                        if before:
                            before(4 * i + u)
                        channel_unit(i + g0, u, X, UT * half, bank[j], half == 0, half == 1)
                if before:
                    for i in range(first, pairs):
                        body(i)
                else:
                    with pe.Fori(first, pairs) as i:
                        body(i)

            def token_block(g, p, X, ks, width, pair=0, before=None):
                k0 = 0
                pe.wait_ge(prod_free, p - 3)
                for u, nk in enumerate(ks):
                    if before:
                        before(u)
                    for _ in token_unit(g + u // RING, u % RING, X, k0, nk, width, u == 0, u == len(ks) - 1,
                                        pair):
                        pe.wait_ge(prod_free, p - 2)
                    k0 += nk

            def token_stage(g0, p0, blocks, X, ks=(2,) * 8, width=512, first=0, flip=0, before=None,
                            in_loop=None):
                if before:
                    for i in range(first, blocks):
                        token_block(i * (len(ks) // RING) + g0, i * 2 + p0, X, ks, width, 2 * ((i + flip) % 2),
                                    lambda u, i=i: before(i * len(ks) + u))
                else:
                    with pe.Fori(first // 2, blocks // 2) as i:
                        for j in range(2):
                            token_block(i * (len(ks) // RING * 2) + (g0 + j * (len(ks) // RING)), i * 4 + (p0 + 2 * j),
                                        X, ks, width, 2 * ((j + flip) % 2), in_loop)

            def norm_transpose(which, b):
                _, xn_, _, _ = NORM[which]
                if which in ALONE and b >= NB // 2:
                    pe.wait_ge(n_xn_act, XN_ACT[which] + b // 2 - 1)
                else:
                    pe.wait_ge(n_xn, XN_DVE[which] + b // 2 + 1)
                banks = 6 if which in ALONE else 4
                if b >= banks:
                    pe.wait_ge(n_lo, NB * which + b + 1 - banks)
                for k in (2 * b, 2 * b + 1):
                    for t in range(2):
                        c = (k % 2) * T + t * P
                        ins = pe.transpose(norm_bank(which, b)[:, c:c + P], xn_[:, t, k * P:(k + 1) * P], ident)
                ins.then_inc(n_tr, 1)

            pe.wait_ge(c_loaded, 32)

            def norm_side(which):
                def side(u):
                    for b in ((0, 1, 2, 3, 4, 5), (6, 7), (), ())[u]:
                        norm_transpose(which, b)
                    if u in (0, 2):
                        pe.wait_ge(n_lo, NB * which + NB // 2 * (u // 2 + 1))
                return side

            channel_stage(0, P_CH, 1, xT, before=norm_side(0))
            channel_stage(0, P_CH, P_VA // 2, xT, first=1)
            token_block(G0_VA, P_VA, xT, (4,) * 4, SWA_KV * SWA_D, 2)

            def lru_product(n):
                if n == 0:
                    pe.wait_ge(lruw_loaded, 16)
                pe.wait_ge(l_xc, n + 1)
                if n >= 2:
                    pe.wait_ge(l_sig, 2 * (n - 1))
                for j in range(2):
                    ins = pe.matmul(bank[4 + n % 2][:, j * T:(j + 1) * T], lru_w[:, j, n, :], lru_t[:, n % 2, 0, :],
                                    start=True, stop=True)
                ins.then_inc(l_ps, 1)

            def swa_scores(n):
                big, half, blk, tile0, tiles = SWA[n]
                w = 512 // tiles
                rows = slice(64 * half, 64 * half + 64)
                if n == 0:
                    pe.wait_ge(l_sig, 2 * BT)
                else:
                    pe.wait_ge(s_max, n)
                for j in range(tiles):
                    ins = pe.matmul(bank[4][:, j * w:(j + 1) * w], chT[rows, 16 + tile0 + j, blk * P:blk * P + P],
                                    chT[rows, 24 + big, 0:w], start=True, stop=True)
                ins.then_inc(s_sc, 1)

            def swa_transpose(n):
                pe.wait_ge(s_p, n + 1)
                if n >= 1:
                    pe.wait_ge(s_pT, n)
                for j in range(4):
                    ins = pe.transpose(bank[5][:, j * P:(j + 1) * P], swa_p[:, n % 2, j * P:(j + 1) * P], ident)
                ins.then_inc(s_tr, 1)

            def swa_values(n):
                big, half, blk, tile0, tiles = SWA[n]
                pe.wait_ge(s_pT, n + 1)
                if n == 6:
                    pe.wait_ge(s_lo, 2)
                kv = 2 * big + half
                for j in range(tiles):
                    local = (tile0 + j) % 4
                    c = (local % 2) * T + blk * P
                    out = bank[6 + local // 2][64 * half:64 * half + 64, c:c + P]
                    nb = 4 // tiles
                    for kb in range(nb):
                        at_ = (j * nb + kb) * P
                        ins = pe.matmul(out, va[:, kb, kv * 64:(kv + 1) * 64], swa_pT[:, n % 2, at_:at_ + P],
                                        start=kb == 0, stop=kb == nb - 1)
                ins.then_inc(s_pv, 1)

            def swa_side(u):
                n = u // 4
                if u % 4 == 0 and 1 <= n <= len(SWA):
                    swa_transpose(n - 1)
                if u % 4 == 0 and n < len(SWA):
                    swa_scores(n)
                if u % 4 == 1 and 1 <= n <= len(SWA):
                    swa_values(n - 1)

            def ret_side(u):
                n = u // LRU_PERIOD
                if n < BT and u % LRU_PERIOD == 3:
                    lru_product(n)
                if u >= SWA_FROM:
                    swa_side(u - SWA_FROM)
            token_stage(G0_RET, P_RET, 8, xT, before=ret_side)

            def retention_side(u):
                if u < 0:
                    return
                h, phase = u // RET_PERIOD, u % RET_PERIOD
                if 1 <= h <= RET_HEADS and phase == 3:
                    pe.wait_ge(r_o, h)
                    if h >= 2:
                        pe.wait_ge(r_lo, h - 1)
                    for t in range(2):
                        ins = pe.transpose(bank[7][:, t * P:(t + 1) * P], ret_y[:, (h - 1) % 2, 3, t, :], ident)
                    ins.then_inc(r_otr, 1)
                if h >= RET_HEADS:
                    return
                if phase == 0:
                    pe.wait_ge(r_rot, 2 * h + 2)
                    if h >= 1:
                        pe.wait_ge(r_qkT, h)
                    for qk in range(2):
                        for t in range(2):
                            c = qk * T + t * P
                            ins = pe.transpose(bank[4][:, c:c + P], rot[:, h % 2, qk, t, :], ident)
                    ins.then_inc(r_tr, 1)
                if phase == 2:
                    pe.wait_ge(r_qkT, h + 1)
                    if h >= 1:
                        pe.wait_ge(r_sT, h)
                    q_, k_ = qkT[:, h % 2, 0:T], qkT[:, h % 2, T:2 * T]
                    pe.matmul(bank[5][:, 0:T], k_[:, 0:P], q_, start=True, stop=True)
                    pe.matmul(bank[5][:, T:T + P], k_[:, P:T], q_[:, P:T], start=True, stop=True).then_inc(r_sc, 1)
                if phase == 4:
                    pe.wait_ge(r_sT, h + 1)
                    if h >= 1:
                        pe.wait_ge(r_o, h)
                    v_ = ret[:, :, 2, h * P:(h + 1) * P]
                    pe.matmul(bank[6][:, 0:P], sT[:, h % 2, 0:P], v_[:, 0, :], start=True, stop=True)
                    pe.matmul(bank[6][:, P:T], sT[:, h % 2, P:T], v_[:, 0, :], start=True, stop=False)
                    pe.matmul(bank[6][:, P:T], sT[:, h % 2, T:T + P], v_[:, 1, :], start=False, stop=True).then_inc(r_y, 1)

            def branch_body(b, i, oT, before=None):
                for n in range(4):
                    p = i * 8 + (P_BR + 2 * KT * b + 2 * n)
                    g = i * 3 + (G0_BR + G_BR * b)
                    pe.wait_ge(prod_free, p - 2)
                    for j in range(3):
                        u = 3 * n + j
                        if before:
                            before(12 * i + u)
                        if j < 2:
                            channel_unit(g + u // RING, u % RING, xT, UT * j, bank[2 * n % 4], j == 0, j == 1)
                        else:
                            if before and i == 0 and n == 0:
                                pe.wait_ge(*((l_done, BT), (s_lo, 4))[b])
                            channel_unit(g + u // RING, u % RING, oT, 0, bank[(2 * n + 1) % 4], True, True)

            for i in range(4):
                branch_body(0, i, ocT, lambda u: swa_side(u + 64 - SWA_FROM))
            for i in range(4):
                branch_body(1, i, oaT, lambda u: retention_side(u - RET_FROM))
            pe.wait_ge(r_lo, RET_HEADS)
            with pe.Fori(0, 4) as i:
                branch_body(2, i, obT)

            def out_side(u):
                if u == 0:
                    pe.wait_ge(prod_free, P_OUT - 2)
                if u == 7:
                    pe.wait_ge(prod_free, P_OUT)
                if 13 <= u < 13 + NB:
                    norm_transpose(1, u - 13)
            token_stage(G0_OUT, P_OUT, 4, mT, before=out_side)
            pe.wait_ge(n_lo, 2 * NB)
            channel_stage(G0_K, P_K, 1, memT, before=lambda u: None, older=2)
            channel_stage(G0_K, P_K, 4, memT, first=1,
                          before=lambda u: norm_transpose(2, u - 8) if 8 <= u < 8 + NB else None)
            channel_stage(G0_K, P_K, 8, memT, first=4)
            pe.wait_ge(n_lo, 3 * NB)
            channel_stage(G0_Q, P_Q, 8, xT)

            def x_scores(h):
                if h == 0:
                    pe.wait_ge(prod_free, P_V)
                else:
                    pe.wait_ge(x_exp, h)
                for t in range(2):
                    for j in range(4):
                        ins = pe.matmul(bank[4][:, t * MEM:(t + 1) * MEM], qT[:, 4 * h + j, t * P:(t + 1) * P],
                                        kT[:, 4 * h + j, :], start=j == 0, stop=j == 3)
                ins.then_inc(x_sc, 1)

            def x_transpose(h):
                pe.wait_ge(x_p, h + 1)
                if h >= 1:
                    pe.wait_ge(x_pT, h)
                for mb in range(2):
                    for t in range(2):
                        c = mb * T + t * P
                        ins = pe.transpose(bank[5][:, c:c + P], xp[:, h % 2, t * MEM + mb * P:t * MEM + (mb + 1) * P],
                                           ident)
                ins.then_inc(x_tr, 1)

            def x_values(h):
                pe.wait_ge(x_pT, h + 1)
                pe.wait_ge(prod_free, P_V + 2 * h + 2)
                for j in range(2):
                    if h >= 1:
                        pe.wait_ge(x_lo, 2 * h - 1 + j)
                    for d in range(2):
                        c0 = (4 * h + 2 * j + d) * P
                        for mb in range(2):
                            ins = pe.matmul(bank[6 + j][:, d * T:(d + 1) * T], v[:, mb, c0:c0 + P],
                                            xpT[:, h, mb * T:(mb + 1) * T], start=mb == 0, stop=mb == 1)
                    ins.then_inc(x_pv, 1)

            def x_side(u):
                h = u // 6
                if h < X_HEADS and u % 6 == 1:
                    x_scores(h)
                if h < X_HEADS and u % 6 == 5:
                    x_transpose(h)
                if u in (10, 18, 26):
                    x_values(u // 8 - 1)
            token_stage(G0_V, P_V, 4, memT, flip=1, before=x_side)

            def o_side(u):
                if u == 0:
                    pe.wait_ge(x_lo, 6)
                if u == 2:
                    x_values(3)
                if u == 6:
                    pe.wait_ge(x_lo, 8)
            token_stage(G0_O, P_O, 2, xT, flip=1, before=o_side)
            token_stage(G0_O, P_O, 4, xT, flip=1, first=2)
            channel_stage(G0_UP, P_UP, 1, xT, before=norm_side(3))
            channel_stage(G0_UP, P_UP, FT, xT, first=1)
            pe.wait_ge(f_conv, FT)

            def down_side(u):
                if u == len(DOWN_K) - 1:
                    pe.wait_ge(act_whole, 1)
            token_stage(G0_DOWN, P_DOWN, DOWN_BLOCKS, actT, DOWN_K, flip=1, in_loop=down_side)


def channel_units(w):
    k, n = w.shape
    t = w.reshape(k // (UT * P), UT, P, n // P, P).transpose(3, 0, 2, 1, 4)
    return t.reshape(n // P, k // (UT * P), P, UW)


def in_pairs(units):
    return units.reshape(-1, 2, 2, P, UW).swapaxes(1, 2).reshape(-1, UW)


def token_units(w, nk, width):
    k, n = w.shape
    return w.reshape(k // (nk * P), nk, P, n // width, width).transpose(3, 0, 2, 1, 4).reshape(-1, UW)


def lay_out(a):
    w_in, wb = a["w_in"][0], a["w_branch"][0]
    sizes = (1024, 256, 256, 1024, 1024, 1024, 1024, 1024, 1024, D, D, D)
    at = np.cumsum((0,) + sizes)
    q_a, k_a, v_a, q_r, k_r, v_r, g_r, x_c, y_c, ga, gb, gc = (w_in[:, at[i]:at[i + 1]] for i in range(12))
    order = [h for m in range(8) for h in (m + 4 * (m // 4), m + 4 * (m // 4) + 4)]
    q_a = q_a.reshape(D, SWA_HEADS, SWA_D)[:, order].reshape(D, -1)
    wb_a = wb[0].reshape(SWA_HEADS, SWA_D, D)[order].reshape(BW, D)

    def branch(gate, w):
        return np.concatenate([channel_units(gate), channel_units(w)], axis=1).reshape(-1, UW)

    up = a["ffn_w_up"][0]
    wkv = a["xattn_wkv"][0]
    stream = np.concatenate([
        in_pairs(channel_units(np.concatenate([x_c, y_c, q_a, k_a], axis=1))),
        token_units(v_a, 4, 256),
        token_units(np.concatenate([q_r, k_r, v_r, g_r], axis=1), 2, 512),
        branch(gc, wb[2]), branch(ga, wb_a), branch(gb, wb[1]),
        token_units(a["w_out"][0], 2, 512),
        in_pairs(channel_units(wkv[:, :D])),
        in_pairs(channel_units(a["xattn_wq"][0])),
        token_units(wkv[:, D:], 2, 512),
        token_units(a["xattn_wo"][0], 2, 512),
        in_pairs(np.stack([channel_units(up[:, :F]), channel_units(up[:, F:])], axis=1)),
    ], axis=0)
    down = []
    w_down = a["ffn_w_down"][0].reshape(FT, P, DOWN_BLOCKS, 512)
    for c in range(DOWN_BLOCKS):
        k0 = 0
        for k in DOWN_K:
            down.append(w_down[k0:k0 + k, :, c].transpose(1, 0, 2).reshape(-1, 512))
            k0 += k

    def tiles(v):
        return v.reshape(-1, P).T

    vecs = np.concatenate([tiles(a[n]) for n in (
        "mem_norm_g", "norm_mix_g", "norm_xattn_g", "norm_ffn_g", "lru_conv_w", "lru_conv_b", "lru_ba", "lru_bx",
        "lru_lambda", "ffn_conv_w", "ffn_conv_b")], axis=1)
    lru_w = np.stack([a["lru_wa"][0], a["lru_wx"][0]]).transpose(2, 0, 1, 3)
    return {"x": a["x"][0], "mem": a["mem"][0], "stream": stream, "down": np.concatenate(down, axis=0), "vecs": vecs,
            "sinks": a["attn_sinks"][0], "lru_w": lru_w, "final_g": a["final_norm_g"], **shape_constants()}


def shape_constants():
    f = np.float32
    theta = (f(10000.0) ** (-np.linspace(0.0, 1.0, RET_D // 2, dtype=f))).astype(f)
    ang = np.arange(T, dtype=f)[:, None] * theta[None, :]
    i, j = np.arange(P)[:, None], np.arange(P)[None, :]

    def half(t):
        return t.astype(f).reshape(2, P, RET_D // 2).transpose(1, 0, 2).reshape(P, P)

    consts = np.concatenate([np.eye(P, dtype=f), half(np.cos(ang)), half(np.sin(ang)),
                             np.where(j > i, 0.0, -1e30).astype(f), np.where(j <= i, 0.0, -1e30).astype(f)], axis=1)
    log_gamma = np.log1p(-np.exp2(-5.0 - np.arange(RET_HEADS)))
    gap = (np.arange(T)[None, :] - np.arange(P)[:, None]).astype(float)
    full = np.where(gap[:, None] >= 0, np.exp(np.maximum(gap, 0)[:, None] * log_gamma[None, :, None]), 0.0)
    full = full * RET_D ** -0.5
    decay = np.concatenate([full, full[:, :, 0:P]], axis=2).astype(f)
    return {"consts": consts, "decay": decay}


INPUTS = ["x", "mem", "stream", "down", "vecs", "sinks", "lru_w", "final_g", "consts", "decay"]


def kernel(**inputs):
    import concourse.bacc as bacc
    from concourse.bass_utils import run_bass_kernel_spmd

    nc = bacc.Bacc("TRN2", target_bir_lowering=False, num_devices=1)
    laid = lay_out({k: np.asarray(v) for k, v in inputs.items()})
    arrays, args = {}, []
    for name in INPUTS:
        arr = np.ascontiguousarray(laid[name])
        arrays[f"in_{name}"] = arr
        args.append(nc.dram_tensor(f"in_{name}", arr.shape, mybir.dt.from_np(arr.dtype), kind="ExternalInput").ap())
    out = nc.dram_tensor("out_y", (T, D), mybir.dt.float32, kind="ExternalOutput").ap()
    trunk_kernel(nc, *args, out)
    r = run_bass_kernel_spmd(nc, [arrays], core_ids=[0])
    return r.results[0]["out_y"].reshape(1, T, D)
```
